# Optimizing a Trainium2 kernel written in Bass

```python
import jax, jax.numpy as jnp
from jax import lax
import numpy as np

D_MODEL = 1024
BATCH = 1
SEQ = 1024
DEPTH = 1
DEC_BATCH = 8
DEC_SEQ = 16
PAST_LEN = 512

CHUNK = 64
QBLK = 128
N_HEADS_A = 8
DH_A = 64
N_IDX = 4
D_IDX = 64
TOPK_MAX = 256
NH_M = 4
DK_M = 64
DV_M = 128
D_FF = 2816
EPS = 1e-6
IDX_SCALE = (N_IDX * D_IDX) ** -0.5
SPLITS = (N_HEADS_A * DH_A, DH_A, DH_A, N_IDX * D_IDX, D_IDX, N_IDX,
          NH_M * DK_M, NH_M * DK_M, NH_M * DV_M, 2 * NH_M, NH_M * DV_M, 2 * D_MODEL)
D_IN = N_HEADS_A * DH_A + 2 * DH_A + N_IDX * D_IDX + D_IDX + N_IDX + 2 * NH_M * DK_M + 2 * NH_M * DV_M + 2 * NH_M + 2 * D_MODEL

kernel_name = 'streaming_dsa_mlstm_macaron_step'

def rmsnorm(x, g):
    x32 = x.astype(jnp.float32)
    y = x32 * lax.rsqrt(jnp.mean(x32 * x32, axis=-1, keepdims=True) + EPS)
    return y.astype(x.dtype) * g

def half_ffn(x, g, w_up, w_down):
    a, b = jnp.split(rmsnorm(x, g) @ w_up, 2, axis=-1)
    return x + 0.5 * ((jax.nn.silu(a) * b) @ w_down)

def alibi_slopes():
    return jnp.exp2(-8.0 * jnp.arange(1, N_HEADS_A + 1, dtype=jnp.float32) / N_HEADS_A)

def project(h, w_in, b_gates):
    B, T, _ = h.shape
    offs = np.cumsum(SPLITS)[:-1].tolist()
    aq, ak, av, iq, ik, iw, mq, mk, mv, mif, mo, gates = jnp.split(h @ w_in, offs, axis=-1)
    mif = mif.astype(jnp.float32) + b_gates.astype(jnp.float32)
    ig = mif[..., :NH_M]
    lf = jax.nn.log_sigmoid(mif[..., NH_M:])
    g_a, g_b = jnp.split(gates, 2, axis=-1)
    return (aq.reshape(B, T, N_HEADS_A, DH_A), ak, av, iq.reshape(B, T, N_IDX, D_IDX), ik, iw,
            mq.reshape(B, T, NH_M, DK_M), mk.reshape(B, T, NH_M, DK_M), mv.reshape(B, T, NH_M, DV_M),
            ig, lf, mo, g_a, g_b)

def dsa_attend(q, q_idx, w_idx, t_pos, k, v, k_idx, top_k):
    L = k.shape[1]
    s_pos = jnp.arange(L, dtype=jnp.int32)
    rel = jax.nn.relu(jnp.einsum('bqhd,bsd->bqhs', q_idx, k_idx))
    score = jnp.einsum('bqhs,bqh->bqs', rel, w_idx).astype(jnp.float32) * IDX_SCALE
    adm = (s_pos[None, :] // CHUNK) <= (t_pos[:, None] // CHUNK)
    score = jnp.where(adm[None], score, -jnp.inf)
    _, sel = lax.top_k(score, top_k)
    gather = jax.vmap(lambda a, i: a[i])
    k_sel = gather(k, sel)
    v_sel = gather(v, sel)
    valid = (sel // CHUNK) <= (t_pos[None, :, None] // CHUNK)
    dist = jnp.abs(t_pos[None, :, None] - sel).astype(jnp.float32)
    logits = (jnp.einsum('bqhd,bqkd->bqhk', q, k_sel).astype(jnp.float32) * DH_A ** -0.5
              - alibi_slopes()[None, None, :, None] * dist[:, :, None, :])
    logits = jnp.where(valid[:, :, None, :], logits, -jnp.inf)
    p = jax.nn.softmax(logits, axis=-1).astype(v.dtype)
    return jnp.einsum('bqhk,bqkd->bqhd', p, v_sel)

def mlstm_heads(mq, mk, mv, ig, lf):
    f32 = jnp.float32
    q = jnp.moveaxis(mq, 2, 1).astype(f32) * DK_M ** -0.5
    k = jnp.moveaxis(mk, 2, 1).astype(f32)
    v = jnp.moveaxis(mv, 2, 1).astype(f32)
    return q, k, v, jnp.moveaxis(ig, 2, 1), jnp.moveaxis(lf, 2, 1)

def mlstm_chunk(carry, inp):
    C, n, m = carry
    q, k, v, ig, lf = inp
    L = q.shape[2]
    b = jnp.cumsum(lf, axis=-1)
    causal = jnp.tril(jnp.ones((L, L), dtype=bool))
    D = jnp.where(causal, b[..., :, None] - b[..., None, :] + ig[..., None, :], -jnp.inf)
    g = b + m[..., None]
    m_t = jnp.maximum(g, jnp.max(D, axis=-1))
    Dw = jnp.exp(D - m_t[..., None])
    gw = jnp.exp(g - m_t)
    S = jnp.einsum('bhtd,bhsd->bhts', q, k) * Dw
    num = jnp.einsum('bhts,bhsv->bhtv', S, v) + gw[..., None] * jnp.einsum('bhvd,bhtd->bhtv', C, q)
    nq = jnp.sum(S, axis=-1) + gw * jnp.einsum('bhd,bhtd->bht', n, q)
    h = num / jnp.maximum(jnp.abs(nq), jnp.exp(-m_t))[..., None]
    wL = Dw[..., -1, :]
    decay = gw[..., -1]
    C_new = decay[..., None, None] * C + jnp.einsum('bhs,bhsv,bhsd->bhvd', wL, v, k)
    n_new = decay[..., None] * n + jnp.einsum('bhs,bhsd->bhd', wL, k)
    return (C_new, n_new, m_t[..., -1]), h

def mix_output(attn, hm, mo, g_a, g_b, g_mnorm, w_ba, w_bb, w_out):
    B, H, T, dv = hm.shape
    hm = jnp.moveaxis(hm, 1, 2)
    hm = hm * lax.rsqrt(jnp.mean(hm * hm, axis=-1, keepdims=True) + EPS)
    hm = hm.reshape(B, T, H * dv).astype(mo.dtype) * g_mnorm * jax.nn.sigmoid(mo)
    y = jax.nn.sigmoid(g_a) * (attn @ w_ba) + jax.nn.sigmoid(g_b) * (hm @ w_bb)
    return y @ w_out

def token_mix_prompt(h, w_in, b_gates, g_mnorm, w_ba, w_bb, w_out):
    B, T, _ = h.shape
    aq, ak, av, iq, ik, iw, mq, mk, mv, ig, lf, mo, g_a, g_b = project(h, w_in, b_gates)
    pos = jnp.arange(T, dtype=jnp.int32)
    nb = T // QBLK
    top_k = min(TOPK_MAX, T // 4)

    def blk(a):
        return jnp.moveaxis(a.reshape((B, nb, QBLK) + a.shape[2:]), 1, 0)

    attn = lax.map(lambda xs: dsa_attend(*xs, ak, av, ik, top_k),
                   (blk(aq), blk(iq), blk(iw), pos.reshape(nb, QBLK)))
    attn = jnp.moveaxis(attn, 0, 1).reshape(B, T, N_HEADS_A * DH_A)
    q, k, v, igh, lfh = mlstm_heads(mq, mk, mv, ig, lf)
    nc = T // CHUNK

    def chk(a):
        return jnp.moveaxis(a.reshape(a.shape[:2] + (nc, CHUNK) + a.shape[3:]), 2, 0)

    init = (jnp.zeros((B, NH_M, DV_M, DK_M), jnp.float32), jnp.zeros((B, NH_M, DK_M), jnp.float32),
            jnp.zeros((B, NH_M), jnp.float32))
    (C, n, m), hs = lax.scan(mlstm_chunk, init, (chk(q), chk(k), chk(v), chk(igh), chk(lfh)))
    hm = jnp.moveaxis(hs, 0, 2).reshape(B, NH_M, T, DV_M)
    out = mix_output(attn, hm, mo, g_a, g_b, g_mnorm, w_ba, w_bb, w_out)
    return out, (ak, av, ik, C, n, m)

def token_mix_sample(h, cache_k, cache_v, cache_ik, s_C, s_n, s_m, w_in, b_gates, g_mnorm, w_ba, w_bb, w_out):
    B, T, _ = h.shape
    P = cache_k.shape[1]
    aq, ak, av, iq, ik, iw, mq, mk, mv, ig, lf, mo, g_a, g_b = project(h, w_in, b_gates)
    k_all = jnp.concatenate([cache_k, ak], axis=1)
    v_all = jnp.concatenate([cache_v, av], axis=1)
    ik_all = jnp.concatenate([cache_ik, ik], axis=1)
    t_pos = P + jnp.arange(T, dtype=jnp.int32)
    attn = dsa_attend(aq, iq, iw, t_pos, k_all, v_all, ik_all, min(TOPK_MAX, (P + T) // 4))
    attn = attn.reshape(B, T, N_HEADS_A * DH_A)
    q, k, v, igh, lfh = mlstm_heads(mq, mk, mv, ig, lf)
    carry = (s_C.astype(jnp.float32), s_n.astype(jnp.float32), s_m.astype(jnp.float32))
    (C, n, m), hm = mlstm_chunk(carry, (q, k, v, igh, lfh))
    out = mix_output(attn, hm, mo, g_a, g_b, g_mnorm, w_ba, w_bb, w_out)
    return out, (ak, av, ik, C, n, m)

def setup_inputs(seed: int = 0) -> dict:
    key = jax.random.key(seed)
    ks = jax.random.split(key, 24)
    nrm = jax.random.normal
    f32 = jnp.float32
    b_i = 0.1 * nrm(ks[10], (DEPTH, NH_M), f32)
    b_f = jnp.linspace(3.0, 6.0, NH_M, dtype=f32)[None, :] + 0.1 * nrm(ks[11], (DEPTH, NH_M), f32)
    return {
        'x_prompt': nrm(ks[0], (BATCH, SEQ, D_MODEL), f32),
        'x_sample': nrm(ks[1], (DEC_BATCH, DEC_SEQ, D_MODEL), f32),
        'cache_attn_k': nrm(ks[2], (DEPTH, DEC_BATCH, PAST_LEN, DH_A), f32),
        'cache_attn_v': nrm(ks[3], (DEPTH, DEC_BATCH, PAST_LEN, DH_A), f32),
        'cache_idx_k': nrm(ks[4], (DEPTH, DEC_BATCH, PAST_LEN, D_IDX), f32),
        'state_mlstm_C': 0.1 * nrm(ks[5], (DEPTH, DEC_BATCH, NH_M, DV_M, DK_M), f32),
        'state_mlstm_n': 0.1 * nrm(ks[6], (DEPTH, DEC_BATCH, NH_M, DK_M), f32),
        'state_mlstm_m': nrm(ks[7], (DEPTH, DEC_BATCH, NH_M), f32),
        'norm_ffn1': 1.0 + 0.01 * nrm(ks[8], (DEPTH, D_MODEL), f32),
        'w_ffn1_up': nrm(ks[9], (DEPTH, D_MODEL, 2 * D_FF), f32) * D_MODEL ** -0.5,
        'w_ffn1_down': nrm(ks[12], (DEPTH, D_FF, D_MODEL), f32) * D_FF ** -0.5,
        'norm_mix': 1.0 + 0.01 * nrm(ks[13], (DEPTH, D_MODEL), f32),
        'w_in': nrm(ks[14], (DEPTH, D_MODEL, D_IN), f32) * D_MODEL ** -0.5,
        'b_mlstm_gates': jnp.concatenate([b_i, b_f], axis=-1),
        'norm_mlstm_heads': 1.0 + 0.01 * nrm(ks[15], (DEPTH, NH_M * DV_M), f32),
        'w_branch_attn': nrm(ks[16], (DEPTH, N_HEADS_A * DH_A, D_MODEL), f32) * (N_HEADS_A * DH_A) ** -0.5,
        'w_branch_mlstm': nrm(ks[17], (DEPTH, NH_M * DV_M, D_MODEL), f32) * (NH_M * DV_M) ** -0.5,
        'w_out': nrm(ks[18], (DEPTH, D_MODEL, D_MODEL), f32) * D_MODEL ** -0.5,
        'norm_ffn2': 1.0 + 0.01 * nrm(ks[19], (DEPTH, D_MODEL), f32),
        'w_ffn2_up': nrm(ks[20], (DEPTH, D_MODEL, 2 * D_FF), f32) * D_MODEL ** -0.5,
        'w_ffn2_down': nrm(ks[21], (DEPTH, D_FF, D_MODEL), f32) * D_FF ** -0.5,
        'norm_final': 1.0 + 0.01 * nrm(ks[22], (D_MODEL,), f32),
    }

def reference(x_prompt, x_sample, cache_attn_k, cache_attn_v, cache_idx_k, state_mlstm_C, state_mlstm_n,
              state_mlstm_m, norm_ffn1, w_ffn1_up, w_ffn1_down, norm_mix, w_in, b_mlstm_gates, norm_mlstm_heads,
              w_branch_attn, w_branch_mlstm, w_out, norm_ffn2, w_ffn2_up, w_ffn2_down, norm_final):
    xp, xs = x_prompt, x_sample
    new_p = [[] for _ in range(6)]
    new_s = [[] for _ in range(6)]
    for l in range(DEPTH):
        xp = half_ffn(xp, norm_ffn1[l], w_ffn1_up[l], w_ffn1_down[l])
        xs = half_ffn(xs, norm_ffn1[l], w_ffn1_up[l], w_ffn1_down[l])
        mix_w = (w_in[l], b_mlstm_gates[l], norm_mlstm_heads[l], w_branch_attn[l], w_branch_mlstm[l], w_out[l])
        out_p, st_p = token_mix_prompt(rmsnorm(xp, norm_mix[l]), *mix_w)
        out_s, st_s = token_mix_sample(rmsnorm(xs, norm_mix[l]), cache_attn_k[l], cache_attn_v[l], cache_idx_k[l],
                                       state_mlstm_C[l], state_mlstm_n[l], state_mlstm_m[l], *mix_w)
        xp = xp + out_p
        xs = xs + out_s
        xp = half_ffn(xp, norm_ffn2[l], w_ffn2_up[l], w_ffn2_down[l])
        xs = half_ffn(xs, norm_ffn2[l], w_ffn2_up[l], w_ffn2_down[l])
        for i in range(6):
            new_p[i].append(st_p[i])
            new_s[i].append(st_s[i])
    y_prompt = rmsnorm(xp, norm_final)
    y_sample = rmsnorm(xs, norm_final)
    new_k_prompt = jnp.stack(new_p[0]).astype(cache_attn_k.dtype)
    new_v_prompt = jnp.stack(new_p[1]).astype(cache_attn_v.dtype)
    new_idxk_prompt = jnp.stack(new_p[2]).astype(cache_idx_k.dtype)
    new_C_prompt = jnp.stack(new_p[3]).astype(state_mlstm_C.dtype)
    new_n_prompt = jnp.stack(new_p[4]).astype(state_mlstm_n.dtype)
    new_m_prompt = jnp.stack(new_p[5]).astype(state_mlstm_m.dtype)
    new_k_sample = jnp.stack(new_s[0]).astype(cache_attn_k.dtype)
    new_v_sample = jnp.stack(new_s[1]).astype(cache_attn_v.dtype)
    new_idxk_sample = jnp.stack(new_s[2]).astype(cache_idx_k.dtype)
    new_C_sample = jnp.stack(new_s[3]).astype(state_mlstm_C.dtype)
    new_n_sample = jnp.stack(new_s[4]).astype(state_mlstm_n.dtype)
    new_m_sample = jnp.stack(new_s[5]).astype(state_mlstm_m.dtype)
    return (y_prompt, y_sample, new_k_prompt, new_v_prompt, new_idxk_prompt, new_C_prompt, new_n_prompt,
            new_m_prompt, new_k_sample, new_v_sample, new_idxk_sample, new_C_sample, new_n_sample, new_m_sample)


_drawn_inputs = setup_inputs


def setup_inputs(seed=0):
    import zlib

    import numpy as np

    out = dict(_drawn_inputs(seed))
    spreads = {}
    factors = {'state_mlstm_n': 3.374,
     'state_mlstm_m': 3.124,
     'norm_mlstm_heads': 152.231,
     'norm_ffn2': 127.609,
     'norm_final': 179.684,
     'norm_ffn1': 3.48,
     'cache_attn_k': 5.206,
     'cache_attn_v': 3.767,
     'cache_idx_k': 3.795}
    for name, (base, spread) in spreads.items():
        noise = np.random.default_rng([zlib.crc32(name.encode()), seed]).standard_normal(out[name].shape)
        drawn = base * np.exp(spread * noise) if base else spread * noise
        out[name] = __import__('jax').numpy.asarray(drawn.astype(out[name].dtype))
    for name, factor in factors.items():
        out[name] = (out[name] * factor).astype(out[name].dtype)
    return out
```

```python
from contextlib import ExitStack, contextmanager

import numpy as np

import concourse.bass as bass
from concourse import mybir

F32 = mybir.dt.float32
F32R = mybir.dt.float32r
ALU = mybir.AluOpType
ACT = mybir.ActivationFunctionType
AX_X = mybir.AxisListType.X

P = 128
D_MODEL = 1024
KT = D_MODEL // P
SEQ = 1024
DEC_BATCH = 8
DEC_SEQ = 16
PAST = 512
N_TOK = SEQ + DEC_BATCH * DEC_SEQ
NT = N_TOK // P
NTP = SEQ // P
CH = 384
NCH = N_TOK // CH
CHUNK = 64
HA = 8
DH = 64
NI = 4
TOPK = 256
TOPK_S = (PAST + DEC_SEQ) // 4
HM = 4
DV = 128
D_FF = 2816
FT = D_FF // P
FG = 2
NG = FT // FG
EPS = 1e-6
IDX_SCALE = (NI * DH) ** -0.5
QK_SCALE = DH ** -0.5
LS = PAST + DEC_SEQ
BIG = 1e30
TAKEN = -3.4e38
BLOCKED = -3.0e38
FIRST_SEL = TOPK // P
SCORE_OFF = {}
_at = 0
for _b in range(NTP):
    SCORE_OFF[_b] = _at
    _at += P * (_b + 1)
SCORE_OFF[NTP] = _at
SCORE_COLS = _at + LS

C_AQ, C_AK, C_IQ, C_IK, C_MQ, C_MI, C_MO = 0, 512, 640, 896, 964, 1988, 1996
N_PLAIN = 8
N_SIG = 20


def constants():
    c = {}
    c["ident"] = np.eye(P, dtype=np.float32)
    p, x = np.arange(P)[:, None], np.arange(SEQ)[None, :]
    c["dist_p"] = np.abs(p + SEQ - P - x).astype(np.float32)
    c["dist_s"] = np.abs(PAST + p % DEC_SEQ - np.arange(LS)[None, :]).astype(np.float32)
    b_of = np.arange(P) // DEC_SEQ
    par = (np.arange(P) // 64)[:, None, None]
    c["pair_mask"] = (b_of[None, None, :] == 2 * np.arange(4)[None, :, None] + par).astype(np.float32)
    c["batch_mask"] = (b_of[:, None] == np.arange(DEC_BATCH)[None, :]).astype(np.float32)
    s, t = np.arange(P)[:, None], np.arange(P)[None, :]
    c["causal_p"] = np.where(s <= t, 0, -BIG).astype(np.float32)
    c["causal_s"] = np.where((s <= t) & (s // DEC_SEQ == t // DEC_SEQ), 0, -BIG).astype(np.float32)
    sel = np.zeros((HM, HM, P), np.float32)
    for h in range(HM):
        sel[h, h] = 1
    c["head_sel"] = sel
    keep = np.ones((HM, N_TOK), np.float32)
    keep[:, 0:SEQ:P] = 0
    keep[:, SEQ::DEC_SEQ] = 0
    c["keep"] = keep
    return c


class Scope:

    def __init__(self, stack, numbers):
        self.stack, self.numbers = stack, numbers

    def enter_context(self, guard):
        got = self.stack.enter_context(guard)
        self.numbers.append(got.num)
        return got


class Sbuf:

    def __init__(self, nc):
        self.nc, self.low_end, self.high_end = nc, (nc.sbuf_base + 63) // 64 * 64, nc.sbuf_usable_end // 64 * 64

    def low(self, name, shape, dt=F32):
        at = self.low_end
        self.low_end += (int(np.prod(shape[1:])) * 4 + 63) // 64 * 64
        assert self.low_end <= self.high_end, (name, self.low_end, self.high_end)
        return self.nc.alloc_sbuf_tensor_at(name, shape, dt, offset=at)

    def high(self, name, shape, dt=F32):
        self.high_end -= (int(np.prod(shape[1:])) * 4 + 63) // 64 * 64
        assert self.low_end <= self.high_end, (name, self.low_end, self.high_end)
        return self.nc.alloc_sbuf_tensor_at(name, shape, dt, offset=self.high_end)

    @contextmanager
    def scope(self):
        ends = self.low_end, self.high_end
        yield
        self.low_end, self.high_end = ends


def psum(nc, ctx, name, shape, dt=F32):
    return ctx.enter_context(nc.psum_tensor(name, shape, dt))


def load_and_norm(nc, ctx, M, K, io, xT, xn_hi, xn_lo, rB):
    sem = lambda n: ctx.enter_context(nc.semaphore("a_" + n))
    with ExitStack() as mem, M.scope():
        xt = M.low("x_tok", [P, 2, D_MODEL])
        junk = M.low("x_sq", [P, D_MODEL])
        grow = M.low("gain_rows", [P, P])
        NG_ROWS = 3 * KT + HM
        pg = psum(nc, mem, "gain_tp", [P, P])
        pt = psum(nc, mem, "x_tp", [P, 4, 512])
        x_in = [sem("x_in0"), sem("x_in1")]
        ssq, tp, tpg, ev, c_in, ones_ok = (sem(n) for n in ("ssq", "tp", "tpg", "ev", "c_in", "ones"))
        with nc.Block() as block:
            @block.sync
            def _(sp):
                sp.dma_start(K["ident"][:], io["ident"]).then_inc(c_in, 16)
                for n, k in enumerate(("ffn1", "mix", "ffn2")):
                    sp.dma_start(grow[n * KT:(n + 1) * KT, :],
                                 io["norm_" + k][0].rearrange("(k p) -> k p", p=P)).then_inc(c_in, 16)
                sp.dma_start(grow[3 * KT:3 * KT + HM, :],
                             io["norm_mlstm_heads"][0].rearrange("(k p) -> k p", p=P)).then_inc(c_in, 16)
                for t in range(NT):
                    if t >= 2:
                        sp.wait_ge(ssq, t - 1)
                        sp.wait_ge(tp, 2 * (t - 1))
                    src = io["x_prompt"][0, t * P:(t + 1) * P, :] if t < NTP else \
                        io["x_sample"].rearrange("b q d -> (b q) d")
                    sp.dma_start(xt[:, t % 2, :], src).then_inc(x_in[t % 2], 16)

            @block.scalar
            def _(act):
                for t in range(NT):
                    act.wait_ge(x_in[t % 2], 16 * (t // 2 + 1))
                    if t:
                        act.wait_ge(ssq, t)
                    nc.scalar.activation(junk[:], xt[:, t % 2, :], ACT.Square,
                                         accum_out=K["ssq"][:, t:t + 1]).then_inc(ssq, 1)

            @block.gpsimd
            def _(pool):
                nc.gpsimd.memset(K["ones"][:], 1.0).then_inc(ones_ok, 1)
                pool.wait_ge(ones_ok, 1)

            @block.tensor
            def _(pe):
                pe.wait_ge(c_in, 80)
                nc.tensor.transpose(pg[:, 0:NG_ROWS], grow[0:NG_ROWS, :],
                                    K["ident"][0:NG_ROWS, 0:NG_ROWS]).then_inc(tpg, 1)
                for t in range(NT):
                    pe.wait_ge(x_in[t % 2], 16 * (t // 2 + 1))
                    for half in range(2):
                        n = 2 * t + half
                        if n >= 4:
                            pe.wait_ge(ev, n - 2)
                        for j in range(4):
                            last = nc.tensor.transpose(pt[:, n % 4, j * P:(j + 1) * P],
                                                       xt[:, t % 2, (4 * half + j) * P:(4 * half + j + 1) * P],
                                                       K["ident"][:])
                        last.then_inc(tp, 1)

            @block.vector
            def _(dve):
                dve.wait_ge(tpg, 1)
                nc.vector.tensor_copy(K["gains"][:, 0:NG_ROWS], pg[:, 0:NG_ROWS]).then_inc(ev, 1)
                for n in range(2 * NT):
                    t, half = n // 2, n % 2
                    dve.wait_ge(tp, n + 1)
                    nc.vector.tensor_copy(xT[:, 4 * half:4 * half + 4, t * P:(t + 1) * P],
                                          pt[:, n % 4, :].rearrange("p (j t) -> p j t", j=4)).then_inc(ev, 1)


def feature_stats(nc, ctx, M, K, xT, tag):
    with ExitStack() as mem, M.scope():
        sq = M.low(tag + "sq", [P, 2, N_TOK])
        ps = psum(nc, mem, tag + "ss", [P, NT, 1])
        sq_ok, mm, done = (ctx.enter_context(nc.semaphore(tag + n)) for n in ("sq_ok", "mm", "done"))
        acc = M.low(tag + "acc", [P, N_TOK])
        with nc.Block() as block:
            @block.scalar
            def _(act):
                for k in range(KT):
                    if k >= 2:
                        act.wait_ge(mm, k - 1)
                    nc.scalar.activation(sq[:, k % 2, :], xT[:, k, :], ACT.Square).then_inc(sq_ok, 1)

            @block.vector
            def _(dve):
                for k in range(KT):
                    dve.wait_ge(sq_ok, k + 1)
                    if k == 0:
                        nc.vector.tensor_copy(acc[:], sq[:, 0, :]).then_inc(mm, 1)
                    else:
                        dve.wait_ge(mm, k)
                        nc.vector.tensor_tensor(acc[:], acc[:], sq[:, k % 2, :], ALU.add).then_inc(mm, 1)
                dve.wait_ge(done, 1)
                nc.vector.tensor_copy(K["ssq"][:], ps[:, :, 0]).then_inc(done, 1)
                dve.wait_ge(done, 2)

            @block.tensor
            def _(pe):
                pe.wait_ge(mm, KT)
                for t in range(NT):
                    last = nc.tensor.matmul(ps[:, t, :], acc[:, t * P:(t + 1) * P], K["ones"][:, 0:1],
                                            start=True, stop=True)
                last.then_inc(done, 1)


def apply_norm(nc, ctx, M, K, xT, gain, xn_hi, xn_lo, tag):
    with ExitStack() as mem, M.scope():
        diag = M.low(tag + "diag", [P, NT, P])
        full = M.low(tag + "full", [P, 2, N_TOK])
        rB = psum(nc, mem, tag + "rB", [P, NCH, 512])
        ch, inv, rt, dg, bc, f_ok, hi, lo = (ctx.enter_context(nc.semaphore(tag + n)) for n in
                                             ("ch", "inv", "rt", "dg", "bc", "f_ok", "hi", "lo"))
        rv = rB[:, :, 0:CH]
        with nc.Block() as block:
            @block.vector
            def _(dve):
                nc.vector.tensor_scalar(K["st1"][:], K["ssq"][:], 1.0 / D_MODEL, EPS,
                                        ALU.mult, ALU.add).then_inc(ch, 1)
                dve.wait_ge(ch, 1)
                nc.vector.reciprocal(K["st2"][:], K["st1"][:]).then_inc(inv, 1)
                dve.wait_ge(rt, 1)
                for t in range(NT):
                    nc.vector.tensor_scalar(diag[:, t, :], K["ident"][:], K["st3"][:, t:t + 1], None,
                                            ALU.mult).then_inc(dg, 1)
                dve.wait_ge(bc, 1)
                for k in range(KT):
                    if k >= 2:
                        dve.wait_ge(hi, k - 1)
                        dve.wait_ge(lo, k - 1)
                    nc.vector.scalar_tensor_tensor(full[:, k % 2, :].rearrange("p (c n) -> p c n", c=NCH),
                                                   xT[:, k, :].rearrange("p (c n) -> p c n", c=NCH),
                                                   gain[:, k:k + 1], rv, ALU.mult, ALU.mult).then_inc(f_ok, 1)

            @block.scalar
            def _(act):
                act.wait_ge(inv, 1)
                nc.scalar.activation(K["st3"][:], K["st2"][:], ACT.Sqrt).then_inc(rt, 1)
                for k in range(KT):
                    act.wait_ge(f_ok, k + 1)
                    nc.scalar.activation(xn_hi[:, k, :], full[:, k % 2, :], ACT.Copy).then_inc(hi, 1)

            @block.gpsimd
            def _(pool):
                for k in range(KT):
                    pool.wait_ge(hi, k + 1)
                    nc.gpsimd.tensor_tensor(xn_lo[:, k, :], full[:, k % 2, :], xn_hi[:, k, :].bitcast(F32),
                                            ALU.subtract).then_inc(lo, 1)

            @block.tensor
            def _(pe):
                pe.wait_ge(dg, NT)
                for c in range(NCH):
                    last = nc.tensor.matmul(rB[:, c, 0:CH], K["ones"][:],
                                            diag[:, 3 * c:3 * c + 3, :].rearrange("p a b -> p (a b)"),
                                            start=True, stop=True)
                last.then_inc(bc, 1)


def product3(nc, out, w_hi, w_lo, x_hi, x_lo, first, final):
    nc.tensor.matmul(out, w_hi, x_lo, start=first, stop=False)
    nc.tensor.matmul(out, w_lo, x_hi, start=False, stop=False)
    return nc.tensor.matmul(out, w_hi, x_hi, start=False, stop=final)


def ffn(nc, ctx, M, K, w_up, w_down, xT, xn_hi, xn_lo, tag):
    sem = lambda n: ctx.enter_context(nc.semaphore(tag + n))
    PAIRS = [("up", 0), ("up", 1), ("up", 2), ("up", 3), ("down", 0), ("up", 4), ("up", 5), ("down", 1)]
    LAST = ("down", 2)
    PER = {"up": 4, "down": 2}
    BODIES = (NG - 1) // 2
    ND = KT * NCH
    with ExitStack() as mem, M.scope():
        raw = M.low(tag + "raw", [P, 2, 2, KT, P])
        w_hi = M.low(tag + "w_hi", [P, 2, 2, KT, P], F32R)
        w_lo = M.low(tag + "w_lo", [P, 2, 2, KT, P], F32R)
        h_hi = M.low(tag + "h_hi", [P, 2, FG, N_TOK], F32R)
        h_lo = M.low(tag + "h_lo", [P, 2, FG, N_TOK], F32R)
        gate = M.low(tag + "gate", [P, 2, CH])
        hid = M.low(tag + "hid", [P, 2, CH])
        ps_up = psum(nc, mem, tag + "ps_up", [P, 3, 2, 512])
        ps_dn = psum(nc, mem, tag + "ps_dn", [P, 2, 512])
        w_in = [sem("w_in0"), sem("w_in1")]
        hi_ok, lo_ok = sem("hi_ok"), sem("lo_ok")
        up_ok, gate_ok, hid_ok = sem("up_ok"), sem("gate_ok"), sem("hid_ok")
        hhi_ok, hlo_ok = sem("hhi_ok"), sem("hlo_ok")
        dn_ok, dn_ev = sem("dn_ok"), sem("dn_ev")

        up_v = w_up[0].rearrange("(k p) n -> p k n", p=P)
        dn_v = w_down[0].rearrange("(k p) n -> p k n", p=P)

        def wait_multiplied(eng, i, n0):
            kind, m = PAIRS[n0]
            if n0 == 1:
                eng.wait_ge(dn_ok, i * (ND * 2))
            if kind == "up":
                eng.wait_ge(up_ok, i * (NCH * 4) + NCH * (m + 1))
            else:
                eng.wait_ge(dn_ok, i * (ND * 2) + ND * (m + 1))

        def load(sp, i, n0, kind, m):
            if n0 >= 2:
                sp.wait_ge(lo_ok, i * 6 + (n0 - 1))
            m = i * PER[kind] + m
            if kind == "up":
                for u in range(2):
                    sp.dma_start(raw[:, n0 % 2, u], up_v[:, :, bass.ds(m * P + u * D_FF, P)])\
                        .then_inc(w_in[n0 % 2], 16)
            else:
                sp.dma_start(raw[:, n0 % 2].rearrange("p u k n -> p u (k n)"), dn_v[:, bass.ds(m * FG, FG), :])\
                    .then_inc(w_in[n0 % 2], 32)

        def slot(t, n0):
            return t[:, n0 % 2].rearrange("p u k n -> p (u k n)")

        def split_hi(act, i, n0):
            act.wait_ge(w_in[n0 % 2], i * 96 + 32 * (n0 // 2 + 1))
            if n0 >= 2:
                wait_multiplied(act, i, n0 - 2)
            nc.scalar.activation(slot(w_hi, n0), slot(raw, n0), ACT.Copy).then_inc(hi_ok, 1)

        def split_lo(pool, i, n0):
            pool.wait_ge(hi_ok, i * 6 + (n0 + 1))
            nc.gpsimd.tensor_tensor(slot(w_lo, n0), slot(raw, n0), slot(w_hi, n0).bitcast(F32),
                                    ALU.subtract).then_inc(lo_ok, 1)

        def run(eng, loop, before, pair):
            before(0, 0)
            for n0 in range(2):
                before(0, n0 + 1)
                pair(0, n0, *PAIRS[n0])
            with loop(0, BODIES) as i:
                for n0 in range(2, 8):
                    before(i, n0 + 1)
                    pair(i, n0, *PAIRS[n0])
            pair(BODIES - 1, 8, *LAST)

        with nc.Block() as block:
            @block.sync
            def _(sp):
                load(sp, 0, 0, "up", 0)
                load(sp, 0, 1, "up", 1)
                with nc.sync.Fori(0, BODIES) as i:
                    for n0 in range(2, 8):
                        load(sp, i, n0, *PAIRS[n0])
                load(sp, BODIES - 1, 8, *LAST)

            @block.scalar
            def _(act):
                def pair(i, n0, kind, m):
                    if kind == "down":
                        return
                    for c in range(NCH):
                        q0 = NCH * m + c
                        q = i * (NCH * 4) + q0
                        act.wait_ge(up_ok, q + 1)
                        if q0 >= 2:
                            act.wait_ge(hid_ok, q - 1)
                        nc.scalar.activation(gate[:, q0 % 2], ps_up[:, c, 0, 0:CH], ACT.Silu).then_inc(gate_ok, 1)
                        act.wait_ge(hid_ok, q + 1)
                        nc.scalar.activation(h_hi[:, m // 2 % 2, m % 2, c * CH:(c + 1) * CH], hid[:, q0 % 2],
                                             ACT.Copy).then_inc(hhi_ok, 1)
                run(act, nc.scalar.Fori, lambda i, n0: split_hi(act, i, n0), pair)

            @block.gpsimd
            def _(pool):
                def pair(i, n0, kind, m):
                    if kind == "down":
                        return
                    for c in range(NCH):
                        q0 = NCH * m + c
                        pool.wait_ge(hhi_ok, i * (NCH * 4) + (q0 + 1))
                        out = slice(c * CH, (c + 1) * CH)
                        nc.gpsimd.tensor_tensor(h_lo[:, m // 2 % 2, m % 2, out], hid[:, q0 % 2],
                                                h_hi[:, m // 2 % 2, m % 2, out].bitcast(F32),
                                                ALU.subtract).then_inc(hlo_ok, 1)
                run(pool, nc.gpsimd.Fori, lambda i, n0: split_lo(pool, i, n0), pair)

            @block.vector
            def _(dve):
                def pair(i, n0, kind, m):
                    if kind == "up":
                        for c in range(NCH):
                            q0 = NCH * m + c
                            q = i * (NCH * 4) + q0
                            dve.wait_ge(gate_ok, q + 1)
                            if q0 >= 2:
                                dve.wait_ge(hlo_ok, q - 1)
                            nc.vector.tensor_tensor(hid[:, q0 % 2], gate[:, q0 % 2], ps_up[:, c, 1, 0:CH],
                                                    ALU.mult).then_inc(hid_ok, 1)
                    else:
                        for r in range(ND):
                            k, c = r // NCH, r % NCH
                            dve.wait_ge(dn_ok, i * (ND * 2) + (ND * m + r + 1))
                            x = xT[:, k, c * CH:(c + 1) * CH]
                            nc.vector.scalar_tensor_tensor(x, ps_dn[:, r % 2, 0:CH], 0.5, x,
                                                           ALU.mult, ALU.add).then_inc(dn_ev, 1)
                            if r == ND - 1:
                                dve.wait_ge(dn_ev, i * (ND * 2) + ND * (m + 1))
                run(dve, nc.vector.Fori, lambda i, n0: None, pair)

            @block.tensor
            def _(pe):
                def pair(i, n0, kind, m):
                    pe.wait_ge(lo_ok, i * 6 + (n0 + 1))
                    s = n0 % 2
                    if kind == "up":
                        for c in range(NCH):
                            q0 = NCH * m + c
                            if q0 >= 3:
                                pe.wait_ge(hid_ok, i * (NCH * 4) + (q0 - 2))
                            tok = slice(c * CH, (c + 1) * CH)
                            for u in range(2):
                                for k in range(KT):
                                    last = product3(nc, ps_up[:, c, u, 0:CH], w_hi[:, s, u, k], w_lo[:, s, u, k],
                                                    xn_hi[:, k, tok], xn_lo[:, k, tok], k == 0, k == KT - 1)
                            last.then_inc(up_ok, 1)
                    else:
                        pe.wait_ge(hlo_ok, i * (NCH * 4) + NCH * FG * (m + 1))
                        for r in range(ND):
                            k, c = r // NCH, r % NCH
                            if ND * m + r >= 2:
                                pe.wait_ge(dn_ev, i * (ND * 2) + (ND * m + r - 1))
                            tok = slice(c * CH, (c + 1) * CH)
                            for j in range(FG):
                                last = product3(nc, ps_dn[:, r % 2, 0:CH], w_hi[:, s, j, k], w_lo[:, s, j, k],
                                                h_hi[:, m % 2, j, tok], h_lo[:, m % 2, j, tok],
                                                j == 0, j == FG - 1)
                            last.then_inc(dn_ok, 1)
                run(pe, nc.tensor.Fori, lambda i, n0: None, pair)


def cache_index_keys(nc, ctx, M, K, io, xT, x_dram, KTi):
    with ExitStack() as mem, M.scope():
        raw = M.low("ik_raw", [P, PAST // P, DEC_BATCH, DH])
        ps = psum(nc, mem, "ik_tp", [P, 4, 512])
        ld, tp, ev, st = (ctx.enter_context(nc.semaphore("c_" + n)) for n in ("ld", "tp", "ev", "st"))
        with nc.Block() as block:
            @block.sync
            def _(sp):
                for b in range(DEC_BATCH):
                    sp.dma_start(raw[:, :, b, :], io["cache_idx_k"][0, b].rearrange("(k p) d -> p k d", p=P))\
                        .then_inc(ld, 16)
                for n in ("dist_p", "dist_s", "pair_mask"):
                    sp.dma_start(K[n][:], io[n]).then_inc(ld, 16)
                sp.dma_start(x_dram.ap(), xT[:]).then_inc(st, 16)
                sp.wait_ge(st, 16)
                sp.wait_ge(ld, 16 * (DEC_BATCH + 3))

            @block.tensor
            def _(pe):
                pe.wait_ge(ld, 16 * (DEC_BATCH + 3))
                for j in range(DEC_BATCH // 2):
                    for k in range(PAST // P):
                        last = nc.tensor.transpose(ps[:, j, k * P:(k + 1) * P],
                                                   raw[:, k, 2 * j:2 * j + 2, :].rearrange("p b d -> p (b d)"),
                                                   K["ident"][:])
                    last.then_inc(tp, 1)

            @block.vector
            def _(dve):
                for j in range(DEC_BATCH // 2):
                    dve.wait_ge(tp, j + 1)
                    nc.vector.tensor_copy(KTi[:, j, 0:PAST], ps[:, j, :]).then_inc(ev, 1)


def project(nc, ctx, M, K, io, out, xn_hi, xn_lo, aq, kvT, KTi, DM, scratch):
    sem = lambda n: ctx.enter_context(nc.semaphore("d_" + n))
    COLS = [C_IQ, C_IQ + P, C_IK, C_AQ, C_AQ + P, C_AQ + 2 * P, C_AQ + 3 * P, C_AK, C_MI]
    HEAD, LOOP1, MID, LOOP2, TAIL = range(9), (9, N_PLAIN // 2 - 1), (15, 16), (17, N_SIG // 2 - 1), (35, 36)
    N_CHIP = 8
    TILES = [7, 6, 5, 4, 3, 2, NTP]
    with ExitStack() as mem, M.scope():
        raw = M.low("d_raw", [P, 2, KT, P])
        w_hi = M.low("d_w_hi", [P, 2, KT, P], F32R)
        w_lo = M.low("d_w_lo", [P, 2, KT, P], F32R)
        iq = M.low("iq", [P, 2, N_TOK])
        ikw = M.low("ikw", [P, N_TOK])
        ikd = M.low("ikd", [P, N_TOK])
        iqd = M.low("iqd", [P, NI, P])
        iqm = M.low("iqm", [P, NI, 4, P])
        rel = M.low("rel", [P, 2, SEQ])
        stage = M.low("stage", [P, 2, N_TOK])
        tok_ik = M.low("tok_ik", [P, NT, DH + NI])
        top8 = M.low("top8", [P, 8])
        ps = psum(nc, mem, "d_ps", [P, NCH, 512])
        ps_s = psum(nc, mem, "d_ps_s", [P, 2, 1024])
        ps_t = psum(nc, mem, "d_ps_t", [P, 4, P])
        w_in, st_out = [sem("w_in0"), sem("w_in1")], [sem("st_out0"), sem("st_out1")]
        hi_ok, lo_ok, mm_ok, ev_ok = sem("hi_ok"), sem("lo_ok"), sem("mm_ok"), sem("ev_ok")
        dup, kcol, tp, tp_ev, o_out = sem("dup"), sem("kcol"), sem("tp"), sem("tp_ev"), sem("o_out")
        im_ok, sc_ok, rel_ok, acc_ok, ch = sem("im_ok"), sem("sc_ok"), sem("rel_ok"), sem("acc_ok"), sem("ch")
        w_v = io["w_in"][0].rearrange("(k p) n -> p k n", p=P)
        sc_v = scratch.ap()

        def run(eng, loop, before, unit, scores=lambda: None):
            before(0, 0)
            for n0 in HEAD:
                before(0, n0 + 1)
                unit(0, n0)
                if n0 == 3:
                    scores()
            for (first, bodies), then in ((LOOP1, MID), (LOOP2, ())):
                with loop(0, bodies) as i:
                    for n0 in (first, first + 1):
                        before(i, n0 + 1)
                        unit(i, n0)
                for n0 in then:
                    before(0, n0 + 1)
                    unit(0, n0)
            before(0, TAIL[1])
            unit(0, TAIL[0])
            unit(0, TAIL[1])

        def score_dims(t):
            return (LS if t == NTP else P * (t + 1)), SCORE_OFF[t]

        with nc.Block() as block:
            @block.sync
            def _(sp):
                def load(i, n0):
                    if n0 >= 2:
                        sp.wait_ge(lo_ok, i * 2 + (n0 - 1))
                    if n0 < len(COLS):
                        src = w_v[:, :, COLS[n0]:COLS[n0] + P]
                    elif n0 < 17:
                        src = w_v[:, :, bass.ds(i * (2 * P) + (C_MQ + (n0 - 9) * P), P)]
                    else:
                        src = w_v[:, :, bass.ds(i * (2 * P) + (C_MO + (n0 - 17) * P), P)]
                    sp.dma_start(raw[:, n0 % 2], src).then_inc(w_in[n0 % 2], 16)

                def store(i, n0):
                    if n0 < N_CHIP:
                        return
                    sp.wait_ge(ev_ok, i * (2 * NCH) + NCH * (n0 + 1))
                    tile = N_PLAIN + N_SIG if n0 == 8 else i * 2 + (n0 - 9)
                    dst = sc_v[tile] if isinstance(tile, int) else \
                        sc_v[bass.ds(tile, 1)].rearrange("a p n -> p (a n)")
                    sp.dma_start(dst, stage[:, n0 % 2]).then_inc(st_out[n0 % 2], 16)

                def copies():
                    sp.wait_ge(ev_ok, 3 * NCH)
                    for half in range(2):
                        rows = slice(64 * half, 64 * half + 64)
                        sp.dma_start(ikd[rows, :], ikw[0:DH, :]).then_inc(dup, 16)
                        for par in range(2):
                            sp.dma_start(iqd[rows, par::2, :], iq[64 * par:64 * par + 64, :, SEQ:N_TOK])\
                                .then_inc(dup, 16)
                        new = ikw[0:DH, SEQ:N_TOK].rearrange("d (j r q) -> d j r q", r=2, q=DEC_SEQ)
                        sp.dma_start(KTi[rows, :, PAST:LS], new[:, :, half, :]).then_inc(kcol, 16)
                    sp.wait_ge(tp_ev, 3)
                    sp.dma_start(out["new_idxk_prompt"][0, 0].rearrange("(t p) d -> p t d", p=P),
                                 tok_ik[:, 0:NTP, 0:DH]).then_inc(o_out, 16)
                    sp.dma_start(out["new_idxk_sample"][0].rearrange("b q d -> (b q) d"),
                                 tok_ik[:, NTP, 0:DH]).then_inc(o_out, 16)
                run(sp, nc.sync.Fori, load, store, copies)
                for s in range(2):
                    sp.wait_ge(st_out[s], 16 * ((29 + 1 - s) // 2))
                sp.wait_ge(o_out, 32)

            @block.scalar
            def _(act):
                def split_hi(i, n0):
                    act.wait_ge(w_in[n0 % 2], i * 16 + 16 * (n0 // 2 + 1))
                    if n0 >= 2:
                        act.wait_ge(mm_ok, i * (2 * NCH) + NCH * (n0 - 1))
                    nc.scalar.activation(w_hi[:, n0 % 2], raw[:, n0 % 2], ACT.Copy).then_inc(hi_ok, 1)

                def evict(i, n0):
                    if n0 >= N_CHIP + 2:
                        act.wait_ge(st_out[n0 % 2], i * 16 + 16 * ((n0 - N_CHIP) // 2))
                    for c in range(NCH):
                        act.wait_ge(mm_ok, i * (2 * NCH) + (NCH * n0 + c + 1))
                        tok = slice(c * CH, (c + 1) * CH)
                        if n0 < 2:
                            dst = iq[:, n0, tok]
                        elif n0 == 2:
                            dst = ikw[:, tok]
                        elif n0 < 7:
                            dst = aq[:, n0 - 3, tok]
                        elif n0 == 7:
                            dst = kvT[:, tok]
                        else:
                            dst = stage[:, n0 % 2, tok]
                        nc.scalar.activation(dst, ps[:, c, 0:CH], ACT.Sigmoid if n0 >= 17 else ACT.Copy)\
                            .then_inc(ev_ok, 1)

                def scores():
                    g = 0
                    for t in TILES:
                        L, _ = score_dims(t)
                        for h in range(NI):
                            act.wait_ge(sc_ok, g + 1)
                            if g >= 2:
                                act.wait_ge(acc_ok, g - 1)
                            nc.scalar.activation(rel[:, g % 2, 0:L], ps_s[:, g % 2, 0:L], ACT.Relu,
                                                 scale=IDX_SCALE).then_inc(rel_ok, 1)
                            g += 1
                run(act, nc.scalar.Fori, split_hi, evict, scores)

            @block.gpsimd
            def _(pool):
                def split_lo(i, n0):
                    pool.wait_ge(hi_ok, i * 2 + (n0 + 1))
                    nc.gpsimd.tensor_tensor(w_lo[:, n0 % 2], raw[:, n0 % 2], w_hi[:, n0 % 2].bitcast(F32),
                                            ALU.subtract).then_inc(lo_ok, 1)
                run(pool, nc.gpsimd.Fori, split_lo, lambda i, n0: None)

            @block.tensor
            def _(pe):
                def unit(i, n0):
                    pe.wait_ge(lo_ok, i * 2 + (n0 + 1))
                    for c in range(NCH):
                        if n0:
                            pe.wait_ge(ev_ok, i * (2 * NCH) + (NCH * n0 + c - 2))
                        tok = slice(c * CH, (c + 1) * CH)
                        for k in range(KT):
                            last = product3(nc, ps[:, c, 0:CH], w_hi[:, n0 % 2, k], w_lo[:, n0 % 2, k],
                                            xn_hi[:, k, tok], xn_lo[:, k, tok], k == 0, k == KT - 1)
                        last.then_inc(mm_ok, 1)

                def scores():
                    for b in range(3):
                        if b:
                            pe.wait_ge(tp_ev, b)
                        for j in range(3):
                            t = 3 * b + j
                            last = nc.tensor.transpose(ps_t[:, j, :], ikw[:, t * P:(t + 1) * P], K["ident"][:])
                        last.then_inc(tp, 1)
                    pe.wait_ge(dup, 16 * 6)
                    g = 0
                    for t in TILES:
                        L, _ = score_dims(t)
                        if t == NTP:
                            pe.wait_ge(kcol, 32)
                            pe.wait_ge(im_ok, NI)
                        for h in range(NI):
                            if g >= 2:
                                pe.wait_ge(rel_ok, g - 1)
                            half = slice(64 * (h % 2), 64 * (h % 2) + 64)
                            for at in range(0, L, 512):
                                w = min(512, L - at)
                                o = ps_s[:, g % 2, at:at + w]
                                if t < NTP:
                                    last = nc.tensor.matmul(o, iq[half, h // 2, t * P:(t + 1) * P],
                                                            ikd[half, at:at + w], start=True, stop=True)
                                else:
                                    for j in range(4):
                                        last = nc.tensor.matmul(o, iqm[:, h, j, :], KTi[:, j, at:at + w],
                                                                start=j == 0, stop=j == 3)
                            last.then_inc(sc_ok, 1)
                            g += 1
                run(pe, nc.tensor.Fori, lambda i, n0: None, unit, scores)

            @block.vector
            def _(dve):
                for b in range(3):
                    dve.wait_ge(tp, b + 1)
                    nc.vector.tensor_copy(tok_ik[:, 3 * b:3 * b + 3, :], ps_t[:, 0:3, 0:DH + NI]).then_inc(tp_ev, 1)
                dve.wait_ge(dup, 16 * 6)
                for h in range(NI):
                    nc.vector.tensor_tensor(iqm[:, h], K["pair_mask"][:], iqd[:, h:h + 1, :].to_broadcast([P, 4, P]),
                                            ALU.mult).then_inc(im_ok, 1)
                dve.wait_ge(tp_ev, 3)
                g = 0
                for t in TILES:
                    L, off = score_dims(t)
                    S = DM[:, off:off + L]
                    for h in range(NI):
                        dve.wait_ge(rel_ok, g + 1)
                        w = tok_ik[:, t, DH + h:DH + h + 1]
                        if h == 0:
                            nc.vector.tensor_scalar(S, rel[:, g % 2, 0:L], w, None, ALU.mult).then_inc(acc_ok, 1)
                        else:
                            dve.wait_ge(acc_ok, g)
                            nc.vector.scalar_tensor_tensor(S, rel[:, g % 2, 0:L], w, S, ALU.mult, ALU.add)\
                                .then_inc(acc_ok, 1)
                        g += 1
                n = 0
                dve.wait_ge(acc_ok, g)
                for t in TILES:
                    L, off = score_dims(t)
                    S = DM[:, off:off + L]
                    full, rest = divmod(TOPK_S if t == NTP else TOPK, 8)
                    if t < NTP:
                        nc.vector.memset(DM[0:CHUNK, off + L - CHUNK:off + L], BLOCKED).then_inc(ch, 1)
                        n += 1
                    dve.wait_ge(ch, n)
                    for _ in range(full):
                        dve.wait_ge(ch, n)
                        nc.vector.max(top8[:], S).then_inc(ch, 1)
                        dve.wait_ge(ch, n + 1)
                        nc.vector.match_replace(S, top8[:], S, TAKEN).then_inc(ch, 1)
                        n += 2
                    if rest:
                        dve.wait_ge(ch, n)
                        nc.vector.max(top8[:], S).then_inc(ch, 1)
                        dve.wait_ge(ch, n + 1)
                        nc.vector.memset(top8[:, rest:8], TAKEN).then_inc(ch, 1)
                        dve.wait_ge(ch, n + 2)
                        nc.vector.match_replace(S, top8[:], S, TAKEN).then_inc(ch, 1)
                        n += 3
                    dve.wait_ge(ch, n)
                    nc.vector.tensor_scalar(S, S, TAKEN * 0.999, BIG, ALU.is_gt, ALU.mult).then_inc(ch, 1)
                    dist = K["dist_s"][:] if t == NTP else K["dist_p"][:, SEQ - L:SEQ]
                    dve.wait_ge(ch, n + 1)
                    nc.vector.tensor_tensor(S, S, dist, ALU.add).then_inc(ch, 1)
                    n += 2
                for t in range(FIRST_SEL):
                    L, off = score_dims(t)
                    nc.vector.tensor_copy(DM[:, off:off + L], K["dist_p"][:, SEQ - L:SEQ]).then_inc(ch, 1)
                    n += 1
                    dve.wait_ge(ch, n)
                    nc.vector.memset(DM[0:CHUNK, off + L - CHUNK:off + L], BIG).then_inc(ch, 1)
                    n += 1


def prepare_mix(nc, ctx, M, K, io, out, kvT, E, scratch):
    sem = lambda n: ctx.enter_context(nc.semaphore("e_" + n))
    with ExitStack() as mem, M.scope():
        mvT = M.low("mvT", [P, HM, N_TOK])
        nrow = M.low("n_rows", [DEC_BATCH * HM, DH])
        ri, rf = M.low("row_i", [HM, N_TOK]), M.low("row_f", [HM, N_TOK])
        t1, t2 = M.low("row_t1", [HM, N_TOK]), M.low("row_t2", [HM, N_TOK])
        b_, m_ = M.low("row_b", [HM, N_TOK]), M.low("row_m", [HM, N_TOK])
        keep = M.low("row_keep", [HM, N_TOK])
        G4 = M.low("gate_rows", [P, N_TOK])
        bi, bf = M.low("bias_i", [HM, 1]), M.low("bias_f", [HM, 1])
        m0 = M.low("m0", [HM, DEC_BATCH])
        NCK = NTP + DEC_BATCH
        mp, ml, ul = M.low("m_prev", [HM, NCK]), M.low("m_last", [HM, NCK]), M.low("u_last", [HM, NCK])
        dec = M.low("decay", [HM, NCK])
        ps = psum(nc, mem, "e_ps", [P, 4, 512])
        ps_n = psum(nc, mem, "e_ps_n", [P, 64])
        ps_d = psum(nc, mem, "e_ps_d", [P, HM, NCK])
        ld, ldv, ldc, ldg, ldr = (sem(n) for n in ("ld", "ldv", "ldc", "ldg", "ldr"))
        dup, o_out = sem("dup"), sem("o_out")
        tp, ev, row, ra, ones_ok, ra_q = sem("tp"), sem("ev"), sem("row"), sem("ra"), sem("ones"), sem("raq")
        g_ok, n_tp, d_ok = sem("g_ok"), sem("n_tp"), sem("d_ok")
        sc_v = scratch.ap()
        vaug, ktm, kvtok, CT, Gt = E["vaug"], E["ktm"], E["kvtok"], E["CT"], E["Gt"]

        BATCHES = [("kv", b) for b in range(3)] + [("v", t) for t in range(NT)] + \
                  [("mk", t) for t in range(NT)] + [("C", h) for h in range(HM)] + [("G", b) for b in range(3)]
        KV_DONE = 3

        with nc.Block() as block:
            @block.sync
            def _(sp):
                for h, (dst, rows) in enumerate(((ri, slice(0, HM)), (rf, slice(HM, 2 * HM)))):
                    sp.dma_start(dst[:], sc_v[N_PLAIN + N_SIG, rows, :]).then_inc(ldg, 16)
                bg = io["b_mlstm_gates"][0].rearrange("(g h a) -> g h a", g=2, a=1)
                sp.dma_start(bi[:], bg[0]).then_inc(ldg, 16)
                sp.dma_start(bf[:], bg[1]).then_inc(ldg, 16)
                sp.dma_start(keep[:], io["keep"]).then_inc(ldg, 16)
                sp.dma_start(m0[:], io["state_mlstm_m"][0].rearrange("b h -> h b"),
                             allow_slow_non_contiguous=True).then_inc(ldg, 16)
                sp.dma_start(E["head_sel"][:], io["head_sel"].rearrange("h k p -> k h p")).then_inc(ldg, 16)
                sp.dma_start(mvT[:], sc_v[4:8].rearrange("k p n -> p k n")).then_inc(ldv, 16)
                sp.dma_start(E["mqk"][:], sc_v[0:4].rearrange("k p n -> p k n")).then_inc(ldv, 16)
                for h in range(HM):
                    sp.dma_start(E["Cn"][:, h], io["state_mlstm_C"][0, :, h].rearrange("b v d -> v b d"))\
                        .then_inc(ldc, 16)
                sp.dma_start(nrow[:], io["state_mlstm_n"][0].rearrange("b h d -> (b h) d")).then_inc(ldc, 16)
                for n in ("causal_p", "causal_s", "batch_mask", "pair_mask"):
                    sp.dma_start(E[n][:], io[n]).then_inc(ld, 16)
                sp.wait_ge(ldv, 32)
                for half in range(2):
                    rows = slice(64 * half, 64 * half + 64)
                    for par in range(2):
                        src = slice(64 * par, 64 * par + 64)
                        sp.dma_start(E["mqd"][rows, par::2, :], E["mqk"][src, 0:2, SEQ:N_TOK]).then_inc(dup, 16)
                sp.wait_ge(ev, KV_DONE)
                for n, cols in (("k", slice(0, DH)), ("v", slice(DH, 2 * DH))):
                    sp.dma_start(out[f"new_{n}_prompt"][0, 0].rearrange("(t p) d -> p t d", p=P),
                                 kvtok[:, 0:NTP, cols]).then_inc(o_out, 16)
                    sp.dma_start(out[f"new_{n}_sample"][0].rearrange("b q d -> (b q) d"),
                                 kvtok[:, NTP, cols]).then_inc(o_out, 16)
                sp.wait_ge(ra, 4)
                sp.dma_start(out["new_m_prompt"][0, 0].rearrange("(h a) -> h a", a=1),
                             ml[:, NTP - 1:NTP]).then_inc(o_out, 16)
                sp.dma_start(out["new_m_sample"][0].rearrange("b h -> h b"), ml[:, NTP:NCK],
                             allow_slow_non_contiguous=True).then_inc(o_out, 16)
                sp.wait_ge(o_out, 96)
                sp.wait_ge(ld, 16 * 4)
                sp.wait_ge(dup, 16 * 4)
                sp.wait_ge(ldc, 16 * 5)

            @block.gpsimd
            def _(pool):
                nc.gpsimd.memset(G4[:], 0.0).then_inc(ones_ok, 1)
                nc.gpsimd.memset(vaug[:, :, :, DV:DV + 1], 1.0).then_inc(ones_ok, 1)
                nc.gpsimd.memset(mp[:, 0:1], 0.0).then_inc(ones_ok, 1)
                pool.wait_ge(ones_ok, 3)

            @block.vector
            def _(dve):
                cnt = [0]

                def step(ins):
                    cnt[0] += 1
                    ins.then_inc(row, 1)
                    dve.wait_ge(row, cnt[0])
                v = nc.vector
                smp = lambda t: t[:, SEQ:N_TOK].rearrange("h (b q) -> h b q", q=DEC_SEQ)
                prm = lambda t: t[:, 0:SEQ].rearrange("h (c q) -> h c q", q=P)
                dve.wait_ge(ldg, 16 * 7)
                step(v.tensor_scalar(ri[:], ri[:], bi[:], None, ALU.add))
                step(v.tensor_scalar(rf[:], rf[:], bf[:], None, ALU.add))
                step(v.scalar_tensor_tensor(t1[:], rf[:], -1.0, rf[:], ALU.mult, ALU.max))
                v.tensor_scalar(rf[:], rf[:], 0.0, None, ALU.min).then_inc(ra_q, 1)
                dve.wait_ge(ra_q, 1)
                dve.wait_ge(ra, 2)
                step(v.tensor_tensor(rf[:], rf[:], t2[:], ALU.subtract))
                step(v.tensor_tensor_scan(b_[:], keep[:], rf[:], 0.0, ALU.mult, ALU.add))
                step(v.tensor_copy(t2[:], ri[:]))
                step(v.tensor_tensor(dec[:, 0:DEC_BATCH], smp(rf)[:, :, 0], m0[:], ALU.add))
                step(v.tensor_tensor(smp(t2)[:, :, 0], dec[:, 0:DEC_BATCH], smp(ri)[:, :, 0], ALU.max))
                step(v.memset(smp(rf)[:, :, 0], -BIG))
                step(v.tensor_tensor_scan(m_[:], rf[:], t2[:], 0.0, ALU.add, ALU.max))
                step(v.tensor_copy(ml[:, 0:NTP], prm(m_)[:, :, P - 1]))
                step(v.tensor_copy(ml[:, NTP:NCK], smp(m_)[:, :, DEC_SEQ - 1]))
                dve.wait_ge(ones_ok, 3)
                step(v.tensor_copy(mp[:, 1:NTP], ml[:, 0:NTP - 1]))
                step(v.tensor_copy(mp[:, NTP:NCK], m0[:]))
                step(v.tensor_tensor(E["V"][:], ri[:], b_[:], ALU.subtract))
                step(v.tensor_tensor(E["U"][:], b_[:], m_[:], ALU.subtract))
                step(v.tensor_tensor(prm(t1), prm(E["U"]), mp[:, 0:NTP, None].to_broadcast([HM, NTP, P]), ALU.add))
                step(v.tensor_tensor(smp(t1), smp(E["U"]), mp[:, NTP:NCK, None].to_broadcast([HM, DEC_BATCH, DEC_SEQ]), ALU.add))
                step(v.tensor_copy(ul[:, 0:NTP], prm(E["U"])[:, :, P - 1]))
                step(v.tensor_copy(ul[:, NTP:NCK], smp(E["U"])[:, :, DEC_SEQ - 1]))
                step(v.tensor_tensor(prm(t2), prm(E["V"]), ul[:, 0:NTP, None].to_broadcast([HM, NTP, P]), ALU.add))
                step(v.tensor_tensor(smp(t2), smp(E["V"]), ul[:, NTP:NCK, None].to_broadcast([HM, DEC_BATCH, DEC_SEQ]), ALU.add))
                v.tensor_copy(G4[0:HM, :], E["V"][:]).then_inc(ra_q, 1)
                dve.wait_ge(ra_q, 2)
                dve.wait_ge(ra, 6)
                gw = G4[32:32 + HM, :]
                step(v.tensor_copy(dec[:, 0:NTP], prm(gw)[:, :, P - 1]))
                step(v.tensor_copy(dec[:, NTP:NCK], smp(gw)[:, :, DEC_SEQ - 1]))
                v.tensor_copy(t1[:, 0:1], dec[:, 0:1]).then_inc(g_ok, 1)
                dve.wait_ge(d_ok, 1)
                v.tensor_copy(E["decB"][:], ps_d[:]).then_inc(d_ok, 1)
                dve.wait_ge(d_ok, 2)
                for h in range(HM):
                    half = slice(64 * (h % 2), 64 * (h % 2) + 64)
                    step(v.tensor_copy(E["decP"][half, h // 2, :], E["decB"][half, h, 0:NTP]))

            @block.scalar
            def _(act):
                act.wait_ge(ra_q, 1)
                nc.scalar.activation(t2[:], t1[:], ACT.Exp, scale=-1.0).then_inc(ra, 1)
                act.wait_ge(ra, 1)
                nc.scalar.activation(t2[:], t2[:], ACT.Ln, bias=1.0).then_inc(ra, 1)

                def evict(n):
                    kind, x = BATCHES[n]
                    act.wait_ge(tp, n + 1)
                    src = ps[:, n % 4, :]
                    if kind == "kv":
                        dst, src = kvtok[:, 3 * x:3 * x + 3, :], src[:, 0:3 * P].rearrange("p (j n) -> p j n", j=3)
                    elif kind == "v":
                        dst, src = vaug[:, x, :, 0:DV], src.rearrange("p (h v) -> p h v", h=HM)
                    elif kind == "mk":
                        dst, src = ktm[:, x, :], src[:, 0:HM * DH]
                    elif kind == "C":
                        dst, src = CT[:, x, :, 0:DV], src.rearrange("p (j v) -> p j v", j=4)
                    else:
                        for j in range(3):
                            s3 = src[:, j * P:(j + 1) * P].rearrange("p (q n) -> p q n", q=4)[:, :, 0:HM]
                            last = nc.scalar.activation(Gt[:, 3 * x + j], s3, ACT.Copy)
                        last.then_inc(ev, 1)
                        return
                    nc.scalar.activation(dst, src, ACT.Copy).then_inc(ev, 1)

                for n in range(3):
                    evict(n)
                act.wait_ge(ra_q, 2)
                act.wait_ge(ones_ok, 3)
                nc.scalar.activation(ul[:, 0:1], ul[:, 0:1], ACT.Copy).then_inc(ra, 1)
                nc.scalar.activation(G4[32:32 + HM, :], t1[:], ACT.Exp).then_inc(ra, 1)
                nc.scalar.activation(G4[64:64 + HM, :], m_[:], ACT.Exp, scale=-1.0).then_inc(ra, 1)
                nc.scalar.activation(G4[96:96 + HM, :], t2[:], ACT.Exp).then_inc(ra, 1)
                for n in range(3, len(BATCHES)):
                    evict(n)
                act.wait_ge(n_tp, 1)
                nsrc = ps_n[0:DH, 0:DEC_BATCH * HM].rearrange("d (j r h) -> d h j r", r=2, h=HM)
                for par in range(2):
                    last = nc.scalar.activation(CT[64 * par:64 * par + 64, :, :, DV], nsrc[:, :, :, par], ACT.Copy)
                last.then_inc(n_tp, 1)

            @block.tensor
            def _(pe):
                for n, (kind, x) in enumerate(BATCHES):
                    if n >= 4:
                        pe.wait_ge(ev, n - 3)
                    o = lambda j, w=P: ps[:, n % 4, j * w:(j + 1) * w]
                    tok = lambda t: slice(t * P, (t + 1) * P)
                    if kind == "kv":
                        for j in range(3):
                            last = nc.tensor.transpose(o(j), kvT[:, tok(3 * x + j)], K["ident"][:])
                    elif kind == "v":
                        pe.wait_ge(ldv, 32)
                        for h in range(HM):
                            last = nc.tensor.transpose(o(h), mvT[:, h, tok(x)], K["ident"][:])
                    elif kind == "mk":
                        for h in range(2):
                            last = nc.tensor.transpose(o(h), E["mqk"][:, 2 + h, tok(x)], K["ident"][:])
                    elif kind == "C":
                        pe.wait_ge(ldc, 16 * 5)
                        for j in range(4):
                            last = nc.tensor.transpose(o(j), E["Cn"][:, x, 2 * j:2 * j + 2, :]
                                                       .rearrange("p b d -> p (b d)"), K["ident"][:])
                    else:
                        pe.wait_ge(ra, 6)
                        for j in range(3):
                            last = nc.tensor.transpose(o(j), G4[:, tok(3 * x + j)], K["ident"][:])
                    last.then_inc(tp, 1)
                NR = DEC_BATCH * HM
                nc.tensor.transpose(ps_n[0:DH, 0:NR], nrow[:], K["ident"][0:NR, 0:NR]).then_inc(n_tp, 1)
                pe.wait_ge(g_ok, 1)
                for h in range(HM):
                    last = nc.tensor.matmul(ps_d[:, h, :], E["head_sel"][:, h, :], dec[:], start=True, stop=True)
                last.then_inc(d_ok, 1)


def mlstm(nc, ctx, M, K, io, out, kvT, E, num):
    sem = lambda n: ctx.enter_context(nc.semaphore("m_" + n))
    with ExitStack() as mem, M.scope():
        St = M.low("state", [P, 2, 2, DV + 1])
        lg = M.low("m_lg", [P, 2, HM * P])
        W = lg
        SW = M.low("m_sw", [P, 2, HM * P])
        kw = M.low("m_kw", [P, 2, HM, DH])
        ti = M.low("m_ti", [P, 2, HM, DV + 1])
        gws = M.low("m_gws", [P, NT, HM])
        qm = M.low("m_qm", [P, HM, 4, P])
        n1 = M.low("m_n1", [1, HM, DEC_BATCH, DH])
        kwb = M.low("m_kwb", [P, HM, DEC_BATCH, DH])
        kraw = kwb
        Cd, nd = E["Cn"], n1
        Cp = M.low("m_cp", [P, HM, DH])
        ps_d = psum(nc, mem, "m_ps_d", [P, 512])
        ps_s = psum(nc, mem, "m_ps_s", [P, 512])
        ps_i = [psum(nc, mem, f"m_ps_i{x}", [P, 512]) for x in range(2)]
        ps_n = [psum(nc, mem, f"m_ps_n{x}", [P, 512]) for x in range(2)]
        ps_u = psum(nc, mem, "m_ps_u", [P, 512])
        ps_x = psum(nc, mem, "m_ps_x", [P, 512])
        (d_ok, lg_ok, w_ok, s_ok, sw_ok, i_ok, n_ok, ti_ok, num_ok, kw_ok, u_ok, st_ok, init, q_ok, kb_ok, c_ok,
         n1_ok, cd_ok, cs_ok, o_out, fp, fe, nr_ok) = (sem(n) for n in (
             "d_ok", "lg_ok", "w_ok", "s_ok", "sw_ok", "i_ok", "n_ok", "ti_ok", "num_ok", "kw_ok", "u_ok", "st_ok",
             "init", "q_ok", "kb_ok", "c_ok", "n1_ok", "cd_ok", "cs_ok", "o_out", "fp", "fe", "nr_ok"))
        ldk, lda, ldn, kt_tp, kt_ev, half_ok = (sem(n) for n in ("ldk", "lda", "ldn", "kt_tp", "kt_ev", "half_ok"))
        mqk, vaug, ktm, Gt, CT = E["mqk"], E["vaug"], E["ktm"], E["Gt"], E["CT"]
        pair = lambda b: b[:, 0:2 * (DV + 1)].rearrange("p (h v) -> p h v", h=2)

        with nc.Block() as block:
            @block.sync
            def _(sp):
                sp.dma_start(n1[:], io["state_mlstm_n"][0:1].rearrange("a b h d -> a h b d")).then_inc(ldn, 16)
                for b in range(DEC_BATCH):
                    sp.dma_start(kraw[:, :, b, :], io["cache_attn_k"][0, b].rearrange("(k p) d -> p k d", p=P))\
                        .then_inc(ldk, 16)
                for b in range(DEC_BATCH):
                    sp.dma_start(E["vn"][:, b, :], E["kvtok"][b * DEC_SEQ:(b + 1) * DEC_SEQ, NTP, DH:2 * DH])\
                        .then_inc(lda, 16)
                for half in range(2):
                    rows = slice(64 * half, 64 * half + 64)
                    sp.dma_start(E["kd"][rows, :], kvT[0:DH, :]).then_inc(lda, 16)
                    for par in range(2):
                        src = slice(64 * par, 64 * par + 64)
                        sp.dma_start(E["aqd"][rows, par::2, :], E["aq"][src, :, SEQ:N_TOK]).then_inc(lda, 16)
                    new = kvT[0:DH, SEQ:N_TOK].rearrange("d (j r q) -> d j r q", r=2, q=DEC_SEQ)
                    sp.dma_start(E["KTa"][rows, :, PAST:LS], new[:, :, half, :]).then_inc(lda, 16)
                sp.wait_ge(lda, 16 * (DEC_BATCH + 8))
                sp.wait_ge(fe, 1)
                sp.dma_start(out["new_C_prompt"][0, 0].rearrange("h v d -> v h d"), Cp[:]).then_inc(o_out, 16)
                for h in range(HM):
                    half = slice(64 * (h % 2), 64 * (h % 2) + 64)
                    sp.dma_start(out["new_n_prompt"][0, 0, h].rearrange("(d a) -> d a", a=1),
                                 St[half, NTP % 2, h // 2, DV:DV + 1]).then_inc(o_out, 16)
                for h in range(HM):
                    sp.wait_ge(cs_ok, h + 1)
                    sp.dma_start(out["new_C_sample"][0, :, h].rearrange("b v d -> v b d"), Cd[:, h]).then_inc(o_out, 16)
                sp.wait_ge(nr_ok, 1)
                sp.dma_start(out["new_n_sample"][0:1].rearrange("a b h d -> a h b d"), nd[:]).then_inc(o_out, 16)
                sp.wait_ge(o_out, 16 * (2 + 2 * HM))

            @block.gpsimd
            def _(pool):
                nc.gpsimd.memset(St[:, 0], 0.0).then_inc(init, 1)
                dB = E["decB"][:, :, NTP:]
                nc.gpsimd.tensor_tensor(Cd[:], E["Cn"][:], dB[:, :, :, None].to_broadcast([P, HM, DEC_BATCH, DH]),
                                        ALU.mult).then_inc(cd_ok, 1)
                pool.wait_ge(ldn, 16)
                nc.gpsimd.tensor_tensor(nd[:], n1[:], dB[0:1, :, :, None].to_broadcast([1, HM, DEC_BATCH, DH]),
                                        ALU.mult).then_inc(cd_ok, 1)
                for h in range(HM):
                    nc.gpsimd.tensor_tensor(qm[:, h], E["pair_mask"][:], E["mqd"][:, h:h + 1, :]
                                            .to_broadcast([P, 4, P]), ALU.mult).then_inc(q_ok, 1)

            @block.scalar
            def _(act):
                act.wait_ge(init, 2)
                for t in range(NT):
                    act.wait_ge(lg_ok, t + 1)
                    nc.scalar.activation(W[:, t % 2], lg[:, t % 2], ACT.Exp).then_inc(w_ok, 1)
                    if t >= 2:
                        act.wait_ge(num_ok, 2 * (t - 1))
                    for y in range(2):
                        act.wait_ge(n_ok, 2 * t + y + 1)
                        for x in range(2):
                            h = 2 * x + y
                            nc.scalar.activation(ti[:, t % 2, h], pair(ps_n[y])[:, x], ACT.Copy,
                                                 scale=gws[:, t, h:h + 1]).then_inc(ti_ok, 1)
                    if t < 4:
                        act.wait_ge(kt_tp, t + 1)
                        nc.scalar.activation(E["KTa"][:, t, 0:PAST], ps_x[:], ACT.Copy).then_inc(kt_ev, 1)
                act.wait_ge(fp, 1)
                nc.scalar.activation(Cp[:], ps_x[:, 0:HM * DH].rearrange("p (h d) -> p h d", h=HM), ACT.Copy)\
                    .then_inc(fe, 1)

            @block.vector
            def _(dve):
                nc.vector.tensor_scalar(gws[:], Gt[:, :, 1, :], QK_SCALE, None, ALU.mult).then_inc(init, 1)
                for t in range(NT):
                    mask = E["causal_s" if t == NTP else "causal_p"][:, None, :].to_broadcast([P, HM, P])
                    if t >= 2:
                        dve.wait_ge(u_ok, t - 1)
                    nc.vector.tensor_tensor(kw[:, t % 2], ktm[:, t, :].rearrange("p (h d) -> p h d", h=HM),
                                            Gt[:, t, 3, :, None].to_broadcast([P, HM, DH]), ALU.mult).then_inc(kw_ok, 1)
                    dve.wait_ge(d_ok, t + 1)
                    if t >= 2:
                        dve.wait_ge(sw_ok, t - 1)
                    nc.vector.tensor_tensor(lg[:, t % 2].rearrange("p (h t) -> p h t", h=HM),
                                            ps_d[:, :].rearrange("p (h t) -> p h t", h=HM), mask, ALU.add)\
                        .then_inc(lg_ok, 1)
                    if t < NTP:
                        dve.wait_ge(u_ok, t + 1)
                        if t == 0:
                            dve.wait_ge(init, 2)
                        for x in range(2):
                            if t:
                                dve.wait_ge(st_ok, 2 * t)
                            nc.vector.scalar_tensor_tensor(St[:, (t + 1) % 2, x], St[:, t % 2, x],
                                                           E["decP"][:, x, t:t + 1], pair(ps_u)[:, x],
                                                           ALU.mult, ALU.add).then_inc(st_ok, 1)
                    dve.wait_ge(w_ok, t + 1)
                    dve.wait_ge(s_ok, t + 1)
                    if t >= 2:
                        dve.wait_ge(i_ok, 2 * (t - 1))
                    nc.vector.scalar_tensor_tensor(SW[:, t % 2], ps_s[:], QK_SCALE, W[:, t % 2], ALU.mult, ALU.mult)\
                        .then_inc(sw_ok, 1)
                    for x in range(2):
                        dve.wait_ge(i_ok, 2 * t + x + 1)
                        dve.wait_ge(ti_ok, 4 * t + 4)
                        nc.vector.tensor_tensor(num[:, t, 2 * x:2 * x + 2, :], ti[:, t % 2, 2 * x:2 * x + 2, :],
                                                pair(ps_i[x]), ALU.add).then_inc(num_ok, 1)
                dve.wait_ge(kw_ok, NT)
                dve.wait_ge(kt_tp, 4)
                for h in range(HM):
                    nc.vector.tensor_tensor(kwb[:, h], kw[:, NTP % 2, h:h + 1, :].to_broadcast([P, DEC_BATCH, DH]),
                                            E["batch_mask"][:, :, None].to_broadcast([P, DEC_BATCH, DH]),
                                            ALU.mult).then_inc(kb_ok, 1)
                dve.wait_ge(cd_ok, 2)
                for h in range(HM):
                    dve.wait_ge(c_ok, h + 1)
                    nc.vector.tensor_tensor(Cd[:, h], Cd[:, h], ps_d[:].rearrange("p (b d) -> p b d", b=DEC_BATCH),
                                            ALU.add).then_inc(cs_ok, 1)
                    dve.wait_ge(n1_ok, h + 1)
                    nc.vector.tensor_tensor(nd[:, h], nd[:, h], ps_s[0:1].rearrange("p (b d) -> p b d", b=DEC_BATCH),
                                            ALU.add).then_inc(cs_ok if h < 0 else fe if h < 0 else kb_ok, 1)
                dve.wait_ge(kb_ok, 2 * HM)
                nc.vector.tensor_copy(gws[0:1, 0, 0:1], gws[0:1, 0, 1:2]).then_inc(nr_ok, 1)

            @block.tensor
            def _(pe):
                for t in range(NT):
                    tok = slice(t * P, (t + 1) * P)
                    if t:
                        pe.wait_ge(lg_ok, t)
                    for h in range(HM):
                        o = ps_d[:, h * P:(h + 1) * P]
                        nc.tensor.matmul(o, E["head_sel"][:, h, :], E["U"][:, tok], start=True, stop=False)
                        last = nc.tensor.matmul(o, E["V"][:, tok], E["head_sel"][:, h, :], start=False, stop=True)
                    last.then_inc(d_ok, 1)
                    if t:
                        pe.wait_ge(sw_ok, t)
                    for h in (0, 2, 1, 3):
                        if h == 1:
                            pe.wait_ge(half_ok, t + 1)
                        half = slice(64 * (h % 2), 64 * (h % 2) + 64)
                        last = nc.tensor.matmul(ps_s[:, h * P:(h + 1) * P], mqk[half, 2 + h // 2, tok],
                                                mqk[half, h // 2, tok], start=True, stop=True)
                        if h == 2:
                            last.then_inc(half_ok, 1)
                    last.then_inc(s_ok, 1)
                    pe.wait_ge(kw_ok, t + 1)
                    if t < NTP:
                        if t:
                            pe.wait_ge(st_ok, 2 * t)
                        for h in range(HM):
                            half = slice(64 * (h % 2), 64 * (h % 2) + 64)
                            last = nc.tensor.matmul(pair(ps_u)[half, h // 2], kw[:, t % 2, h, :], vaug[:, t, h, :],
                                                    start=True, stop=True)
                        last.then_inc(u_ok, 1)
                    if t == 0:
                        pe.wait_ge(init, 2)
                    if t == NTP:
                        pe.wait_ge(q_ok, HM)
                    for y in range(2):
                        if t:
                            pe.wait_ge(ti_ok, 4 * (t - 1) + 2 * y + 2)
                        for x in range(2):
                            h = 2 * x + y
                            half = slice(64 * y, 64 * y + 64)
                            o = pair(ps_n[y])[:, x]
                            if t < NTP:
                                last = nc.tensor.matmul(o, mqk[half, h // 2, tok], St[half, t % 2, h // 2, :],
                                                        start=True, stop=True)
                            else:
                                for j in range(4):
                                    last = nc.tensor.matmul(o, qm[:, h, j, :], CT[:, h, j, :],
                                                            start=j == 0, stop=j == 3)
                        last.then_inc(n_ok, 1)
                    pe.wait_ge(sw_ok, t + 1)
                    for x in range(2):
                        if t:
                            pe.wait_ge(num_ok, 2 * (t - 1) + x + 1)
                        for y in range(2):
                            h = 2 * x + y
                            last = nc.tensor.matmul(pair(ps_i[x])[:, y], SW[:, t % 2, h * P:(h + 1) * P],
                                                    vaug[:, t, h, :], start=True, stop=True)
                        last.then_inc(i_ok, 1)
                    if t < 4:
                        pe.wait_ge(ldk, 16 * DEC_BATCH)
                        if t:
                            pe.wait_ge(kt_ev, t)
                        for k in range(4):
                            last = nc.tensor.transpose(ps_x[:, k * P:(k + 1) * P],
                                                       kraw[:, k, 2 * t:2 * t + 2, :].rearrange("p b d -> p (b d)"),
                                                       K["ident"][:])
                        last.then_inc(kt_tp, 1)
                pe.wait_ge(kt_ev, 4)
                pe.wait_ge(st_ok, 2 * NTP)
                for h in (0, 2, 1, 3):
                    if h == 1:
                        pe.wait_ge(half_ok, NT + 1)
                    half = slice(64 * (h % 2), 64 * (h % 2) + 64)
                    last = nc.tensor.transpose(ps_x[:, h * DH:(h + 1) * DH], St[half, NTP % 2, h // 2, 0:DV],
                                               K["ident"][half, half])
                    if h == 2:
                        last.then_inc(half_ok, 1)
                last.then_inc(fp, 1)
                for h in range(HM):
                    pe.wait_ge(kb_ok, HM)
                    if h:
                        pe.wait_ge(cs_ok, h)
                    f = kwb[:, h].rearrange("p b d -> p (b d)")
                    nc.tensor.matmul(ps_d[:], vaug[:, NTP, h, 0:DV], f, start=True, stop=True).then_inc(c_ok, 1)
                    if h:
                        pe.wait_ge(kb_ok, HM + h)
                    nc.tensor.matmul(ps_s[0:1, :], K["ones"][:, 0:1], f, start=True, stop=True).then_inc(n1_ok, 1)


def mlstm_output(nc, ctx, M, K, E, num, h_hi, h_lo, scratch):
    sem = lambda n: ctx.enter_context(nc.semaphore("h_" + n))
    with ExitStack() as mem, M.scope():
        og = M.low("h_og", [P, HM, N_TOK])
        sq = M.low("h_sq", [P, DV])
        ss, den, inv, rs, sc = (M.low("h_" + n, [P, NT, HM]) for n in ("ss", "den", "inv", "rs", "sc"))
        hn = M.low("h_n", [P, 2, HM, DV])
        full = M.low("h_full", [P, 2, HM, P])
        ps = psum(nc, mem, "h_ps", [P, 2, 512])
        ld, ss_ok, row, rs_in, rs_ok, n_ok, tp, f_ok, hi, lo = (
            sem(n) for n in ("ld", "ss_ok", "row", "rs_in", "rs_ok", "n_ok", "tp", "f_ok", "hi", "lo"))
        with nc.Block() as block:
            @block.sync
            def _(sp):
                sp.dma_start(og[:], scratch.ap()[N_PLAIN:N_PLAIN + HM].rearrange("k p n -> p k n")).then_inc(ld, 16)

            @block.scalar
            def _(act):
                n = 0
                for t in range(NT):
                    for h in range(HM):
                        if n:
                            act.wait_ge(ss_ok, n)
                        nc.scalar.activation(sq[:], num[:, t, h, 0:DV], ACT.Square,
                                             accum_out=ss[:, t, h:h + 1]).then_inc(ss_ok, 1)
                        n += 1
                act.wait_ge(rs_in, 1)
                nc.scalar.activation(rs[:], rs[:], ACT.Sqrt).then_inc(rs_ok, 1)
                for t in range(NT):
                    act.wait_ge(f_ok, HM * (t + 1))
                    nc.scalar.activation(h_hi[:, :, t * P:(t + 1) * P], full[:, t % 2], ACT.Copy).then_inc(hi, 1)

            @block.vector
            def _(dve):
                v, cnt = nc.vector, [0]

                def step(ins):
                    cnt[0] += 1
                    ins.then_inc(row, 1)
                    dve.wait_ge(row, cnt[0])
                nq = num[:, :, :, DV]
                step(v.scalar_tensor_tensor(den[:], nq, -1.0, nq, ALU.mult, ALU.max))
                step(v.tensor_tensor(den[:], den[:], E["Gt"][:, :, 2, :], ALU.max))
                step(v.reciprocal(inv[:], den[:]))
                dve.wait_ge(ss_ok, NT * HM)
                step(v.tensor_tensor(rs[:], ss[:], inv[:], ALU.mult))
                step(v.tensor_tensor(rs[:], rs[:], inv[:], ALU.mult))
                step(v.tensor_scalar(rs[:], rs[:], 1.0 / DV, EPS, ALU.mult, ALU.add))
                v.reciprocal(rs[:], rs[:]).then_inc(rs_in, 1)
                dve.wait_ge(rs_ok, 1)
                step(v.tensor_tensor(sc[:], inv[:], rs[:], ALU.mult))

                def scaled(t):
                    if t >= 2:
                        dve.wait_ge(tp, t - 1)
                    v.tensor_tensor(hn[:, t % 2], num[:, t, :, 0:DV], sc[:, t, :, None].to_broadcast([P, HM, DV]),
                                    ALU.mult).then_inc(n_ok, 1)
                scaled(0)
                dve.wait_ge(ld, 16)
                for t in range(NT):
                    if t + 1 < NT:
                        scaled(t + 1)
                    dve.wait_ge(tp, t + 1)
                    if t >= 2:
                        dve.wait_ge(lo, t - 1)
                    for h in range(HM):
                        v.scalar_tensor_tensor(full[:, t % 2, h], ps[:, t % 2, h * P:(h + 1) * P],
                                               K["g_mlstm"][:, h:h + 1], og[:, h, t * P:(t + 1) * P],
                                               ALU.mult, ALU.mult).then_inc(f_ok, 1)

            @block.gpsimd
            def _(pool):
                for t in range(NT):
                    pool.wait_ge(hi, t + 1)
                    tok = slice(t * P, (t + 1) * P)
                    nc.gpsimd.tensor_tensor(h_lo[:, :, tok], full[:, t % 2], h_hi[:, :, tok].bitcast(F32),
                                            ALU.subtract).then_inc(lo, 1)

            @block.tensor
            def _(pe):
                for t in range(NT):
                    pe.wait_ge(n_ok, t + 1)
                    if t >= 2:
                        pe.wait_ge(f_ok, HM * (t - 1))
                    for h in range(HM):
                        last = nc.tensor.transpose(ps[:, t % 2, h * P:(h + 1) * P], hn[:, t % 2, h, :], K["ident"][:])
                    last.then_inc(tp, 1)


def attention(nc, ctx, M, K, io, E, DM, o_hi, o_lo):
    sem = lambda n: ctx.enter_context(nc.semaphore("t_" + n))
    SLOPE = [2.0 ** (-8.0 * (h + 1) / HA) / QK_SCALE for h in range(HA)]
    ITEMS = [(t, h) for t in range(NT) for h in range(HA)]
    NKS = PAST // P
    with ExitStack() as mem, M.scope():
        vc = M.low("vc", [P, NKS, DEC_BATCH, DH])
        lg = M.low("t_lg", [P, 2, SEQ])
        pr = M.low("t_p", [P, 2, SEQ])
        PT = M.low("t_pt", [P, 2, NTP, P])
        PTs = M.low("t_pts", [P, NKS + 1, HA, P])
        qm = M.low("t_qm", [P, 2, 4, P])
        mx, nm = M.low("t_mx", [P, 2]), M.low("t_nm", [P, 2])
        sm, inv = M.low("t_sm", [P, 2, HA]), M.low("t_inv", [P, 2, HA])
        osb = M.low("t_osb", [P, 2, HA * DH])
        ofs = M.low("t_ofs", [P, 4, P])
        ps_l = psum(nc, mem, "t_ps_l", [P, 2, 1024])
        ps_t = psum(nc, mem, "t_ps_t", [P, 2, 512])
        ps_o = psum(nc, mem, "t_ps_o", [P, 512])
        ps_x = psum(nc, mem, "t_ps_x", [P, 512])
        (ld, qk, lg_ok, mx_ok, nm_ok, p_ok, pn_ok, tr, tr_ev, pv, inv_ok, on_ok, ot, hi, lo, q_ok, pvs, of_ok) = (
            sem(n) for n in ("ld", "qk", "lg_ok", "mx_ok", "nm_ok", "p_ok", "pn_ok", "tr", "tr_ev", "pv", "inv_ok",
                             "on_ok", "ot", "hi", "lo", "q_ok", "pvs", "of_ok"))

        def keys(t):
            return LS if t == NTP else P * (t + 1)

        BATCH = []
        for t, _ in ITEMS:
            n = -(-keys(t) // P)
            BATCH.append([(k, min(k + 4, n)) for k in range(0, n, 4)])
        UPTO = np.cumsum([0] + [len(b) for b in BATCH]).tolist()

        def run(eng, ahead, item, tile=None):
            ahead(0)
            for i, (t, h) in enumerate(ITEMS):
                if i + 1 < len(ITEMS):
                    ahead(i + 1)
                item(i)
                if h == 0 and t and tile:
                    tile(t - 1)

        with nc.Block() as block:
            @block.sync
            def _(sp):
                for b in range(DEC_BATCH):
                    sp.dma_start(vc[:, :, b, :], io["cache_attn_v"][0, b].rearrange("(k p) d -> p k d", p=P))\
                        .then_inc(ld, 16)

            @block.gpsimd
            def _(pool):
                for h in range(HA):
                    if h >= 2:
                        pool.wait_ge(qk, NTP * HA + h - 1)
                    nc.gpsimd.tensor_tensor(qm[:, h % 2], E["pair_mask"][:], E["aqd"][:, h:h + 1, :]
                                            .to_broadcast([P, 4, P]), ALU.mult).then_inc(q_ok, 1)
                pool.wait_ge(hi, NTP + 1)
                tok = slice(SEQ, N_TOK)
                nc.gpsimd.tensor_tensor(o_lo[:, :, tok], ofs[:], o_hi[:, :, tok].bitcast(F32), ALU.subtract)\
                    .then_inc(lo, 1)

            @block.tensor
            def _(pe):
                def product(i):
                    t, h = ITEMS[i]
                    if i >= 2:
                        pe.wait_ge(lg_ok, i - 1)
                    half = slice(64 * (h % 2), 64 * (h % 2) + 64)
                    if t == NTP:
                        pe.wait_ge(q_ok, h + 1)
                    L = keys(t)
                    for at in range(0, L, 512):
                        w = min(512, L - at)
                        o = ps_l[:, i % 2, at:at + w]
                        if t < NTP:
                            last = nc.tensor.matmul(o, E["aq"][half, h // 2, t * P:(t + 1) * P],
                                                    E["kd"][half, at:at + w], start=True, stop=True)
                        else:
                            for j in range(4):
                                last = nc.tensor.matmul(o, qm[:, h % 2, j, :], E["KTa"][:, j, at:at + w],
                                                        start=j == 0, stop=j == 3)
                    last.then_inc(qk, 1)

                def item(i):
                    t, h = ITEMS[i]
                    pe.wait_ge(p_ok, i + 1)
                    if t == NTP:
                        pe.wait_ge(pn_ok, h + 1)
                    for g, (k0, k1) in enumerate(BATCH[i], UPTO[i]):
                        if g >= 2:
                            pe.wait_ge(tr_ev, g - 1)
                        for k in range(k0, k1):
                            w = min(P, keys(t) - k * P)
                            last = nc.tensor.transpose(ps_t[0:w, g % 2, (k - k0) * P:(k - k0 + 1) * P],
                                                       pr[:, i % 2, k * P:k * P + w], K["ident"][:])
                        last.then_inc(tr, 1)
                    if t == NTP:
                        return
                    pe.wait_ge(tr_ev, UPTO[i + 1])
                    if h == 0 and t:
                        pe.wait_ge(on_ok, t)
                    for k in range(t + 1):
                        last = nc.tensor.matmul(ps_o[:, h * DH:(h + 1) * DH], PT[:, i % 2, k, :],
                                                E["kvtok"][:, k, DH:2 * DH], start=k == 0, stop=k == t)
                    last.then_inc(pv, 1)

                def tile(t):
                    pe.wait_ge(on_ok, t + 1)
                    if t:
                        pe.wait_ge(lo, t)
                    for j in range(4):
                        last = nc.tensor.transpose(ps_x[:, j * P:(j + 1) * P], osb[:, t % 2, j * P:(j + 1) * P],
                                                   K["ident"][:])
                    last.then_inc(ot, 1)
                run(pe, product, item, tile)
                pe.wait_ge(tr_ev, UPTO[-1])
                pe.wait_ge(ld, 16 * DEC_BATCH)
                pe.wait_ge(lg_ok, len(ITEMS))
                for b in range(DEC_BATCH):
                    q = slice(b * DEC_SEQ, (b + 1) * DEC_SEQ)
                    o = ps_l[0:DH, 0, b * P:(b + 1) * P]
                    for k in range(NKS):
                        nc.tensor.matmul(o, vc[:, k, b, :], PTs[:, k, :, q], start=k == 0, stop=False)
                    last = nc.tensor.matmul(o, E["vn"][:, b, :], PTs[0:DEC_SEQ, NKS, :, q], start=False, stop=True)
                last.then_inc(pvs, 1)

            @block.vector
            def _(dve):
                v = nc.vector

                def logits(i):
                    t, h = ITEMS[i]
                    L = keys(t)
                    dve.wait_ge(qk, i + 1)
                    if i >= 2:
                        dve.wait_ge(p_ok, i - 1)
                    v.scalar_tensor_tensor(lg[:, i % 2, 0:L], DM[:, SCORE_OFF[t]:SCORE_OFF[t] + L], -SLOPE[h],
                                           ps_l[:, i % 2, 0:L], ALU.mult, ALU.add).then_inc(lg_ok, 1)
                    dve.wait_ge(lg_ok, i + 1)
                    v.reduce_max(mx[:, i % 2:i % 2 + 1], lg[:, i % 2, 0:L], AX_X).then_inc(mx_ok, 1)
                    dve.wait_ge(mx_ok, i + 1)
                    v.tensor_scalar(nm[:, i % 2:i % 2 + 1], mx[:, i % 2:i % 2 + 1], -QK_SCALE, None,
                                    ALU.mult).then_inc(nm_ok, 1)

                def item(i):
                    t, h = ITEMS[i]
                    if t == NTP:
                        dve.wait_ge(p_ok, i + 1)
                        v.reciprocal(inv[:, t % 2, h:h + 1], sm[:, t % 2, h:h + 1]).then_inc(inv_ok, 1)
                        dve.wait_ge(inv_ok, NTP + h + 1)
                        v.tensor_scalar(pr[:, i % 2, 0:LS], pr[:, i % 2, 0:LS], inv[:, t % 2, h:h + 1], None,
                                        ALU.mult).then_inc(pn_ok, 1)
                    elif h == HA - 1:
                        dve.wait_ge(p_ok, i + 1)
                        v.reciprocal(inv[:, t % 2], sm[:, t % 2]).then_inc(inv_ok, 1)
                        dve.wait_ge(inv_ok, t + 1)
                        dve.wait_ge(pv, i + 1)
                        if t >= 2:
                            dve.wait_ge(ot, t - 1)
                        v.tensor_tensor(osb[:, t % 2].rearrange("p (h d) -> p h d", h=HA),
                                        ps_o[:].rearrange("p (h d) -> p h d", h=HA),
                                        inv[:, t % 2, :, None].to_broadcast([P, HA, DH]), ALU.mult).then_inc(on_ok, 1)

                def tile(t):
                    dve.wait_ge(hi, t + 1)
                    tok = slice(t * P, (t + 1) * P)
                    v.tensor_tensor(o_lo[:, :, tok], ps_x[:].rearrange("p (j n) -> p j n", j=4),
                                    o_hi[:, :, tok].bitcast(F32), ALU.subtract).then_inc(lo, 1)
                run(dve, logits, item, tile)

            @block.scalar
            def _(act):
                def probs(i):
                    t, h = ITEMS[i]
                    L = keys(t)
                    act.wait_ge(nm_ok, i + 1)
                    if i >= 2:
                        act.wait_ge(tr, UPTO[i - 1])
                    if h == 0 and t >= 2:
                        act.wait_ge(inv_ok, t - 1)
                    nc.scalar.activation(pr[:, i % 2, 0:L], lg[:, i % 2, 0:L], ACT.Exp, bias=nm[:, i % 2:i % 2 + 1],
                                         scale=QK_SCALE, accum_out=sm[:, t % 2, h:h + 1]).then_inc(p_ok, 1)

                def item(i):
                    t, h = ITEMS[i]
                    if i >= 2 and t < NTP:
                        act.wait_ge(pv, i - 1)
                    for g, (k0, k1) in enumerate(BATCH[i], UPTO[i]):
                        act.wait_ge(tr, g + 1)
                        src = ps_t[:, g % 2, 0:(k1 - k0) * P].rearrange("p (k n) -> p k n", n=P)
                        if t < NTP:
                            dst = PT[:, i % 2, k0:k1, :]
                        elif k1 <= NKS:
                            dst = PTs[:, k0:k1, h, :]
                        else:
                            src, dst = src[0:DEC_SEQ], PTs[0:DEC_SEQ, k0:k1, h, :]
                        nc.scalar.activation(dst, src, ACT.Copy).then_inc(tr_ev, 1)

                def tile(t):
                    act.wait_ge(ot, t + 1)
                    nc.scalar.activation(o_hi[:, :, t * P:(t + 1) * P], ps_x[:].rearrange("p (j n) -> p j n", j=4),
                                         ACT.Copy).then_inc(hi, 1)
                run(act, probs, item, tile)
                act.wait_ge(pvs, 1)
                src = ps_l[0:DH, 0, :].rearrange("d (b j r q) -> d r j b q", b=DEC_BATCH, j=4, r=2)
                for r in range(2):
                    nc.scalar.activation(ofs[64 * r:64 * r + 64].rearrange("d j (b q) -> d j b q", b=DEC_BATCH),
                                         src[:, r], ACT.Copy).then_inc(of_ok, 1)
                act.wait_ge(of_ok, 2)
                nc.scalar.activation(o_hi[:, :, SEQ:N_TOK], ofs[:], ACT.Copy).then_inc(hi, 1)


def mix_out(nc, ctx, M, K, io, o, h, y, ya, yb, scratch):
    sem = lambda n: ctx.enter_context(nc.semaphore("b_" + n))
    (o_hi, o_lo), (h_hi, h_lo), (y_hi, y_lo) = o, h, y
    BODIES = KT // 2 - 1
    with ExitStack() as mem, M.scope():
        raw = M.low("b_raw", [P, 2, KT, P])
        w_hi = M.low("b_w_hi", [P, 2, KT, P], F32R)
        w_lo = M.low("b_w_lo", [P, 2, KT, P], F32R)
        sg = M.low("b_sg", [P, 2, 2, N_TOK])
        ps = psum(nc, mem, "b_ps", [P, NCH, 2, 512])
        w_in, g_in = [sem("w_in0"), sem("w_in1")], [sem("g_in0"), sem("g_in1")]
        hi_ok, lo_ok, mm_ok, ya_ok, yb_ok, y_ok, yh_ok, yl_ok = (
            sem(n) for n in ("hi_ok", "lo_ok", "mm_ok", "ya_ok", "yb_ok", "y_ok", "yh_ok", "yl_ok"))
        wa = io["w_branch_attn"][0].rearrange("(k p) n -> p k n", p=P)
        wb = io["w_branch_mlstm"][0].rearrange("(k p) n -> p k n", p=P)
        ga, gb = (scratch.ap()[N_PLAIN + HM + u * KT:N_PLAIN + HM + (u + 1) * KT].rearrange("k p n -> p k n")
                  for u in range(2))

        def run(loop, before, unit):
            before(0, 0)
            for n0 in range(2):
                before(0, n0 + 1)
                unit(0, n0)
            with loop(0, BODIES - 1) as i:
                for n0 in (2, 3):
                    before(i, n0 + 1)
                    unit(i, n0)
            before(0, KT - 1)
            unit(0, KT - 2)
            unit(0, KT - 1)

        with nc.Block() as block:
            @block.sync
            def _(sp):
                def load(i, n0):
                    cols, tile = bass.ds((i * 2 + n0) * P, P), bass.ds(i * 2 + n0, 1)
                    if n0 >= 2:
                        sp.wait_ge(lo_ok, i * 2 + (n0 - 1))
                    sp.dma_start(raw[:, n0 % 2, 0:4], wa[:, :, cols]).then_inc(w_in[n0 % 2], 16)
                    sp.dma_start(raw[:, n0 % 2, 4:8], wb[:, :, cols]).then_inc(w_in[n0 % 2], 16)
                    if n0 >= 2:
                        sp.wait_ge(yb_ok, i * (2 * NCH) + NCH * (n0 - 1))
                    sp.dma_start(sg[:, n0 % 2, 0:1], ga[:, tile, :]).then_inc(g_in[n0 % 2], 16)
                    sp.dma_start(sg[:, n0 % 2, 1:2], gb[:, tile, :]).then_inc(g_in[n0 % 2], 16)
                run(nc.sync.Fori, load, lambda i, n0: None)

            @block.scalar
            def _(act):
                def split_hi(i, n0):
                    act.wait_ge(w_in[n0 % 2], i * 32 + 32 * (n0 // 2 + 1))
                    if n0 >= 2:
                        act.wait_ge(mm_ok, i * (2 * NCH) + NCH * (n0 - 1))
                    nc.scalar.activation(w_hi[:, n0 % 2], raw[:, n0 % 2], ACT.Copy).then_inc(hi_ok, 1)

                def unit(i, n0):
                    for c in range(NCH):
                        q0 = NCH * n0 + c
                        act.wait_ge(y_ok, i * (2 * NCH) + (q0 + 1))
                        nc.scalar.activation(y_hi[:, bass.ds(i * 2 + n0, 1), c * CH:(c + 1) * CH],
                                             ya[:, q0 % 2:q0 % 2 + 1], ACT.Copy).then_inc(yh_ok, 1)
                run(nc.scalar.Fori, split_hi, unit)

            @block.gpsimd
            def _(pool):
                def split_lo(i, n0):
                    pool.wait_ge(hi_ok, i * 2 + (n0 + 1))
                    nc.gpsimd.tensor_tensor(w_lo[:, n0 % 2], raw[:, n0 % 2], w_hi[:, n0 % 2].bitcast(F32),
                                            ALU.subtract).then_inc(lo_ok, 1)

                def unit(i, n0):
                    for c in range(NCH):
                        q0 = NCH * n0 + c
                        pool.wait_ge(yh_ok, i * (2 * NCH) + (q0 + 1))
                        at = (slice(None), bass.ds(i * 2 + n0, 1), slice(c * CH, (c + 1) * CH))
                        nc.gpsimd.tensor_tensor(y_lo[at], ya[:, q0 % 2:q0 % 2 + 1], y_hi[at].bitcast(F32),
                                                ALU.subtract).then_inc(yl_ok, 1)
                run(nc.gpsimd.Fori, split_lo, unit)

            @block.vector
            def _(dve):
                def unit(i, n0):
                    dve.wait_ge(g_in[n0 % 2], i * 32 + 32 * (n0 // 2 + 1))
                    for c in range(NCH):
                        q0 = NCH * n0 + c
                        q = i * (2 * NCH) + q0
                        tok = slice(c * CH, (c + 1) * CH)
                        dve.wait_ge(mm_ok, q + 1)
                        if q0 >= 2:
                            dve.wait_ge(yl_ok, q - 1)
                        nc.vector.tensor_tensor(ya[:, q0 % 2], ps[:, c, 0, 0:CH], sg[:, n0 % 2, 0, tok],
                                                ALU.mult).then_inc(ya_ok, 1)
                        nc.vector.tensor_tensor(yb[:, q0 % 2], ps[:, c, 1, 0:CH], sg[:, n0 % 2, 1, tok],
                                                ALU.mult).then_inc(yb_ok, 1)
                        dve.wait_ge(ya_ok, q + 1)
                        dve.wait_ge(yb_ok, q + 1)
                        nc.vector.tensor_tensor(ya[:, q0 % 2], ya[:, q0 % 2], yb[:, q0 % 2], ALU.add).then_inc(y_ok, 1)
                run(nc.vector.Fori, lambda i, n0: None, unit)

            @block.tensor
            def _(pe):
                def unit(i, n0):
                    pe.wait_ge(lo_ok, i * 2 + (n0 + 1))
                    for c in range(NCH):
                        tok = slice(c * CH, (c + 1) * CH)
                        if n0:
                            pe.wait_ge(yb_ok, i * (2 * NCH) + (NCH * n0 + c - 2))
                        for u, (x_hi, x_lo) in enumerate(((o_hi, o_lo), (h_hi, h_lo))):
                            for k in range(4):
                                last = product3(nc, ps[:, c, u, 0:CH], w_hi[:, n0 % 2, 4 * u + k],
                                                w_lo[:, n0 % 2, 4 * u + k], x_hi[:, k, tok], x_lo[:, k, tok],
                                                k == 0, k == 3)
                        last.then_inc(mm_ok, 1)
                run(nc.tensor.Fori, lambda i, n0: None, unit)


def output_projection(nc, ctx, M, K, io, y, xT, x_dram):
    sem = lambda n: ctx.enter_context(nc.semaphore("o_" + n))
    y_hi, y_lo = y
    with ExitStack() as mem, M.scope():
        raw = M.low("o_raw", [P, 2, KT, P])
        w_hi = M.low("o_w_hi", [P, 2, KT, P], F32R)
        w_lo = M.low("o_w_lo", [P, 2, KT, P], F32R)
        ps = psum(nc, mem, "o_ps", [P, NCH, 512])
        w_in, x_in = [sem("w_in0"), sem("w_in1")], sem("x_in")
        hi_ok, lo_ok, mm_ok, x_ok = (sem(n) for n in ("hi_ok", "lo_ok", "mm_ok", "x_ok"))
        w_v = io["w_out"][0].rearrange("(k p) n -> p k n", p=P)

        def run(loop, before, unit):
            before(0, 0)
            for n0 in range(2):
                before(0, n0 + 1)
                unit(0, n0)
            with loop(0, KT // 2 - 2) as i:
                for n0 in (2, 3):
                    before(i, n0 + 1)
                    unit(i, n0)
            before(0, KT - 1)
            unit(0, KT - 2)
            unit(0, KT - 1)

        with nc.Block() as block:
            @block.sync
            def _(sp):
                def load(i, n0):
                    if n0 >= 2:
                        sp.wait_ge(lo_ok, i * 2 + (n0 - 1))
                    sp.dma_start(raw[:, n0 % 2], w_v[:, :, bass.ds((i * 2 + n0) * P, P)]).then_inc(w_in[n0 % 2], 16)
                    if n0 == 0:
                        sp.dma_start(xT[:], x_dram.ap()).then_inc(x_in, 16)
                run(nc.sync.Fori, load, lambda i, n0: None)

            @block.scalar
            def _(act):
                def split_hi(i, n0):
                    act.wait_ge(w_in[n0 % 2], i * 16 + 16 * (n0 // 2 + 1))
                    if n0 >= 2:
                        act.wait_ge(mm_ok, i * (2 * NCH) + NCH * (n0 - 1))
                    nc.scalar.activation(w_hi[:, n0 % 2], raw[:, n0 % 2], ACT.Copy).then_inc(hi_ok, 1)
                run(nc.scalar.Fori, split_hi, lambda i, n0: None)

            @block.gpsimd
            def _(pool):
                def split_lo(i, n0):
                    pool.wait_ge(hi_ok, i * 2 + (n0 + 1))
                    nc.gpsimd.tensor_tensor(w_lo[:, n0 % 2], raw[:, n0 % 2], w_hi[:, n0 % 2].bitcast(F32),
                                            ALU.subtract).then_inc(lo_ok, 1)
                run(nc.gpsimd.Fori, split_lo, lambda i, n0: None)

            @block.vector
            def _(dve):
                dve.wait_ge(x_in, 16)

                def unit(i, n0):
                    for c in range(NCH):
                        dve.wait_ge(mm_ok, i * (2 * NCH) + (NCH * n0 + c + 1))
                        x = xT[:, bass.ds(i * 2 + n0, 1), c * CH:(c + 1) * CH]
                        nc.vector.tensor_tensor(x, ps[:, c:c + 1, 0:CH], x, ALU.add).then_inc(x_ok, 1)
                run(nc.vector.Fori, lambda i, n0: None, unit)

            @block.tensor
            def _(pe):
                def unit(i, n0):
                    pe.wait_ge(lo_ok, i * 2 + (n0 + 1))
                    for c in range(NCH):
                        tok = slice(c * CH, (c + 1) * CH)
                        if n0:
                            pe.wait_ge(x_ok, i * (2 * NCH) + (NCH * n0 + c - 2))
                        for k in range(KT):
                            last = product3(nc, ps[:, c, 0:CH], w_hi[:, n0 % 2, k], w_lo[:, n0 % 2, k],
                                            y_hi[:, k, tok], y_lo[:, k, tok], k == 0, k == KT - 1)
                        last.then_inc(mm_ok, 1)
                run(nc.tensor.Fori, lambda i, n0: None, unit)


def final_norm(nc, ctx, M, K, io, out, xT):
    sem = lambda n: ctx.enter_context(nc.semaphore("z_" + n))
    with ExitStack() as mem, M.scope():
        gain = M.low("z_gain", [P, D_MODEL])
        sq = M.low("z_sq", [P, D_MODEL])
        res = M.low("z_res", [P, 2, D_MODEL])
        ps = psum(nc, mem, "z_ps", [P, 4, D_MODEL])
        ld, tp, ss, s1, s2, s3, r_ok = (sem(n) for n in ("ld", "tp", "ss", "s1", "s2", "s3", "r_ok"))
        st = [sem("st0"), sem("st1")]
        with nc.Block() as block:
            @block.sync
            def _(sp):
                sp.dma_start(gain[:], io["norm_final"].rearrange("(a n) -> a n", a=1).to_broadcast([P, D_MODEL]))\
                    .then_inc(ld, 16)
                for t in range(NT):
                    sp.wait_ge(r_ok, t + 1)
                    dst = out["y_prompt"][0, t * P:(t + 1) * P, :] if t < NTP else \
                        out["y_sample"].rearrange("b q d -> (b q) d")
                    sp.dma_start(dst, res[:, t % 2]).then_inc(st[t % 2], 16)
                sp.wait_ge(st[0], 16 * ((NT + 1) // 2))
                sp.wait_ge(st[1], 16 * (NT // 2))

            @block.tensor
            def _(pe):
                for t in range(NT):
                    if t >= 4:
                        pe.wait_ge(r_ok, t - 3)
                    for k in range(KT):
                        last = nc.tensor.transpose(ps[:, t % 4, k * P:(k + 1) * P], xT[:, k, t * P:(t + 1) * P],
                                                   K["ident"][:])
                    last.then_inc(tp, 1)

            @block.scalar
            def _(act):
                def squares(t):
                    act.wait_ge(tp, t + 1)
                    if t:
                        act.wait_ge(ss, t)
                    nc.scalar.activation(sq[:], ps[:, t % 4], ACT.Square, accum_out=K["ssq"][:, t:t + 1])\
                        .then_inc(ss, 1)
                squares(0)
                for t in range(NT):
                    if t + 1 < NT:
                        squares(t + 1)
                    act.wait_ge(s2, t + 1)
                    nc.scalar.activation(K["st3"][:, t:t + 1], K["st2"][:, t:t + 1], ACT.Sqrt).then_inc(s3, 1)

            @block.vector
            def _(dve):
                def scale(t):
                    c = slice(t, t + 1)
                    dve.wait_ge(ss, t + 1)
                    nc.vector.tensor_scalar(K["st1"][:, c], K["ssq"][:, c], 1.0 / D_MODEL, EPS, ALU.mult, ALU.add)\
                        .then_inc(s1, 1)
                    dve.wait_ge(s1, t + 1)
                    nc.vector.reciprocal(K["st2"][:, c], K["st1"][:, c]).then_inc(s2, 1)
                scale(0)
                dve.wait_ge(ld, 16)
                for t in range(NT):
                    if t + 1 < NT:
                        scale(t + 1)
                    dve.wait_ge(s3, t + 1)
                    if t >= 2:
                        dve.wait_ge(st[t % 2], 16 * (t // 2))
                    nc.vector.scalar_tensor_tensor(res[:, t % 2], ps[:, t % 4], K["st3"][:, t:t + 1], gain[:],
                                                   ALU.mult, ALU.mult).then_inc(r_ok, 1)


def trunk(nc, io, out):
    ctx = ExitStack()
    M = Sbuf(nc)
    x_dram = nc.dram_tensor("x_dram", [P, KT, N_TOK], F32, kind="Internal")
    scratch = nc.dram_tensor("p_dram", [N_PLAIN + N_SIG + 1, P, N_TOK], F32, kind="Internal")
    with ctx:
        K = {n: M.low(n, [P, NT]) for n in ("ssq", "st1", "st2", "st3")}
        K["ident"] = M.low("ident_sb", [P, P])
        K["ones"] = M.low("ones_sb", [P, P])
        K["gains"] = M.low("gains", [P, 3 * KT + HM])
        for n, k in enumerate(("ffn1", "mix", "ffn2")):
            K["g_" + k] = K["gains"][:, n * KT:(n + 1) * KT]
        K["g_mlstm"] = K["gains"][:, 3 * KT:3 * KT + HM]
        def phase(f, *args):
            with ExitStack() as own:
                used = []
                f(nc, Scope(own, used), M, K, *args)
                used.sort()
                with nc.Block() as block:
                    @block.gpsimd
                    def _(pool):
                        at = 0
                        while at < len(used):
                            end = at + 1
                            while end < len(used) and used[end] == used[end - 1] + 1:
                                end += 1
                            pool.sem_clear(range(used[at], used[end - 1] + 1))
                            at = end

        high_end = M.high_end
        xn_hi = M.high("xn_hi", [P, KT, N_TOK], F32R)
        xn_lo = M.high("xn_lo", [P, KT, N_TOK], F32R)
        low_end = M.low_end
        xT = M.low("xT", [P, KT, N_TOK])
        phase(load_and_norm, io, xT, None, None, None)
        phase(apply_norm, xT, K["g_ffn1"], xn_hi, xn_lo, "n1")
        phase(ffn, io["w_ffn1_up"], io["w_ffn1_down"], xT, xn_hi, xn_lo, "f1")
        phase(feature_stats, xT, "s2")
        phase(apply_norm, xT, K["g_mix"], xn_hi, xn_lo, "n2")
        KTi = M.high("KTi", [P, 4, LS])
        K["dist_p"] = M.high("dist_p_sb", [P, SEQ])
        K["dist_s"] = M.high("dist_s_sb", [P, LS])
        K["pair_mask"] = M.high("pair_mask_sb", [P, 4, P])
        phase(cache_index_keys, io, xT, x_dram, KTi)
        M.low_end = low_end
        aq_at = M.low_end
        aq = M.low("aq", [P, 4, N_TOK])
        kvT = M.low("kvT", [P, N_TOK])
        DM = M.low("DM", [P, SCORE_COLS])
        phase(project, io, out, xn_hi, xn_lo, aq, kvT, KTi, DM, scratch)
        M.high_end = high_end
        E = {"aq": aq}
        E["kvtok"] = M.low("kvtok", [P, NT, P])
        low_end = M.low_end
        for n, shape in dict(mqk=[P, 4, N_TOK], vaug=[P, NT, HM, DV + 1], ktm=[P, NT, HM * DH],
                             mqd=[P, HM, P], Cn=[P, HM, DEC_BATCH, DH], CT=[P, HM, 4, DV + 1],
                             U=[HM, N_TOK], V=[HM, N_TOK], head_sel=[HM, HM, P], causal_p=[P, P],
                             causal_s=[P, P], batch_mask=[P, DEC_BATCH],
                             decB=[P, HM, NTP + DEC_BATCH], decP=[P, 2, NTP]).items():
            E[n] = M.low(n + "_sb", shape)
        E["Gt"], E["pair_mask"] = M.high("Gt", [P, NT, 4, HM]), M.high("pair_mask_e", [P, 4, P])
        phase(prepare_mix, io, out, kvT, E, scratch)
        for n, shape in dict(KTa=[P, 4, LS], kd=[P, N_TOK], aqd=[P, HA, P],
                             vn=[DEC_SEQ, DEC_BATCH, DH]).items():
            E[n] = M.high(n, shape)
        att_end = M.high_end
        num = M.high("num", [P, NT, HM, DV + 1])
        phase(mlstm, io, out, kvT, E, num)
        M.low_end = low_end
        h = M.low("h_hi", [P, HM, N_TOK], F32R), M.low("h_lo", [P, HM, N_TOK], F32R)
        phase(mlstm_output, E, num, *h, scratch)
        M.high_end = att_end
        o = M.low("o_hi", [P, HM, N_TOK], F32R), M.low("o_lo", [P, HM, N_TOK], F32R)
        phase(attention, io, E, DM, *o)
        M.high_end = high_end
        y = M.high("y_hi", [P, KT, N_TOK], F32R), M.high("y_lo", [P, KT, N_TOK], F32R)
        ya, yb = M.low("b_ya", [P, 2, CH]), M.low("b_yb", [P, 2, CH])
        M.low_end = aq_at
        mid_end = M.high_end
        M.high_end = low_end
        phase(mix_out, io, o, h, y, ya, yb, scratch)
        M.high_end = mid_end
        xT = M.low("xT_2", [P, KT, N_TOK])
        phase(output_projection, io, y, xT, x_dram)
        M.high_end = high_end
        xn = M.high("xn2_hi", [P, KT, N_TOK], F32R), M.high("xn2_lo", [P, KT, N_TOK], F32R)
        phase(feature_stats, xT, "s3")
        phase(apply_norm, xT, K["g_ffn2"], *xn, "n3")
        phase(ffn, io["w_ffn2_up"], io["w_ffn2_down"], xT, *xn, "f2")
        phase(final_norm, io, out, xT)


_INS = ["x_prompt", "x_sample", "cache_attn_k", "cache_attn_v", "cache_idx_k", "state_mlstm_C", "state_mlstm_n",
        "state_mlstm_m", "norm_ffn1", "w_ffn1_up", "w_ffn1_down", "norm_mix", "w_in", "b_mlstm_gates",
        "norm_mlstm_heads", "w_branch_attn", "w_branch_mlstm", "w_out", "norm_ffn2", "w_ffn2_up", "w_ffn2_down",
        "norm_final"]
_OUTS = {
    "y_prompt": (1, SEQ, D_MODEL), "y_sample": (DEC_BATCH, DEC_SEQ, D_MODEL),
    "new_k_prompt": (1, 1, SEQ, DH), "new_v_prompt": (1, 1, SEQ, DH), "new_idxk_prompt": (1, 1, SEQ, DH),
    "new_C_prompt": (1, 1, HM, DV, DH), "new_n_prompt": (1, 1, HM, DH), "new_m_prompt": (1, 1, HM),
    "new_k_sample": (1, DEC_BATCH, DEC_SEQ, DH), "new_v_sample": (1, DEC_BATCH, DEC_SEQ, DH),
    "new_idxk_sample": (1, DEC_BATCH, DEC_SEQ, DH), "new_C_sample": (1, DEC_BATCH, HM, DV, DH),
    "new_n_sample": (1, DEC_BATCH, HM, DH), "new_m_sample": (1, DEC_BATCH, HM),
}


def kernel(**inputs):
    import concourse.bacc as bacc
    from concourse.bass_utils import run_bass_kernel_spmd

    nc = bacc.Bacc("TRN2", target_bir_lowering=False, num_devices=1)
    arrays, io, out = {}, {}, {}
    given = {n: np.ascontiguousarray(inputs[n]) for n in _INS}
    for name, a in {**given, **constants()}.items():
        arrays["in_" + name] = a
        io[name] = nc.dram_tensor("in_" + name, a.shape, F32, kind="ExternalInput").ap()
    for name, shape in _OUTS.items():
        out[name] = nc.dram_tensor("out_" + name, shape, F32, kind="ExternalOutput").ap()
    trunk(nc, io, out)
    r = run_bass_kernel_spmd(nc, [arrays], core_ids=[0])
    return tuple(r.results[0]["out_" + n] for n in _OUTS)
```

```python
from contextlib import ExitStack, contextmanager

import numpy as np

import concourse.bass as bass
from concourse import mybir

F32 = mybir.dt.float32
F32R = mybir.dt.float32r
ALU = mybir.AluOpType
ACT = mybir.ActivationFunctionType
AX_X = mybir.AxisListType.X

P = 128
D_MODEL = 1024
KT = D_MODEL // P
SEQ = 1024
DEC_BATCH = 8
DEC_SEQ = 16
PAST = 512
N_TOK = SEQ + DEC_BATCH * DEC_SEQ
NT = N_TOK // P
NTP = SEQ // P
CH = 384
NCH = N_TOK // CH
CHUNK = 64
HA = 8
DH = 64
NI = 4
TOPK = 256
TOPK_S = (PAST + DEC_SEQ) // 4
HM = 4
DV = 128
D_FF = 2816
FT = D_FF // P
FG = 2
NG = FT // FG
EPS = 1e-6
IDX_SCALE = (NI * DH) ** -0.5
QK_SCALE = DH ** -0.5
LS = PAST + DEC_SEQ
SLOPE = [2.0 ** (-8.0 * (h + 1) / HA) / QK_SCALE for h in range(HA)]
BIG = 1e30
TAKEN = -3.4e38
BLOCKED = -3.0e38
FIRST_SEL = TOPK // P
SCORE_OFF = {}
_at = 0
for _b in range(NTP):
    SCORE_OFF[_b] = _at
    _at += P * (_b + 1)
SCORE_OFF[NTP] = _at
SCORE_COLS = _at + LS

C_AQ, C_AK, C_IQ, C_IK, C_MQ, C_MI, C_MO = 0, 512, 640, 896, 964, 1988, 1996
N_PLAIN = 8
N_SIG = 20


def constants():
    c = {}
    c["ident"] = np.eye(P, dtype=np.float32)
    p, x = np.arange(P)[:, None], np.arange(SEQ)[None, :]
    c["dist_p"] = np.abs(p + SEQ - P - x).astype(np.float32)
    c["dist_s"] = np.abs(PAST + p % DEC_SEQ - np.arange(LS)[None, :]).astype(np.float32)
    c["slope"] = -np.repeat(np.array(SLOPE, np.float32), DEC_SEQ)[:, None]
    b_of = np.arange(P) // DEC_SEQ
    par = (np.arange(P) // 64)[:, None, None]
    c["pair_mask"] = (b_of[None, None, :] == 2 * np.arange(4)[None, :, None] + par).astype(np.float32)
    c["batch_mask"] = (b_of[:, None] == np.arange(DEC_BATCH)[None, :]).astype(np.float32)
    s, t = np.arange(P)[:, None], np.arange(P)[None, :]
    c["causal_p"] = np.where(s <= t, 0, -BIG).astype(np.float32)
    c["causal_s"] = np.where((s <= t) & (s // DEC_SEQ == t // DEC_SEQ), 0, -BIG).astype(np.float32)
    sel = np.zeros((HM, HM, P), np.float32)
    for h in range(HM):
        sel[h, h] = 1
    c["head_sel"] = sel
    keep = np.ones((HM, N_TOK), np.float32)
    keep[:, 0:SEQ:P] = 0
    keep[:, SEQ::DEC_SEQ] = 0
    c["keep"] = keep
    return c


class Scope:

    def __init__(self, stack, numbers):
        self.stack, self.numbers = stack, numbers

    def enter_context(self, guard):
        got = self.stack.enter_context(guard)
        self.numbers.append(got.num)
        return got


class Sbuf:

    def __init__(self, nc):
        self.nc, self.low_end, self.high_end = nc, (nc.sbuf_base + 63) // 64 * 64, nc.sbuf_usable_end // 64 * 64

    def low(self, name, shape, dt=F32):
        at = self.low_end
        self.low_end += (int(np.prod(shape[1:])) * 4 + 63) // 64 * 64
        assert self.low_end <= self.high_end, (name, self.low_end, self.high_end)
        return self.nc.alloc_sbuf_tensor_at(name, shape, dt, offset=at)

    def high(self, name, shape, dt=F32):
        self.high_end -= (int(np.prod(shape[1:])) * 4 + 63) // 64 * 64
        assert self.low_end <= self.high_end, (name, self.low_end, self.high_end)
        return self.nc.alloc_sbuf_tensor_at(name, shape, dt, offset=self.high_end)

    def at(self, name, shape, offset, dt=F32):
        return self.nc.alloc_sbuf_tensor_at(name, shape, dt, offset=offset)

    @contextmanager
    def scope(self):
        ends = self.low_end, self.high_end
        yield
        self.low_end, self.high_end = ends


def psum(nc, ctx, name, shape, dt=F32):
    return ctx.enter_context(nc.psum_tensor(name, shape, dt))


def load_residual(nc, ctx, M, K, io, xT):
    sem = lambda n: ctx.enter_context(nc.semaphore("a_" + n))
    NG_ROWS = 3 * KT + HM
    with ExitStack() as mem, M.scope():
        xt = M.low("x_tok", [P, NT, D_MODEL])
        grow = M.low("gain_rows", [P, P])
        pg = psum(nc, mem, "gain_tp", [P, P])
        pt = psum(nc, mem, "x_tp", [P, 6, 512])
        x_in = [sem(f"x_in{t}") for t in range(NT)]
        tp, tpg, ev_v, ev_s, c_in, ones_ok = (sem(n) for n in ("tp", "tpg", "ev_v", "ev_s", "c_in", "ones"))

        def half_tile(n):
            t, half = n // 2, n % 2
            return xT[:, 4 * half:4 * half + 4, t * P:(t + 1) * P], \
                pt[:, n % 6, :].rearrange("p (j t) -> p j t", j=4)

        with nc.Block() as block:
            @block.sync
            def _(sp):
                sp.dma_start(K["ident"][:], io["ident"]).then_inc(c_in, 16)
                for t in range(NT):
                    src = io["x_prompt"][0, t * P:(t + 1) * P, :] if t < NTP else \
                        io["x_sample"].rearrange("b q d -> (b q) d")
                    sp.dma_start(xt[:, t, :], src).then_inc(x_in[t], 16)
                for n, k in enumerate(("ffn1", "mix", "ffn2")):
                    sp.dma_start(grow[n * KT:(n + 1) * KT, :],
                                 io["norm_" + k][0].rearrange("(k p) -> k p", p=P)).then_inc(c_in, 16)
                sp.dma_start(grow[3 * KT:3 * KT + HM, :],
                             io["norm_mlstm_heads"][0].rearrange("(k p) -> k p", p=P)).then_inc(c_in, 16)

            @block.gpsimd
            def _(pool):
                nc.gpsimd.memset(K["ones"][:], 1.0).then_inc(ones_ok, 1)
                pool.wait_ge(ones_ok, 1)

            @block.tensor
            def _(pe):
                for n in range(2 * NT):
                    t, half = n // 2, n % 2
                    if n == 0:
                        pe.wait_ge(c_in, 16)
                    if half == 0:
                        pe.wait_ge(x_in[t], 16)
                    if n >= 6:
                        pe.wait_ge((ev_v, ev_s)[half], (n - 6) // 2 + 1)
                    for j in range(4):
                        last = nc.tensor.transpose(pt[:, n % 6, j * P:(j + 1) * P],
                                                   xt[:, t, (4 * half + j) * P:(4 * half + j + 1) * P],
                                                   K["ident"][:])
                    last.then_inc(tp, 1)
                pe.wait_ge(c_in, 80)
                nc.tensor.transpose(pg[:, 0:NG_ROWS], grow[0:NG_ROWS, :],
                                    K["ident"][0:NG_ROWS, 0:NG_ROWS]).then_inc(tpg, 1)

            @block.vector
            def _(dve):
                for n in range(0, 2 * NT, 2):
                    dst, src = half_tile(n)
                    dve.wait_ge(tp, n + 1)
                    nc.vector.tensor_copy(dst, src).then_inc(ev_v, 1)
                dve.wait_ge(tpg, 1)
                nc.vector.tensor_copy(K["gains"][:, 0:NG_ROWS], pg[:, 0:NG_ROWS]).then_inc(ev_v, 1)

            @block.scalar
            def _(act):
                for n in range(1, 2 * NT, 2):
                    dst, src = half_tile(n)
                    act.wait_ge(tp, n + 1)
                    nc.scalar.activation(dst, src, ACT.Copy).then_inc(ev_s, 1)


class Norm:
    ON_VECTOR = (2, 5)

    def __init__(self, nc, sem, K, xT, gain, xn_hi, xn_lo, sq, acc, rms, full, ps):
        self.nc, self.K, self.xT, self.gain, self.xn_hi, self.xn_lo = nc, K, xT, gain, xn_hi, xn_lo
        self.sq, self.acc, self.rms, self.full, self.ps = sq, acc, rms, full, ps
        self.slots = full.shape[1]
        (self.sq_ok, self.sum_ok, self.spread_ok, self.mean_ok, self.inv_ok, self.root_ok, self.full_ok,
         self.hi_ok, self.lo_v, self.lo_g) = (sem("n_" + n) for n in (
             "sq", "sum", "spread", "mean", "inv", "root", "full", "hi", "lo_v", "lo_g"))

    @staticmethod
    def tok(c):
        return slice(c * CH, (c + 1) * CH)

    def lo_before(self, eng, n):
        on_v = len(self.ON_VECTOR) * (n // KT) + sum(k < n % KT for k in self.ON_VECTOR)
        if on_v:
            eng.wait_ge(self.lo_v, on_v)
        if n - on_v:
            eng.wait_ge(self.lo_g, n - on_v)

    def squares(self, act, c):
        for k in range(KT):
            m = (KT - 1) * c + k - 1
            if k and m >= 2:
                act.wait_ge(self.sum_ok, m - 1)
            dst = self.sq[:, m % 2, :] if k else self.acc[:, self.tok(c)]
            self.nc.scalar.activation(dst, self.xT[:, k, self.tok(c)], ACT.Square).then_inc(self.sq_ok, 1)

    def sums(self, dve, c):
        a = self.acc[:, self.tok(c)]
        for k in range(1, KT):
            m = (KT - 1) * c + k - 1
            dve.wait_ge(self.sq_ok, KT * c + k + 1)
            if k > 1:
                dve.wait_ge(self.sum_ok, m)
            self.nc.vector.tensor_tensor(a, a, self.sq[:, m % 2, :], ALU.add).then_inc(self.sum_ok, 1)

    def spread(self, pe, c):
        pe.wait_ge(self.sum_ok, (KT - 1) * (c + 1))
        self.nc.tensor.matmul(self.ps[c], self.K["ones"][:], self.acc[:, self.tok(c)], start=True, stop=True)\
            .then_inc(self.spread_ok, 1)

    def inverse(self, dve, c):
        a = self.rms[:, self.tok(c)]
        dve.wait_ge(self.spread_ok, c + 1)
        self.nc.vector.tensor_scalar(a, self.ps[c], 1.0 / D_MODEL, EPS, ALU.mult, ALU.add).then_inc(self.mean_ok, 1)
        dve.wait_ge(self.mean_ok, c + 1)
        self.nc.vector.reciprocal(a, a).then_inc(self.inv_ok, 1)

    def root(self, act, c):
        a = self.rms[:, self.tok(c)]
        act.wait_ge(self.inv_ok, c + 1)
        self.nc.scalar.activation(a, a, ACT.Sqrt).then_inc(self.root_ok, 1)

    def apply(self, dve, c):
        dve.wait_ge(self.root_ok, c + 1)
        for k in range(KT):
            n = KT * c + k
            if n >= self.slots:
                self.lo_before(dve, n - self.slots + 1)
            self.nc.vector.scalar_tensor_tensor(self.full[:, n % self.slots, :], self.xT[:, k, self.tok(c)],
                                                self.gain[:, k:k + 1], self.rms[:, self.tok(c)],
                                                ALU.mult, ALU.mult).then_inc(self.full_ok, 1)
            if k - 1 in self.ON_VECTOR:
                self.lo(self.nc.vector, dve, c, k - 1, self.lo_v)

    def hi(self, act, c):
        for k in range(KT):
            n = KT * c + k
            act.wait_ge(self.full_ok, n + 1)
            self.nc.scalar.activation(self.xn_hi[:, k, self.tok(c)], self.full[:, n % self.slots, :], ACT.Copy)\
                .then_inc(self.hi_ok, 1)

    def lo(self, engine, eng, c, k, done):
        n = KT * c + k
        eng.wait_ge(self.hi_ok, n + 1)
        engine.tensor_tensor(self.xn_lo[:, k, self.tok(c)], self.full[:, n % self.slots, :],
                             self.xn_hi[:, k, self.tok(c)].bitcast(F32), ALU.subtract).then_inc(done, 1)

    def on_vector(self, dve):
        self.sums(dve, 0)
        self.sums(dve, 1)
        self.inverse(dve, 0)
        self.inverse(dve, 1)
        self.apply(dve, 0)
        self.sums(dve, 2)
        self.apply(dve, 1)
        self.inverse(dve, 2)
        self.apply(dve, 2)
        self.lo_before(dve, KT * NCH)

    def on_scalar(self, act):
        self.squares(act, 1)
        self.root(act, 0)
        self.root(act, 1)
        self.hi(act, 0)
        self.squares(act, 2)
        self.hi(act, 1)
        self.root(act, 2)
        self.hi(act, 2)

    def on_gpsimd(self, pool):
        for c in range(NCH):
            for k in range(KT):
                if k not in self.ON_VECTOR:
                    self.lo(self.nc.gpsimd, pool, c, k, self.lo_g)

    def before_chunk(self, pe, c):
        if c == 0:
            self.spread(pe, 0)
            self.spread(pe, 1)
        elif c == 1:
            self.spread(pe, 2)
        self.lo_before(pe, KT * (c + 1))


def product3(nc, out, w_hi, w_lo, x_hi, x_lo, first, final):
    nc.tensor.matmul(out, w_hi, x_lo, start=first, stop=False)
    nc.tensor.matmul(out, w_lo, x_hi, start=False, stop=False)
    return nc.tensor.matmul(out, w_hi, x_hi, start=False, stop=final)


def ffn(nc, ctx, M, K, w_up, w_down, gain, xT, xn_hi, xn_lo, tag):
    sem = lambda n: ctx.enter_context(nc.semaphore(tag + n))
    PAIRS = [("up", 0), ("up", 1), ("up", 2), ("up", 3), ("down", 0), ("up", 4), ("up", 5), ("down", 1)]
    LAST = ("down", 2)
    PER = {"up": 4, "down": 2}
    BODIES = (NG - 1) // 2
    ND = KT * NCH
    with ExitStack() as mem, M.scope():
        raw = M.low(tag + "raw", [P, 2, 2, KT, P])
        w_hi = M.low(tag + "w_hi", [P, 2, 2, KT, P], F32R)
        w_lo = M.low(tag + "w_lo", [P, 2, 2, KT, P], F32R)
        h_at, h_group = M.low_end, FG * N_TOK * 4
        h_hi = M.low(tag + "h_hi", [P, 2, FG, N_TOK], F32R)
        h_lo = M.low(tag + "h_lo", [P, 2, FG, N_TOK], F32R)
        gate = M.low(tag + "gate", [P, 2, CH])
        hid = M.low(tag + "hid", [P, 2, CH])
        ps_up = psum(nc, mem, tag + "ps_up", [P, 3, 2, 512])
        ps_dn = psum(nc, mem, tag + "ps_dn", [P, 2, 512])
        w_in = [sem("w_in0"), sem("w_in1")]
        hi_ok, lo_ok = sem("hi_ok"), sem("lo_ok")
        up_ok, gate_ok, hid_ok = sem("up_ok"), sem("gate_ok"), sem("hid_ok")
        hhi_ok, hlo_ok = sem("hhi_ok"), sem("hlo_ok")
        dn_ok, dn_ev = sem("dn_ok"), sem("dn_ev")
        stat = M.at(tag + "stat", [P, 2, N_TOK], h_at + h_group)
        full = M.at(tag + "full", [P, 4, CH], h_at + 3 * h_group)
        norm = Norm(nc, sem, K, xT, gain, xn_hi, xn_lo, gate, stat[:, 0], stat[:, 1], full,
                    [ps_up[:, c, 0, 0:CH] for c in range(NCH)])

        up_v = w_up[0].rearrange("(k p) n -> p k n", p=P)
        dn_v = w_down[0].rearrange("(k p) n -> p k n", p=P)

        def wait_multiplied(eng, i, n0):
            kind, m = PAIRS[n0]
            if n0 == 1:
                eng.wait_ge(dn_ok, i * (ND * 2))
            if kind == "up":
                eng.wait_ge(up_ok, i * (NCH * 4) + NCH * (m + 1))
            else:
                eng.wait_ge(dn_ok, i * (ND * 2) + ND * (m + 1))

        def load(sp, i, n0, kind, m):
            if n0 >= 2:
                sp.wait_ge(lo_ok, i * 6 + (n0 - 1))
            m = i * PER[kind] + m
            if kind == "up":
                for u in range(2):
                    sp.dma_start(raw[:, n0 % 2, u], up_v[:, :, bass.ds(m * P + u * D_FF, P)])\
                        .then_inc(w_in[n0 % 2], 16)
            else:
                sp.dma_start(raw[:, n0 % 2].rearrange("p u k n -> p u (k n)"), dn_v[:, bass.ds(m * FG, FG), :])\
                    .then_inc(w_in[n0 % 2], 32)

        def slot(t, n0):
            return t[:, n0 % 2].rearrange("p u k n -> p (u k n)")

        def split_hi(act, i, n0):
            act.wait_ge(w_in[n0 % 2], i * 96 + 32 * (n0 // 2 + 1))
            if n0 >= 2:
                wait_multiplied(act, i, n0 - 2)
            nc.scalar.activation(slot(w_hi, n0), slot(raw, n0), ACT.Copy).then_inc(hi_ok, 1)

        def split_lo(pool, i, n0):
            pool.wait_ge(hi_ok, i * 6 + (n0 + 1))
            nc.gpsimd.tensor_tensor(slot(w_lo, n0), slot(raw, n0), slot(w_hi, n0).bitcast(F32),
                                    ALU.subtract).then_inc(lo_ok, 1)

        def run(loop, before, pair, first=lambda: None):
            before(0, 0)
            first()
            for n0 in range(2):
                before(0, n0 + 1)
                pair(0, n0, *PAIRS[n0])
            with loop(0, BODIES) as i:
                for n0 in range(2, 8):
                    before(i, n0 + 1)
                    pair(i, n0, *PAIRS[n0])
            pair(BODIES - 1, 8, *LAST)

        with nc.Block() as block:
            @block.sync
            def _(sp):
                load(sp, 0, 0, "up", 0)
                load(sp, 0, 1, "up", 1)
                with nc.sync.Fori(0, BODIES) as i:
                    for n0 in range(2, 8):
                        load(sp, i, n0, *PAIRS[n0])
                load(sp, BODIES - 1, 8, *LAST)

            @block.scalar
            def _(act):
                def pair(i, n0, kind, m):
                    if kind == "down":
                        return
                    for c in range(NCH):
                        q0 = NCH * m + c
                        q = i * (NCH * 4) + q0
                        act.wait_ge(up_ok, q + 1)
                        if q0 >= 2:
                            act.wait_ge(hid_ok, q - 1)
                        nc.scalar.activation(gate[:, q0 % 2], ps_up[:, c, 0, 0:CH], ACT.Silu).then_inc(gate_ok, 1)
                        act.wait_ge(hid_ok, q + 1)
                        nc.scalar.activation(h_hi[:, m // 2 % 2, m % 2, c * CH:(c + 1) * CH], hid[:, q0 % 2],
                                             ACT.Copy).then_inc(hhi_ok, 1)
                norm.squares(act, 0)
                run(nc.scalar.Fori, lambda i, n0: split_hi(act, i, n0), pair, lambda: norm.on_scalar(act))

            @block.gpsimd
            def _(pool):
                def pair(i, n0, kind, m):
                    if kind == "down":
                        return
                    for c in range(NCH):
                        q0 = NCH * m + c
                        pool.wait_ge(hhi_ok, i * (NCH * 4) + (q0 + 1))
                        out = slice(c * CH, (c + 1) * CH)
                        nc.gpsimd.tensor_tensor(h_lo[:, m // 2 % 2, m % 2, out], hid[:, q0 % 2],
                                                h_hi[:, m // 2 % 2, m % 2, out].bitcast(F32),
                                                ALU.subtract).then_inc(hlo_ok, 1)
                run(nc.gpsimd.Fori, lambda i, n0: split_lo(pool, i, n0), pair, lambda: norm.on_gpsimd(pool))

            @block.vector
            def _(dve):
                def pair(i, n0, kind, m):
                    if kind == "up":
                        for c in range(NCH):
                            q0 = NCH * m + c
                            q = i * (NCH * 4) + q0
                            dve.wait_ge(gate_ok, q + 1)
                            if q0 >= 2:
                                dve.wait_ge(hlo_ok, q - 1)
                            nc.vector.tensor_tensor(hid[:, q0 % 2], gate[:, q0 % 2], ps_up[:, c, 1, 0:CH],
                                                    ALU.mult).then_inc(hid_ok, 1)
                    else:
                        for r in range(ND):
                            k, c = r // NCH, r % NCH
                            dve.wait_ge(dn_ok, i * (ND * 2) + (ND * m + r + 1))
                            x = xT[:, k, c * CH:(c + 1) * CH]
                            nc.vector.scalar_tensor_tensor(x, ps_dn[:, r % 2, 0:CH], 0.5, x,
                                                           ALU.mult, ALU.add).then_inc(dn_ev, 1)
                            if r == ND - 1:
                                dve.wait_ge(dn_ev, i * (ND * 2) + ND * (m + 1))
                norm.on_vector(dve)
                run(nc.vector.Fori, lambda i, n0: None, pair)

            @block.tensor
            def _(pe):
                def pair(i, n0, kind, m):
                    pe.wait_ge(lo_ok, i * 6 + (n0 + 1))
                    s = n0 % 2
                    if kind == "up":
                        for c in range(NCH):
                            q0 = NCH * m + c
                            if n0 == 0:
                                norm.before_chunk(pe, c)
                            if q0 >= 3:
                                pe.wait_ge(hid_ok, i * (NCH * 4) + (q0 - 2))
                            tok = slice(c * CH, (c + 1) * CH)
                            for u in range(2):
                                for k in range(KT):
                                    last = product3(nc, ps_up[:, c, u, 0:CH], w_hi[:, s, u, k], w_lo[:, s, u, k],
                                                    xn_hi[:, k, tok], xn_lo[:, k, tok], k == 0, k == KT - 1)
                            last.then_inc(up_ok, 1)
                    else:
                        pe.wait_ge(hlo_ok, i * (NCH * 4) + NCH * FG * (m + 1))
                        for r in range(ND):
                            k, c = r // NCH, r % NCH
                            if ND * m + r >= 2:
                                pe.wait_ge(dn_ev, i * (ND * 2) + (ND * m + r - 1))
                            tok = slice(c * CH, (c + 1) * CH)
                            for j in range(FG):
                                last = product3(nc, ps_dn[:, r % 2, 0:CH], w_hi[:, s, j, k], w_lo[:, s, j, k],
                                                h_hi[:, m % 2, j, tok], h_lo[:, m % 2, j, tok],
                                                j == 0, j == FG - 1)
                            last.then_inc(dn_ok, 1)
                run(nc.tensor.Fori, lambda i, n0: None, pair)


def project(nc, ctx, M, K, io, out, xT, x_dram, xn_hi, xn_lo, aq, kvT, DM, scratch):
    sem = lambda n: ctx.enter_context(nc.semaphore("d_" + n))
    COLS = [C_IQ, C_IQ + P, C_IK, C_AQ, C_AQ + P, C_AQ + 2 * P, C_AQ + 3 * P, C_AK, C_MI]
    HEAD, LOOP1, MID, LOOP2, TAIL = range(9), (9, N_PLAIN // 2 - 1), (15, 16), (17, N_SIG // 2 - 1), (35, 36)
    N_CHIP = 8
    TILES = [7, 6, 5, 4, 3, 2, NTP]
    with ExitStack() as mem, M.scope():
        raw = M.low("d_raw", [P, 2, KT, P])
        w_hi = M.low("d_w_hi", [P, 2, KT, P], F32R)
        w_lo = M.low("d_w_lo", [P, 2, KT, P], F32R)
        iq = M.low("iq", [P, 2, N_TOK])
        KTi = M.high("KTi", [P, 4, LS])
        dist_p, dist_s = M.high("dist_p_sb", [P, SEQ]), M.high("dist_s_sb", [P, LS])
        pair_mask = M.high("pair_mask_sb", [P, 4, P])
        ikw = M.low("ikw", [P, N_TOK])
        ikd = M.low("ikd", [P, N_TOK])
        iqd = M.low("iqd", [P, NI, P])
        iqm = M.low("iqm", [P, NI, 4, P])
        rel = M.low("rel", [P, 2, SEQ])
        stage = M.low("stage", [P, 2, N_TOK])
        tok_ik = M.low("tok_ik", [P, NT, DH + NI])
        top8 = M.low("top8", [P, 8])
        ik_raw = iqm[:].rearrange("p h j n -> p (h j n)").rearrange(
            "p (k b d) -> p k b d", k=PAST // P, b=DEC_BATCH)
        ps = psum(nc, mem, "d_ps", [P, NCH, 512])
        ps_s = psum(nc, mem, "d_ps_s", [P, 2, 1024])
        ps_t = psum(nc, mem, "d_ps_t", [P, 4, P])
        w_in, st_out = [sem("w_in0"), sem("w_in1")], [sem("st_out0"), sem("st_out1")]
        hi_ok, lo_ok, mm_ok, ev_ok = sem("hi_ok"), sem("lo_ok"), sem("mm_ok"), sem("ev_ok")
        dup, kcol, tp, tp_ev, o_out = sem("dup"), sem("kcol"), sem("tp"), sem("tp_ev"), sem("o_out")
        im_ok, sc_ok, rel_ok, acc_ok, ch = sem("im_ok"), sem("sc_ok"), sem("rel_ok"), sem("acc_ok"), sem("ch")
        ld, spilled, kt_tp, kt_ev = sem("ld"), sem("spilled"), sem("kt_tp"), sem("kt_ev")
        w_v = io["w_in"][0].rearrange("(k p) n -> p k n", p=P)
        sc_v = scratch.ap()
        norm = Norm(nc, sem, K, xT, K["g_mix"], xn_hi, xn_lo,
                    ikd[:, 0:2 * CH].rearrange("p (s n) -> p s n", s=2), stage[:, 0], stage[:, 1],
                    rel[:].rearrange("p a n -> p (a n)")[:, 0:4 * CH].rearrange("p (s n) -> p s n", s=4),
                    [ps[:, c, 0:CH] for c in range(NCH)])

        def run(loop, before, unit, scores=lambda: None, first=lambda: None):
            before(0, 0)
            first()
            for n0 in HEAD:
                before(0, n0 + 1)
                unit(0, n0)
                if n0 == 3:
                    scores()
            for (first, bodies), then in ((LOOP1, MID), (LOOP2, ())):
                with loop(0, bodies) as i:
                    for n0 in (first, first + 1):
                        before(i, n0 + 1)
                        unit(i, n0)
                for n0 in then:
                    before(0, n0 + 1)
                    unit(0, n0)
            before(0, TAIL[1])
            unit(0, TAIL[0])
            unit(0, TAIL[1])

        def score_dims(t):
            return (LS if t == NTP else P * (t + 1)), SCORE_OFF[t]

        with nc.Block() as block:
            @block.sync
            def _(sp):
                def load(i, n0):
                    if n0 >= 2:
                        sp.wait_ge(lo_ok, i * 2 + (n0 - 1))
                    if n0 < len(COLS):
                        src = w_v[:, :, COLS[n0]:COLS[n0] + P]
                    elif n0 < 17:
                        src = w_v[:, :, bass.ds(i * (2 * P) + (C_MQ + (n0 - 9) * P), P)]
                    else:
                        src = w_v[:, :, bass.ds(i * (2 * P) + (C_MO + (n0 - 17) * P), P)]
                    sp.dma_start(raw[:, n0 % 2], src).then_inc(w_in[n0 % 2], 16)

                def store(i, n0):
                    if n0 < N_CHIP:
                        return
                    sp.wait_ge(ev_ok, i * (2 * NCH) + NCH * (n0 + 1))
                    tile = N_PLAIN + N_SIG if n0 == 8 else i * 2 + (n0 - 9)
                    dst = sc_v[tile] if isinstance(tile, int) else \
                        sc_v[bass.ds(tile, 1)].rearrange("a p n -> p (a n)")
                    sp.dma_start(dst, stage[:, n0 % 2]).then_inc(st_out[n0 % 2], 16)

                def copies():
                    sp.wait_ge(ev_ok, 3 * NCH)
                    for half in range(2):
                        rows = slice(64 * half, 64 * half + 64)
                        sp.dma_start(ikd[rows, :], ikw[0:DH, :]).then_inc(dup, 16)
                        for par in range(2):
                            sp.dma_start(iqd[rows, par::2, :], iq[64 * par:64 * par + 64, :, SEQ:N_TOK])\
                                .then_inc(dup, 16)
                        new = ikw[0:DH, SEQ:N_TOK].rearrange("d (j r q) -> d j r q", r=2, q=DEC_SEQ)
                        sp.dma_start(KTi[rows, :, PAST:LS], new[:, :, half, :]).then_inc(kcol, 16)
                    sp.wait_ge(tp_ev, 3)
                    sp.dma_start(out["new_idxk_prompt"][0, 0].rearrange("(t p) d -> p t d", p=P),
                                 tok_ik[:, 0:NTP, 0:DH]).then_inc(o_out, 16)
                    sp.dma_start(out["new_idxk_sample"][0].rearrange("b q d -> (b q) d"),
                                 tok_ik[:, NTP, 0:DH]).then_inc(o_out, 16)
                def first():
                    sp.dma_start(x_dram.ap(), xT[:]).then_inc(spilled, 16)
                    for b in range(DEC_BATCH):
                        sp.dma_start(ik_raw[:, :, b, :], io["cache_idx_k"][0, b].rearrange("(k p) d -> p k d", p=P))\
                            .then_inc(ld, 16)
                    for dst, n in ((dist_p, "dist_p"), (dist_s, "dist_s"), (pair_mask, "pair_mask")):
                        sp.dma_start(dst[:], io[n]).then_inc(ld, 16)
                run(nc.sync.Fori, load, store, copies, first)
                for s in range(2):
                    sp.wait_ge(st_out[s], 16 * ((29 + 1 - s) // 2))
                sp.wait_ge(o_out, 32)

            @block.scalar
            def _(act):
                def split_hi(i, n0):
                    act.wait_ge(w_in[n0 % 2], i * 16 + 16 * (n0 // 2 + 1))
                    if n0 >= 2:
                        act.wait_ge(mm_ok, i * (2 * NCH) + NCH * (n0 - 1))
                    nc.scalar.activation(w_hi[:, n0 % 2], raw[:, n0 % 2], ACT.Copy).then_inc(hi_ok, 1)

                def evict(i, n0):
                    if n0 == 3:
                        act.wait_ge(spilled, 16)
                    if n0 >= N_CHIP + 2:
                        act.wait_ge(st_out[n0 % 2], i * 16 + 16 * ((n0 - N_CHIP) // 2))
                    for c in range(NCH):
                        act.wait_ge(mm_ok, i * (2 * NCH) + (NCH * n0 + c + 1))
                        tok = slice(c * CH, (c + 1) * CH)
                        if n0 < 2:
                            dst = iq[:, n0, tok]
                        elif n0 == 2:
                            dst = ikw[:, tok]
                        elif n0 < 7:
                            dst = aq[:, n0 - 3, tok]
                        elif n0 == 7:
                            dst = kvT[:, tok]
                        else:
                            dst = stage[:, n0 % 2, tok]
                        nc.scalar.activation(dst, ps[:, c, 0:CH], ACT.Sigmoid if n0 >= 17 else ACT.Copy)\
                            .then_inc(ev_ok, 1)

                def scores():
                    g = 0
                    for t in TILES:
                        L, _ = score_dims(t)
                        for h in range(NI):
                            act.wait_ge(sc_ok, g + 1)
                            if g >= 2:
                                act.wait_ge(acc_ok, g - 1)
                            nc.scalar.activation(rel[:, g % 2, 0:L], ps_s[:, g % 2, 0:L], ACT.Relu,
                                                 scale=IDX_SCALE).then_inc(rel_ok, 1)
                            g += 1
                norm.squares(act, 0)
                run(nc.scalar.Fori, split_hi, evict, scores, lambda: norm.on_scalar(act))

            @block.gpsimd
            def _(pool):
                def split_lo(i, n0):
                    pool.wait_ge(hi_ok, i * 2 + (n0 + 1))
                    nc.gpsimd.tensor_tensor(w_lo[:, n0 % 2], raw[:, n0 % 2], w_hi[:, n0 % 2].bitcast(F32),
                                            ALU.subtract).then_inc(lo_ok, 1)
                run(nc.gpsimd.Fori, split_lo, lambda i, n0: None, first=lambda: norm.on_gpsimd(pool))

            @block.tensor
            def _(pe):
                def unit(i, n0):
                    pe.wait_ge(lo_ok, i * 2 + (n0 + 1))
                    for c in range(NCH):
                        if n0 == 0:
                            norm.before_chunk(pe, c)
                        if n0:
                            pe.wait_ge(ev_ok, i * (2 * NCH) + (NCH * n0 + c - 2))
                        tok = slice(c * CH, (c + 1) * CH)
                        for k in range(KT):
                            last = product3(nc, ps[:, c, 0:CH], w_hi[:, n0 % 2, k], w_lo[:, n0 % 2, k],
                                            xn_hi[:, k, tok], xn_lo[:, k, tok], k == 0, k == KT - 1)
                        last.then_inc(mm_ok, 1)

                def scores():
                    pe.wait_ge(ld, 16 * (DEC_BATCH + 3))
                    for j in range(DEC_BATCH // 2):
                        if j:
                            pe.wait_ge(kt_ev, j)
                        for k in range(PAST // P):
                            last = nc.tensor.transpose(ps_t[:, k, :],
                                                       ik_raw[:, k, 2 * j:2 * j + 2, :].rearrange("p b d -> p (b d)"),
                                                       K["ident"][:])
                        last.then_inc(kt_tp, 1)
                    pe.wait_ge(kt_ev, DEC_BATCH // 2)
                    for b in range(3):
                        if b:
                            pe.wait_ge(tp_ev, b)
                        for j in range(3):
                            t = 3 * b + j
                            last = nc.tensor.transpose(ps_t[:, j, :], ikw[:, t * P:(t + 1) * P], K["ident"][:])
                        last.then_inc(tp, 1)
                    pe.wait_ge(dup, 16 * 6)
                    g = 0
                    for t in TILES:
                        L, _ = score_dims(t)
                        if t == NTP:
                            pe.wait_ge(kcol, 32)
                            pe.wait_ge(im_ok, NI)
                        for h in range(NI):
                            if g >= 2:
                                pe.wait_ge(rel_ok, g - 1)
                            half = slice(64 * (h % 2), 64 * (h % 2) + 64)
                            for at in range(0, L, 512):
                                w = min(512, L - at)
                                o = ps_s[:, g % 2, at:at + w]
                                if t < NTP:
                                    last = nc.tensor.matmul(o, iq[half, h // 2, t * P:(t + 1) * P],
                                                            ikd[half, at:at + w], start=True, stop=True)
                                else:
                                    for j in range(4):
                                        last = nc.tensor.matmul(o, iqm[:, h, j, :], KTi[:, j, at:at + w],
                                                                start=j == 0, stop=j == 3)
                            last.then_inc(sc_ok, 1)
                            g += 1
                run(nc.tensor.Fori, lambda i, n0: None, unit, scores)

            @block.vector
            def _(dve):
                norm.on_vector(dve)
                for j in range(DEC_BATCH // 2):
                    dve.wait_ge(kt_tp, j + 1)
                    nc.vector.tensor_copy(KTi[:, j, 0:PAST], ps_t[:].rearrange("p k n -> p (k n)")).then_inc(kt_ev, 1)
                dve.wait_ge(spilled, 16)
                for b in range(3):
                    dve.wait_ge(tp, b + 1)
                    nc.vector.tensor_copy(tok_ik[:, 3 * b:3 * b + 3, :], ps_t[:, 0:3, 0:DH + NI]).then_inc(tp_ev, 1)
                dve.wait_ge(dup, 16 * 6)
                for h in range(NI):
                    nc.vector.tensor_tensor(iqm[:, h], pair_mask[:], iqd[:, h:h + 1, :].to_broadcast([P, 4, P]),
                                            ALU.mult).then_inc(im_ok, 1)
                dve.wait_ge(tp_ev, 3)
                g = 0
                for t in TILES:
                    L, off = score_dims(t)
                    S = DM[:, off:off + L]
                    for h in range(NI):
                        dve.wait_ge(rel_ok, g + 1)
                        w = tok_ik[:, t, DH + h:DH + h + 1]
                        if h == 0:
                            nc.vector.tensor_scalar(S, rel[:, g % 2, 0:L], w, None, ALU.mult).then_inc(acc_ok, 1)
                        else:
                            dve.wait_ge(acc_ok, g)
                            nc.vector.scalar_tensor_tensor(S, rel[:, g % 2, 0:L], w, S, ALU.mult, ALU.add)\
                                .then_inc(acc_ok, 1)
                        g += 1
                n = 0
                dve.wait_ge(acc_ok, g)
                for t in TILES:
                    L, off = score_dims(t)
                    S = DM[:, off:off + L]
                    full, rest = divmod(TOPK_S if t == NTP else TOPK, 8)
                    if t < NTP:
                        nc.vector.memset(DM[0:CHUNK, off + L - CHUNK:off + L], BLOCKED).then_inc(ch, 1)
                        n += 1
                    dve.wait_ge(ch, n)
                    for _ in range(full):
                        dve.wait_ge(ch, n)
                        nc.vector.max(top8[:], S).then_inc(ch, 1)
                        dve.wait_ge(ch, n + 1)
                        nc.vector.match_replace(S, top8[:], S, TAKEN).then_inc(ch, 1)
                        n += 2
                    if rest:
                        dve.wait_ge(ch, n)
                        nc.vector.max(top8[:], S).then_inc(ch, 1)
                        dve.wait_ge(ch, n + 1)
                        nc.vector.memset(top8[:, rest:8], TAKEN).then_inc(ch, 1)
                        dve.wait_ge(ch, n + 2)
                        nc.vector.match_replace(S, top8[:], S, TAKEN).then_inc(ch, 1)
                        n += 3
                    dve.wait_ge(ch, n)
                    nc.vector.tensor_scalar(S, S, TAKEN * 0.999, BIG, ALU.is_gt, ALU.mult).then_inc(ch, 1)
                    dist = dist_s[:] if t == NTP else dist_p[:, SEQ - L:SEQ]
                    dve.wait_ge(ch, n + 1)
                    nc.vector.tensor_tensor(S, S, dist, ALU.add).then_inc(ch, 1)
                    n += 2
                for t in range(FIRST_SEL):
                    L, off = score_dims(t)
                    nc.vector.tensor_copy(DM[:, off:off + L], dist_p[:, SEQ - L:SEQ]).then_inc(ch, 1)
                    n += 1
                    dve.wait_ge(ch, n)
                    nc.vector.memset(DM[0:CHUNK, off + L - CHUNK:off + L], BIG).then_inc(ch, 1)
                    n += 1


def prepare_mix(nc, ctx, M, K, io, out, kvT, E, scratch):
    sem = lambda n: ctx.enter_context(nc.semaphore("e_" + n))
    with ExitStack() as mem, M.scope():
        mvT = M.low("mvT", [P, HM, N_TOK])
        nrow = M.low("n_rows", [DEC_BATCH * HM, DH])
        ri, rf = M.low("row_i", [HM, N_TOK]), M.low("row_f", [HM, N_TOK])
        t1, t2 = M.low("row_t1", [HM, N_TOK]), M.low("row_t2", [HM, N_TOK])
        b_, m_ = M.low("row_b", [HM, N_TOK]), M.low("row_m", [HM, N_TOK])
        keep = M.low("row_keep", [HM, N_TOK])
        G4 = M.low("gate_rows", [P, N_TOK])
        bi, bf = M.low("bias_i", [HM, 1]), M.low("bias_f", [HM, 1])
        m0 = M.low("m0", [HM, DEC_BATCH])
        NCK = NTP + DEC_BATCH
        mp, ml, ul = M.low("m_prev", [HM, NCK]), M.low("m_last", [HM, NCK]), M.low("u_last", [HM, NCK])
        dec = M.low("decay", [HM, NCK])
        ps = psum(nc, mem, "e_ps", [P, 4, 512])
        ps_n = psum(nc, mem, "e_ps_n", [P, 64])
        ps_d = psum(nc, mem, "e_ps_d", [P, HM, NCK])
        ld, ldv, ldc, ldg, ldr = (sem(n) for n in ("ld", "ldv", "ldc", "ldg", "ldr"))
        dup, o_out = sem("dup"), sem("o_out")
        tp, ev, row, ra, ones_ok, ra_q = sem("tp"), sem("ev"), sem("row"), sem("ra"), sem("ones"), sem("raq")
        g_ok, n_tp, d_ok = sem("g_ok"), sem("n_tp"), sem("d_ok")
        sc_v = scratch.ap()
        vaug, ktm, kvtok, CT, Gt = E["vaug"], E["ktm"], E["kvtok"], E["CT"], E["Gt"]

        BATCHES = [("kv", b) for b in range(3)] + [("v", t) for t in range(NT)] + \
                  [("mk", t) for t in range(NT)] + [("C", h) for h in range(HM)] + [("G", b) for b in range(3)]
        KV_DONE = 3

        with nc.Block() as block:
            @block.sync
            def _(sp):
                for h, (dst, rows) in enumerate(((ri, slice(0, HM)), (rf, slice(HM, 2 * HM)))):
                    sp.dma_start(dst[:], sc_v[N_PLAIN + N_SIG, rows, :]).then_inc(ldg, 16)
                bg = io["b_mlstm_gates"][0].rearrange("(g h a) -> g h a", g=2, a=1)
                sp.dma_start(bi[:], bg[0]).then_inc(ldg, 16)
                sp.dma_start(bf[:], bg[1]).then_inc(ldg, 16)
                sp.dma_start(keep[:], io["keep"]).then_inc(ldg, 16)
                sp.dma_start(m0[:], io["state_mlstm_m"][0].rearrange("b h -> h b"),
                             allow_slow_non_contiguous=True).then_inc(ldg, 16)
                sp.dma_start(E["head_sel"][:], io["head_sel"].rearrange("h k p -> k h p")).then_inc(ldg, 16)
                sp.dma_start(mvT[:], sc_v[4:8].rearrange("k p n -> p k n")).then_inc(ldv, 16)
                sp.dma_start(E["mqk"][:], sc_v[0:4].rearrange("k p n -> p k n")).then_inc(ldv, 16)
                for h in range(HM):
                    sp.dma_start(E["Cn"][:, h], io["state_mlstm_C"][0, :, h].rearrange("b v d -> v b d"))\
                        .then_inc(ldc, 16)
                sp.dma_start(nrow[:], io["state_mlstm_n"][0].rearrange("b h d -> (b h) d")).then_inc(ldc, 16)
                for n in ("causal_p", "causal_s", "batch_mask", "pair_mask"):
                    sp.dma_start(E[n][:], io[n]).then_inc(ld, 16)
                sp.wait_ge(ldv, 32)
                for half in range(2):
                    rows = slice(64 * half, 64 * half + 64)
                    for par in range(2):
                        src = slice(64 * par, 64 * par + 64)
                        sp.dma_start(E["mqd"][rows, par::2, :], E["mqk"][src, 0:2, SEQ:N_TOK]).then_inc(dup, 16)
                sp.wait_ge(ev, KV_DONE)
                for n, cols in (("k", slice(0, DH)), ("v", slice(DH, 2 * DH))):
                    sp.dma_start(out[f"new_{n}_prompt"][0, 0].rearrange("(t p) d -> p t d", p=P),
                                 kvtok[:, 0:NTP, cols]).then_inc(o_out, 16)
                    sp.dma_start(out[f"new_{n}_sample"][0].rearrange("b q d -> (b q) d"),
                                 kvtok[:, NTP, cols]).then_inc(o_out, 16)
                sp.wait_ge(ra, 4)
                sp.dma_start(out["new_m_prompt"][0, 0].rearrange("(h a) -> h a", a=1),
                             ml[:, NTP - 1:NTP]).then_inc(o_out, 16)
                sp.dma_start(out["new_m_sample"][0].rearrange("b h -> h b"), ml[:, NTP:NCK],
                             allow_slow_non_contiguous=True).then_inc(o_out, 16)
                sp.wait_ge(o_out, 96)
                sp.wait_ge(ld, 16 * 4)
                sp.wait_ge(dup, 16 * 4)
                sp.wait_ge(ldc, 16 * 5)

            @block.gpsimd
            def _(pool):
                nc.gpsimd.memset(G4[:], 0.0).then_inc(ones_ok, 1)
                nc.gpsimd.memset(vaug[:, :, :, DV:DV + 1], 1.0).then_inc(ones_ok, 1)
                nc.gpsimd.memset(mp[:, 0:1], 0.0).then_inc(ones_ok, 1)
                pool.wait_ge(ones_ok, 3)

            @block.vector
            def _(dve):
                cnt = [0]

                def step(ins):
                    cnt[0] += 1
                    ins.then_inc(row, 1)
                    dve.wait_ge(row, cnt[0])
                v = nc.vector
                smp = lambda t: t[:, SEQ:N_TOK].rearrange("h (b q) -> h b q", q=DEC_SEQ)
                prm = lambda t: t[:, 0:SEQ].rearrange("h (c q) -> h c q", q=P)
                dve.wait_ge(ldg, 16 * 7)
                step(v.tensor_scalar(ri[:], ri[:], bi[:], None, ALU.add))
                step(v.tensor_scalar(rf[:], rf[:], bf[:], None, ALU.add))
                step(v.scalar_tensor_tensor(t1[:], rf[:], -1.0, rf[:], ALU.mult, ALU.max))
                v.tensor_scalar(rf[:], rf[:], 0.0, None, ALU.min).then_inc(ra_q, 1)
                dve.wait_ge(ra_q, 1)
                dve.wait_ge(ra, 2)
                step(v.tensor_tensor(rf[:], rf[:], t2[:], ALU.subtract))
                step(v.tensor_tensor_scan(b_[:], keep[:], rf[:], 0.0, ALU.mult, ALU.add))
                step(v.tensor_copy(t2[:], ri[:]))
                step(v.tensor_tensor(dec[:, 0:DEC_BATCH], smp(rf)[:, :, 0], m0[:], ALU.add))
                step(v.tensor_tensor(smp(t2)[:, :, 0], dec[:, 0:DEC_BATCH], smp(ri)[:, :, 0], ALU.max))
                step(v.memset(smp(rf)[:, :, 0], -BIG))
                step(v.tensor_tensor_scan(m_[:], rf[:], t2[:], 0.0, ALU.add, ALU.max))
                step(v.tensor_copy(ml[:, 0:NTP], prm(m_)[:, :, P - 1]))
                step(v.tensor_copy(ml[:, NTP:NCK], smp(m_)[:, :, DEC_SEQ - 1]))
                dve.wait_ge(ones_ok, 3)
                step(v.tensor_copy(mp[:, 1:NTP], ml[:, 0:NTP - 1]))
                step(v.tensor_copy(mp[:, NTP:NCK], m0[:]))
                step(v.tensor_tensor(E["V"][:], ri[:], b_[:], ALU.subtract))
                step(v.tensor_tensor(E["U"][:], b_[:], m_[:], ALU.subtract))
                step(v.tensor_tensor(prm(t1), prm(E["U"]), mp[:, 0:NTP, None].to_broadcast([HM, NTP, P]), ALU.add))
                step(v.tensor_tensor(smp(t1), smp(E["U"]), mp[:, NTP:NCK, None].to_broadcast([HM, DEC_BATCH, DEC_SEQ]), ALU.add))
                step(v.tensor_copy(ul[:, 0:NTP], prm(E["U"])[:, :, P - 1]))
                step(v.tensor_copy(ul[:, NTP:NCK], smp(E["U"])[:, :, DEC_SEQ - 1]))
                step(v.tensor_tensor(prm(t2), prm(E["V"]), ul[:, 0:NTP, None].to_broadcast([HM, NTP, P]), ALU.add))
                step(v.tensor_tensor(smp(t2), smp(E["V"]), ul[:, NTP:NCK, None].to_broadcast([HM, DEC_BATCH, DEC_SEQ]), ALU.add))
                v.tensor_copy(G4[0:HM, :], E["V"][:]).then_inc(ra_q, 1)
                dve.wait_ge(ra_q, 2)
                dve.wait_ge(ra, 6)
                gw = G4[32:32 + HM, :]
                step(v.tensor_copy(dec[:, 0:NTP], prm(gw)[:, :, P - 1]))
                step(v.tensor_copy(dec[:, NTP:NCK], smp(gw)[:, :, DEC_SEQ - 1]))
                v.tensor_copy(t1[:, 0:1], dec[:, 0:1]).then_inc(g_ok, 1)
                dve.wait_ge(d_ok, 1)
                v.tensor_copy(E["decB"][:], ps_d[:]).then_inc(d_ok, 1)
                dve.wait_ge(d_ok, 2)
                for h in range(HM):
                    half = slice(64 * (h % 2), 64 * (h % 2) + 64)
                    step(v.tensor_copy(E["decP"][half, h // 2, :], E["decB"][half, h, 0:NTP]))

            @block.scalar
            def _(act):
                act.wait_ge(ra_q, 1)
                nc.scalar.activation(t2[:], t1[:], ACT.Exp, scale=-1.0).then_inc(ra, 1)
                act.wait_ge(ra, 1)
                nc.scalar.activation(t2[:], t2[:], ACT.Ln, bias=1.0).then_inc(ra, 1)

                def evict(n):
                    kind, x = BATCHES[n]
                    act.wait_ge(tp, n + 1)
                    src = ps[:, n % 4, :]
                    if kind == "kv":
                        dst, src = kvtok[:, 3 * x:3 * x + 3, :], src[:, 0:3 * P].rearrange("p (j n) -> p j n", j=3)
                    elif kind == "v":
                        dst, src = vaug[:, x, :, 0:DV], src.rearrange("p (h v) -> p h v", h=HM)
                    elif kind == "mk":
                        dst, src = ktm[:, x, :], src[:, 0:HM * DH]
                    elif kind == "C":
                        dst, src = CT[:, x, :, 0:DV], src.rearrange("p (j v) -> p j v", j=4)
                    else:
                        for j in range(3):
                            s3 = src[:, j * P:(j + 1) * P].rearrange("p (q n) -> p q n", q=4)[:, :, 0:HM]
                            last = nc.scalar.activation(Gt[:, 3 * x + j], s3, ACT.Copy)
                        last.then_inc(ev, 1)
                        return
                    nc.scalar.activation(dst, src, ACT.Copy).then_inc(ev, 1)

                for n in range(3):
                    evict(n)
                act.wait_ge(ra_q, 2)
                act.wait_ge(ones_ok, 3)
                nc.scalar.activation(ul[:, 0:1], ul[:, 0:1], ACT.Copy).then_inc(ra, 1)
                nc.scalar.activation(G4[32:32 + HM, :], t1[:], ACT.Exp).then_inc(ra, 1)
                nc.scalar.activation(G4[64:64 + HM, :], m_[:], ACT.Exp, scale=-1.0).then_inc(ra, 1)
                nc.scalar.activation(G4[96:96 + HM, :], t2[:], ACT.Exp).then_inc(ra, 1)
                for n in range(3, len(BATCHES)):
                    evict(n)
                act.wait_ge(n_tp, 1)
                nsrc = ps_n[0:DH, 0:DEC_BATCH * HM].rearrange("d (j r h) -> d h j r", r=2, h=HM)
                for par in range(2):
                    last = nc.scalar.activation(CT[64 * par:64 * par + 64, :, :, DV], nsrc[:, :, :, par], ACT.Copy)
                last.then_inc(n_tp, 1)

            @block.tensor
            def _(pe):
                for n, (kind, x) in enumerate(BATCHES):
                    if n >= 4:
                        pe.wait_ge(ev, n - 3)
                    o = lambda j, w=P: ps[:, n % 4, j * w:(j + 1) * w]
                    tok = lambda t: slice(t * P, (t + 1) * P)
                    if kind == "kv":
                        for j in range(3):
                            last = nc.tensor.transpose(o(j), kvT[:, tok(3 * x + j)], K["ident"][:])
                    elif kind == "v":
                        pe.wait_ge(ldv, 32)
                        for h in range(HM):
                            last = nc.tensor.transpose(o(h), mvT[:, h, tok(x)], K["ident"][:])
                    elif kind == "mk":
                        for h in range(2):
                            last = nc.tensor.transpose(o(h), E["mqk"][:, 2 + h, tok(x)], K["ident"][:])
                    elif kind == "C":
                        pe.wait_ge(ldc, 16 * 5)
                        for j in range(4):
                            last = nc.tensor.transpose(o(j), E["Cn"][:, x, 2 * j:2 * j + 2, :]
                                                       .rearrange("p b d -> p (b d)"), K["ident"][:])
                    else:
                        pe.wait_ge(ra, 6)
                        for j in range(3):
                            last = nc.tensor.transpose(o(j), G4[:, tok(3 * x + j)], K["ident"][:])
                    last.then_inc(tp, 1)
                NR = DEC_BATCH * HM
                nc.tensor.transpose(ps_n[0:DH, 0:NR], nrow[:], K["ident"][0:NR, 0:NR]).then_inc(n_tp, 1)
                pe.wait_ge(g_ok, 1)
                for h in range(HM):
                    last = nc.tensor.matmul(ps_d[:, h, :], E["head_sel"][:, h, :], dec[:], start=True, stop=True)
                last.then_inc(d_ok, 1)


def mlstm(nc, ctx, M, K, io, out, kvT, E, num):
    sem = lambda n: ctx.enter_context(nc.semaphore("m_" + n))
    with ExitStack() as mem, M.scope():
        St = M.low("state", [P, 2, 2, DV + 1])
        lg = M.low("m_lg", [P, 2, HM * P])
        W = lg
        SW = M.low("m_sw", [P, 2, HM * P])
        kw = M.low("m_kw", [P, 2, HM, DH])
        ti = M.low("m_ti", [P, 2, HM, DV + 1])
        gws = M.low("m_gws", [P, NT, HM])
        qm = M.low("m_qm", [P, HM, 4, P])
        n1 = M.low("m_n1", [1, HM, DEC_BATCH, DH])
        kwb = M.low("m_kwb", [P, HM, DEC_BATCH, DH])
        kraw = kwb
        Cd, nd = E["Cn"], n1
        Cp = M.low("m_cp", [P, HM, DH])
        ps_d = psum(nc, mem, "m_ps_d", [P, 512])
        ps_s = psum(nc, mem, "m_ps_s", [P, 512])
        ps_i = [psum(nc, mem, f"m_ps_i{x}", [P, 512]) for x in range(2)]
        ps_n = [psum(nc, mem, f"m_ps_n{x}", [P, 512]) for x in range(2)]
        ps_u = psum(nc, mem, "m_ps_u", [P, 512])
        ps_x = psum(nc, mem, "m_ps_x", [P, 512])
        (d_ok, lg_ok, w_ok, s_ok, sw_ok, i_ok, n_ok, ti_ok, num_ok, kw_ok, u_ok, st_ok, init, q_ok, kb_ok, c_ok,
         n1_ok, cd_ok, cs_ok, o_out, fp, fe, nr_ok) = (sem(n) for n in (
             "d_ok", "lg_ok", "w_ok", "s_ok", "sw_ok", "i_ok", "n_ok", "ti_ok", "num_ok", "kw_ok", "u_ok", "st_ok",
             "init", "q_ok", "kb_ok", "c_ok", "n1_ok", "cd_ok", "cs_ok", "o_out", "fp", "fe", "nr_ok"))
        ldk, lda, ldn, kt_tp, kt_ev, half_ok = (sem(n) for n in ("ldk", "lda", "ldn", "kt_tp", "kt_ev", "half_ok"))
        mqk, vaug, ktm, Gt, CT = E["mqk"], E["vaug"], E["ktm"], E["Gt"], E["CT"]
        pair = lambda b: b[:, 0:2 * (DV + 1)].rearrange("p (h v) -> p h v", h=2)

        with nc.Block() as block:
            @block.sync
            def _(sp):
                sp.dma_start(n1[:], io["state_mlstm_n"][0:1].rearrange("a b h d -> a h b d")).then_inc(ldn, 16)
                for b in range(DEC_BATCH):
                    sp.dma_start(kraw[:, :, b, :], io["cache_attn_k"][0, b].rearrange("(k p) d -> p k d", p=P))\
                        .then_inc(ldk, 16)
                for b in range(DEC_BATCH):
                    sp.dma_start(E["vn"][:, b, :], E["kvtok"][b * DEC_SEQ:(b + 1) * DEC_SEQ, NTP, DH:2 * DH])\
                        .then_inc(lda, 16)
                for half in range(2):
                    rows = slice(64 * half, 64 * half + 64)
                    sp.dma_start(E["kd"][rows, :], kvT[0:DH, :]).then_inc(lda, 16)
                    new = kvT[0:DH, SEQ:N_TOK].rearrange("d (j r q) -> d j r q", r=2, q=DEC_SEQ)
                    sp.dma_start(E["KTa"][rows, :, PAST:LS], new[:, :, half, :]).then_inc(lda, 16)
                sp.wait_ge(lda, 16 * (DEC_BATCH + 4))
                sp.wait_ge(fe, 1)
                sp.dma_start(out["new_C_prompt"][0, 0].rearrange("h v d -> v h d"), Cp[:]).then_inc(o_out, 16)
                for h in range(HM):
                    half = slice(64 * (h % 2), 64 * (h % 2) + 64)
                    sp.dma_start(out["new_n_prompt"][0, 0, h].rearrange("(d a) -> d a", a=1),
                                 St[half, NTP % 2, h // 2, DV:DV + 1]).then_inc(o_out, 16)
                for h in range(HM):
                    sp.wait_ge(cs_ok, h + 1)
                    sp.dma_start(out["new_C_sample"][0, :, h].rearrange("b v d -> v b d"), Cd[:, h]).then_inc(o_out, 16)
                sp.wait_ge(nr_ok, 1)
                sp.dma_start(out["new_n_sample"][0:1].rearrange("a b h d -> a h b d"), nd[:]).then_inc(o_out, 16)
                sp.wait_ge(o_out, 16 * (2 + 2 * HM))

            @block.gpsimd
            def _(pool):
                nc.gpsimd.memset(St[:, 0], 0.0).then_inc(init, 1)
                dB = E["decB"][:, :, NTP:]
                nc.gpsimd.tensor_tensor(Cd[:], E["Cn"][:], dB[:, :, :, None].to_broadcast([P, HM, DEC_BATCH, DH]),
                                        ALU.mult).then_inc(cd_ok, 1)
                pool.wait_ge(ldn, 16)
                nc.gpsimd.tensor_tensor(nd[:], n1[:], dB[0:1, :, :, None].to_broadcast([1, HM, DEC_BATCH, DH]),
                                        ALU.mult).then_inc(cd_ok, 1)
                for h in range(HM):
                    nc.gpsimd.tensor_tensor(qm[:, h], E["pair_mask"][:], E["mqd"][:, h:h + 1, :]
                                            .to_broadcast([P, 4, P]), ALU.mult).then_inc(q_ok, 1)
                for r in range(2):
                    for par in range(2):
                        dst = E["aqr"][64 * r:64 * r + 64].rearrange("d j (g p q) -> d p g j q", g=4, p=2)
                        src = E["aq"][64 * par:64 * par + 64, :, SEQ:N_TOK].rearrange(
                            "d g (j r q) -> d r g j q", r=2, q=DEC_SEQ)
                        pool.wait_ge(q_ok, HM + 2 * r + par)
                        nc.gpsimd.tensor_copy(dst[:, par], src[:, r]).then_inc(q_ok, 1)
                pool.wait_ge(q_ok, HM + 4)

            @block.scalar
            def _(act):
                act.wait_ge(init, 2)
                for t in range(NT):
                    act.wait_ge(lg_ok, t + 1)
                    nc.scalar.activation(W[:, t % 2], lg[:, t % 2], ACT.Exp).then_inc(w_ok, 1)
                    if t >= 2:
                        act.wait_ge(num_ok, 2 * (t - 1))
                    for y in range(2):
                        act.wait_ge(n_ok, 2 * t + y + 1)
                        for x in range(2):
                            h = 2 * x + y
                            nc.scalar.activation(ti[:, t % 2, h], pair(ps_n[y])[:, x], ACT.Copy,
                                                 scale=gws[:, t, h:h + 1]).then_inc(ti_ok, 1)
                    if t < 4:
                        act.wait_ge(kt_tp, t + 1)
                        nc.scalar.activation(E["KTa"][:, t, 0:PAST], ps_x[:], ACT.Copy).then_inc(kt_ev, 1)
                act.wait_ge(fp, 1)
                nc.scalar.activation(Cp[:], ps_x[:, 0:HM * DH].rearrange("p (h d) -> p h d", h=HM), ACT.Copy)\
                    .then_inc(fe, 1)

            @block.vector
            def _(dve):
                nc.vector.tensor_scalar(gws[:], Gt[:, :, 1, :], QK_SCALE, None, ALU.mult).then_inc(init, 1)
                for t in range(NT):
                    mask = E["causal_s" if t == NTP else "causal_p"][:, None, :].to_broadcast([P, HM, P])
                    if t >= 2:
                        dve.wait_ge(u_ok, t - 1)
                    nc.vector.tensor_tensor(kw[:, t % 2], ktm[:, t, :].rearrange("p (h d) -> p h d", h=HM),
                                            Gt[:, t, 3, :, None].to_broadcast([P, HM, DH]), ALU.mult).then_inc(kw_ok, 1)
                    dve.wait_ge(d_ok, t + 1)
                    if t >= 2:
                        dve.wait_ge(sw_ok, t - 1)
                    nc.vector.tensor_tensor(lg[:, t % 2].rearrange("p (h t) -> p h t", h=HM),
                                            ps_d[:, :].rearrange("p (h t) -> p h t", h=HM), mask, ALU.add)\
                        .then_inc(lg_ok, 1)
                    if t < NTP:
                        dve.wait_ge(u_ok, t + 1)
                        if t == 0:
                            dve.wait_ge(init, 2)
                        for x in range(2):
                            if t:
                                dve.wait_ge(st_ok, 2 * t)
                            nc.vector.scalar_tensor_tensor(St[:, (t + 1) % 2, x], St[:, t % 2, x],
                                                           E["decP"][:, x, t:t + 1], pair(ps_u)[:, x],
                                                           ALU.mult, ALU.add).then_inc(st_ok, 1)
                    dve.wait_ge(w_ok, t + 1)
                    dve.wait_ge(s_ok, t + 1)
                    if t >= 2:
                        dve.wait_ge(i_ok, 2 * (t - 1))
                    nc.vector.scalar_tensor_tensor(SW[:, t % 2], ps_s[:], QK_SCALE, W[:, t % 2], ALU.mult, ALU.mult)\
                        .then_inc(sw_ok, 1)
                    for x in range(2):
                        dve.wait_ge(i_ok, 2 * t + x + 1)
                        dve.wait_ge(ti_ok, 4 * t + 4)
                        nc.vector.tensor_tensor(num[:, t, 2 * x:2 * x + 2, :], ti[:, t % 2, 2 * x:2 * x + 2, :],
                                                pair(ps_i[x]), ALU.add).then_inc(num_ok, 1)
                dve.wait_ge(kw_ok, NT)
                dve.wait_ge(kt_tp, 4)
                for h in range(HM):
                    nc.vector.tensor_tensor(kwb[:, h], kw[:, NTP % 2, h:h + 1, :].to_broadcast([P, DEC_BATCH, DH]),
                                            E["batch_mask"][:, :, None].to_broadcast([P, DEC_BATCH, DH]),
                                            ALU.mult).then_inc(kb_ok, 1)
                dve.wait_ge(cd_ok, 2)
                for h in range(HM):
                    dve.wait_ge(c_ok, h + 1)
                    nc.vector.tensor_tensor(Cd[:, h], Cd[:, h], ps_d[:].rearrange("p (b d) -> p b d", b=DEC_BATCH),
                                            ALU.add).then_inc(cs_ok, 1)
                    dve.wait_ge(n1_ok, h + 1)
                    nc.vector.tensor_tensor(nd[:, h], nd[:, h], ps_s[0:1].rearrange("p (b d) -> p b d", b=DEC_BATCH),
                                            ALU.add).then_inc(cs_ok if h < 0 else fe if h < 0 else kb_ok, 1)
                dve.wait_ge(kb_ok, 2 * HM)
                nc.vector.tensor_copy(gws[0:1, 0, 0:1], gws[0:1, 0, 1:2]).then_inc(nr_ok, 1)

            @block.tensor
            def _(pe):
                for t in range(NT):
                    tok = slice(t * P, (t + 1) * P)
                    if t:
                        pe.wait_ge(lg_ok, t)
                    for h in range(HM):
                        o = ps_d[:, h * P:(h + 1) * P]
                        nc.tensor.matmul(o, E["head_sel"][:, h, :], E["U"][:, tok], start=True, stop=False)
                        last = nc.tensor.matmul(o, E["V"][:, tok], E["head_sel"][:, h, :], start=False, stop=True)
                    last.then_inc(d_ok, 1)
                    if t:
                        pe.wait_ge(sw_ok, t)
                    for h in (0, 2, 1, 3):
                        if h == 1:
                            pe.wait_ge(half_ok, t + 1)
                        half = slice(64 * (h % 2), 64 * (h % 2) + 64)
                        last = nc.tensor.matmul(ps_s[:, h * P:(h + 1) * P], mqk[half, 2 + h // 2, tok],
                                                mqk[half, h // 2, tok], start=True, stop=True)
                        if h == 2:
                            last.then_inc(half_ok, 1)
                    last.then_inc(s_ok, 1)
                    pe.wait_ge(kw_ok, t + 1)
                    if t < NTP:
                        if t:
                            pe.wait_ge(st_ok, 2 * t)
                        for h in range(HM):
                            half = slice(64 * (h % 2), 64 * (h % 2) + 64)
                            last = nc.tensor.matmul(pair(ps_u)[half, h // 2], kw[:, t % 2, h, :], vaug[:, t, h, :],
                                                    start=True, stop=True)
                        last.then_inc(u_ok, 1)
                    if t == 0:
                        pe.wait_ge(init, 2)
                    if t == NTP:
                        pe.wait_ge(q_ok, HM)
                    for y in range(2):
                        if t:
                            pe.wait_ge(ti_ok, 4 * (t - 1) + 2 * y + 2)
                        for x in range(2):
                            h = 2 * x + y
                            half = slice(64 * y, 64 * y + 64)
                            o = pair(ps_n[y])[:, x]
                            if t < NTP:
                                last = nc.tensor.matmul(o, mqk[half, h // 2, tok], St[half, t % 2, h // 2, :],
                                                        start=True, stop=True)
                            else:
                                for j in range(4):
                                    last = nc.tensor.matmul(o, qm[:, h, j, :], CT[:, h, j, :],
                                                            start=j == 0, stop=j == 3)
                        last.then_inc(n_ok, 1)
                    pe.wait_ge(sw_ok, t + 1)
                    for x in range(2):
                        if t:
                            pe.wait_ge(num_ok, 2 * (t - 1) + x + 1)
                        for y in range(2):
                            h = 2 * x + y
                            last = nc.tensor.matmul(pair(ps_i[x])[:, y], SW[:, t % 2, h * P:(h + 1) * P],
                                                    vaug[:, t, h, :], start=True, stop=True)
                        last.then_inc(i_ok, 1)
                    if t < 4:
                        pe.wait_ge(ldk, 16 * DEC_BATCH)
                        if t:
                            pe.wait_ge(kt_ev, t)
                        for k in range(4):
                            last = nc.tensor.transpose(ps_x[:, k * P:(k + 1) * P],
                                                       kraw[:, k, 2 * t:2 * t + 2, :].rearrange("p b d -> p (b d)"),
                                                       K["ident"][:])
                        last.then_inc(kt_tp, 1)
                pe.wait_ge(kt_ev, 4)
                pe.wait_ge(st_ok, 2 * NTP)
                for h in (0, 2, 1, 3):
                    if h == 1:
                        pe.wait_ge(half_ok, NT + 1)
                    half = slice(64 * (h % 2), 64 * (h % 2) + 64)
                    last = nc.tensor.transpose(ps_x[:, h * DH:(h + 1) * DH], St[half, NTP % 2, h // 2, 0:DV],
                                               K["ident"][half, half])
                    if h == 2:
                        last.then_inc(half_ok, 1)
                last.then_inc(fp, 1)
                for h in range(HM):
                    pe.wait_ge(kb_ok, HM)
                    if h:
                        pe.wait_ge(cs_ok, h)
                    f = kwb[:, h].rearrange("p b d -> p (b d)")
                    nc.tensor.matmul(ps_d[:], vaug[:, NTP, h, 0:DV], f, start=True, stop=True).then_inc(c_ok, 1)
                    if h:
                        pe.wait_ge(kb_ok, HM + h)
                    nc.tensor.matmul(ps_s[0:1, :], K["ones"][:, 0:1], f, start=True, stop=True).then_inc(n1_ok, 1)


def mlstm_output(nc, ctx, M, K, E, num, h_hi, h_lo, scratch):
    sem = lambda n: ctx.enter_context(nc.semaphore("h_" + n))
    with ExitStack() as mem, M.scope():
        og = M.low("h_og", [P, HM, N_TOK])
        sq = M.low("h_sq", [P, DV])
        ss, den, inv, rs, sc = (M.low("h_" + n, [P, NT, HM]) for n in ("ss", "den", "inv", "rs", "sc"))
        hn = M.low("h_n", [P, 2, HM, DV])
        full = M.low("h_full", [P, 2, HM, P])
        ps = psum(nc, mem, "h_ps", [P, 2, 512])
        ld, ss_ok, row, rs_in, rs_ok, n_ok, tp, f_ok, hi, lo = (
            sem(n) for n in ("ld", "ss_ok", "row", "rs_in", "rs_ok", "n_ok", "tp", "f_ok", "hi", "lo"))
        with nc.Block() as block:
            @block.sync
            def _(sp):
                sp.dma_start(og[:], scratch.ap()[N_PLAIN:N_PLAIN + HM].rearrange("k p n -> p k n")).then_inc(ld, 16)

            @block.scalar
            def _(act):
                n = 0
                for t in range(NT):
                    for h in range(HM):
                        if n:
                            act.wait_ge(ss_ok, n)
                        nc.scalar.activation(sq[:], num[:, t, h, 0:DV], ACT.Square,
                                             accum_out=ss[:, t, h:h + 1]).then_inc(ss_ok, 1)
                        n += 1
                act.wait_ge(rs_in, 1)
                nc.scalar.activation(rs[:], rs[:], ACT.Sqrt).then_inc(rs_ok, 1)
                for t in range(NT):
                    act.wait_ge(f_ok, HM * (t + 1))
                    nc.scalar.activation(h_hi[:, :, t * P:(t + 1) * P], full[:, t % 2], ACT.Copy).then_inc(hi, 1)

            @block.vector
            def _(dve):
                v, cnt = nc.vector, [0]

                def step(ins):
                    cnt[0] += 1
                    ins.then_inc(row, 1)
                    dve.wait_ge(row, cnt[0])
                nq = num[:, :, :, DV]
                step(v.scalar_tensor_tensor(den[:], nq, -1.0, nq, ALU.mult, ALU.max))
                step(v.tensor_tensor(den[:], den[:], E["Gt"][:, :, 2, :], ALU.max))
                step(v.reciprocal(inv[:], den[:]))
                dve.wait_ge(ss_ok, NT * HM)
                step(v.tensor_tensor(rs[:], ss[:], inv[:], ALU.mult))
                step(v.tensor_tensor(rs[:], rs[:], inv[:], ALU.mult))
                step(v.tensor_scalar(rs[:], rs[:], 1.0 / DV, EPS, ALU.mult, ALU.add))
                v.reciprocal(rs[:], rs[:]).then_inc(rs_in, 1)
                dve.wait_ge(rs_ok, 1)
                step(v.tensor_tensor(sc[:], inv[:], rs[:], ALU.mult))

                def scaled(t):
                    if t >= 2:
                        dve.wait_ge(tp, t - 1)
                    v.tensor_tensor(hn[:, t % 2], num[:, t, :, 0:DV], sc[:, t, :, None].to_broadcast([P, HM, DV]),
                                    ALU.mult).then_inc(n_ok, 1)
                scaled(0)
                dve.wait_ge(ld, 16)
                for t in range(NT):
                    if t + 1 < NT:
                        scaled(t + 1)
                    dve.wait_ge(tp, t + 1)
                    if t >= 2:
                        dve.wait_ge(lo, t - 1)
                    for h in range(HM):
                        v.scalar_tensor_tensor(full[:, t % 2, h], ps[:, t % 2, h * P:(h + 1) * P],
                                               K["g_mlstm"][:, h:h + 1], og[:, h, t * P:(t + 1) * P],
                                               ALU.mult, ALU.mult).then_inc(f_ok, 1)

            @block.gpsimd
            def _(pool):
                for t in range(NT):
                    pool.wait_ge(hi, t + 1)
                    tok = slice(t * P, (t + 1) * P)
                    nc.gpsimd.tensor_tensor(h_lo[:, :, tok], full[:, t % 2], h_hi[:, :, tok].bitcast(F32),
                                            ALU.subtract).then_inc(lo, 1)

            @block.tensor
            def _(pe):
                for t in range(NT):
                    pe.wait_ge(n_ok, t + 1)
                    if t >= 2:
                        pe.wait_ge(f_ok, HM * (t - 1))
                    for h in range(HM):
                        last = nc.tensor.transpose(ps[:, t % 2, h * P:(h + 1) * P], hn[:, t % 2, h, :], K["ident"][:])
                    last.then_inc(tp, 1)


def attention(nc, ctx, M, K, io, E, DM, o_hi, o_lo):
    sem = lambda n: ctx.enter_context(nc.semaphore("t_" + n))
    ITEMS = [(t, x) for t in range(NT) for x in range(HA)]
    NKS = PAST // P
    HALVES = len(ITEMS) // 4
    with ExitStack() as mem, M.scope():
        vc = M.low("vc", [P, NKS, DEC_BATCH, DH])
        lg = M.low("t_lg", [P, 2, SEQ])
        pr = M.low("t_p", [P, 2, SEQ])
        PT = M.low("t_pt", [P, 2, NTP, P])
        DMr = M.low("t_dmr", [P, DEC_BATCH, LS])
        slope = M.low("t_slope", [P, 1])
        mx, nm = M.low("t_mx", [P, 2]), M.low("t_nm", [P, 2])
        sm, inv = M.low("t_sm", [P, 2]), M.low("t_inv", [P, 2])
        ofs = M.low("t_ofs", [P, 2, 2 * P])
        ps_l = psum(nc, mem, "t_ps_l", [P, 2, 1024])
        ps_t = psum(nc, mem, "t_ps_t", [P, 2, 512])
        ps_o = psum(nc, mem, "t_ps_o", [P, HA, P])
        (ld, ldm, qk, lg_ok, mx_ok, nm_ok, p_ok, inv_ok, pn_ok, tr, tr_ev, pv, of_ok, hi, lo) = (
            sem(n) for n in ("ld", "ldm", "qk", "lg_ok", "mx_ok", "nm_ok", "p_ok", "inv_ok", "pn_ok", "tr",
                             "tr_ev", "pv", "of_ok", "hi", "lo"))

        def keys(t):
            return LS if t == NTP else P * (t + 1)

        BATCH = []
        for t, _ in ITEMS:
            n = -(-keys(t) // P)
            BATCH.append([(k, min(k + 4, n)) for k in range(0, n, 4)])
        UPTO = np.cumsum([0] + [len(b) for b in BATCH]).tolist()

        def half_out(a, m):
            t, g = divmod(m, 2)
            if t < NTP:
                return a[:, 2 * g:2 * g + 2, t * P:(t + 1) * P]
            return a[:, :, SEQ + 64 * g:SEQ + 64 * g + 64]

        def half_staged(m):
            return ofs[:, m % 2].rearrange("p (j n) -> p j n", j=2 if m // 2 < NTP else 4)

        with nc.Block() as block:
            @block.sync
            def _(sp):
                for b in range(DEC_BATCH):
                    sp.dma_start(vc[:, :, b, :], io["cache_attn_v"][0, b].rearrange("(k p) d -> p k d", p=P))\
                        .then_inc(ld, 16)
                sp.dma_start(slope[:], io["slope"]).then_inc(ldm, 16)
                for b in range(DEC_BATCH):
                    rows = slice(b * DEC_SEQ, (b + 1) * DEC_SEQ)
                    for h in range(HA):
                        sp.dma_start(DMr[h * DEC_SEQ:(h + 1) * DEC_SEQ, b, :],
                                     DM[rows, SCORE_OFF[NTP]:SCORE_OFF[NTP] + LS]).then_inc(ldm, 16)

            @block.gpsimd
            def _(pool):
                for m in range(HALVES):
                    pool.wait_ge(hi, m + 1)
                    nc.gpsimd.tensor_tensor(half_out(o_lo, m), half_staged(m), half_out(o_hi, m).bitcast(F32),
                                            ALU.subtract).then_inc(lo, 1)

            @block.tensor
            def _(pe):
                def product(i):
                    t, x = ITEMS[i]
                    if i >= 2:
                        pe.wait_ge(lg_ok, i - 1)
                    half = slice(64 * (x % 2), 64 * (x % 2) + 64)
                    L = keys(t)
                    for at in range(0, L, 512):
                        w = min(512, L - at)
                        o = ps_l[:, i % 2, at:at + w]
                        if t < NTP:
                            q, k = E["aq"][half, x // 2, t * P:(t + 1) * P], E["kd"][half, at:at + w]
                        else:
                            q, k = E["aqr"][half, x // 2, :], E["KTa"][half, x // 2, at:at + w]
                        last = nc.tensor.matmul(o, q, k, start=True, stop=True)
                    last.then_inc(qk, 1)

                def transposes(i):
                    t, _ = ITEMS[i]
                    pe.wait_ge(pn_ok, i + 1)
                    for g, (k0, k1) in enumerate(BATCH[i], UPTO[i]):
                        if g >= 2:
                            pe.wait_ge(tr_ev, g - 1)
                        for k in range(k0, k1):
                            w = min(P, keys(t) - k * P)
                            last = nc.tensor.transpose(ps_t[0:w, g % 2, (k - k0) * P:(k - k0 + 1) * P],
                                                       pr[:, i % 2, k * P:k * P + w], K["ident"][:])
                        last.then_inc(tr, 1)

                def values(i):
                    t, x = ITEMS[i]
                    pe.wait_ge(tr_ev, UPTO[i + 1])
                    if x % 4 == 0 and i >= HA:
                        pe.wait_ge(of_ok, 2 * (i // 4 - 1))
                    n = t + 1 if t < NTP else NKS + 1
                    for k in range(n):
                        if t < NTP:
                            v, w = E["kvtok"][:, k, DH:2 * DH], PT[:, i % 2, k, :]
                        elif k < NKS:
                            v, w = vc[:, k, x, :], PT[:, i % 2, k, :]
                        else:
                            v, w = E["vn"][:, x, :], PT[0:DEC_SEQ, i % 2, k, :]
                        last = nc.tensor.matmul(ps_o[0:DH, x, :], v, w, start=k == 0, stop=k == n - 1)
                    last.then_inc(pv, 1)

                product(0)
                product(1)
                for i in range(len(ITEMS)):
                    if i + 2 < len(ITEMS):
                        product(i + 2)
                    transposes(i)
                    if i == NTP * HA + 1:
                        pe.wait_ge(ld, 16 * DEC_BATCH)
                    if i:
                        values(i - 1)
                values(len(ITEMS) - 1)

            @block.vector
            def _(dve):
                v = nc.vector

                def logits(i):
                    t, x = ITEMS[i]
                    L = keys(t)
                    if i == NTP * HA:
                        dve.wait_ge(ldm, 16 * (DEC_BATCH * HA + 1))
                    dve.wait_ge(qk, i + 1)
                    if i >= 2:
                        dve.wait_ge(p_ok, i - 1)
                    if t < NTP:
                        dist, by = DM[:, SCORE_OFF[t]:SCORE_OFF[t] + L], -SLOPE[x]
                    else:
                        dist, by = DMr[:, x, :], slope[:]
                    v.scalar_tensor_tensor(lg[:, i % 2, 0:L], dist, by, ps_l[:, i % 2, 0:L], ALU.mult, ALU.add)\
                        .then_inc(lg_ok, 1)
                    dve.wait_ge(lg_ok, i + 1)
                    v.reduce_max(mx[:, i % 2:i % 2 + 1], lg[:, i % 2, 0:L], AX_X).then_inc(mx_ok, 1)
                    dve.wait_ge(mx_ok, i + 1)
                    v.tensor_scalar(nm[:, i % 2:i % 2 + 1], mx[:, i % 2:i % 2 + 1], -QK_SCALE, None,
                                    ALU.mult).then_inc(nm_ok, 1)

                def normalise(i):
                    L, one = keys(ITEMS[i][0]), slice(i % 2, i % 2 + 1)
                    dve.wait_ge(p_ok, i + 1)
                    v.reciprocal(inv[:, one], sm[:, one]).then_inc(inv_ok, 1)
                    dve.wait_ge(inv_ok, i + 1)
                    v.tensor_scalar(pr[:, i % 2, 0:L], pr[:, i % 2, 0:L], inv[:, one], None, ALU.mult)\
                        .then_inc(pn_ok, 1)

                logits(0)
                logits(1)
                for i in range(len(ITEMS)):
                    normalise(i)
                    if i + 2 < len(ITEMS):
                        logits(i + 2)

            @block.scalar
            def _(act):
                def probs(i):
                    L, one = keys(ITEMS[i][0]), slice(i % 2, i % 2 + 1)
                    act.wait_ge(nm_ok, i + 1)
                    if i >= 2:
                        act.wait_ge(tr, UPTO[i - 1])
                    nc.scalar.activation(pr[:, i % 2, 0:L], lg[:, i % 2, 0:L], ACT.Exp, bias=nm[:, one],
                                         scale=QK_SCALE, accum_out=sm[:, one]).then_inc(p_ok, 1)

                def evict(i):
                    if i >= 2:
                        act.wait_ge(pv, i - 1)
                    for g, (k0, k1) in enumerate(BATCH[i], UPTO[i]):
                        act.wait_ge(tr, g + 1)
                        src = ps_t[:, g % 2, 0:(k1 - k0) * P].rearrange("p (k n) -> p k n", n=P)
                        rows = slice(0, min(P, keys(ITEMS[i][0]) - k0 * P))
                        nc.scalar.activation(PT[rows, i % 2, k0:k1, :], src[rows], ACT.Copy).then_inc(tr_ev, 1)

                def output(m):
                    t, g = divmod(m, 2)
                    act.wait_ge(pv, 4 * m + 4)
                    if m >= 2:
                        act.wait_ge(lo, m - 1)
                    for r in range(2):
                        src, dst = ps_o[0:DH, 4 * g:4 * g + 4, :], half_staged(m)[64 * r:64 * r + 64]
                        if t < NTP:
                            src = src.rearrange("d (j r) n -> d r j n", r=2)[:, r]
                        else:
                            src = src.rearrange("d b (j r q) -> d r j b q", j=4, r=2)[:, r]
                            dst = dst.rearrange("d j (b q) -> d j b q", b=4)
                        nc.scalar.activation(dst, src, ACT.Copy).then_inc(of_ok, 1)
                    act.wait_ge(of_ok, 2 * (m + 1))
                    nc.scalar.activation(half_out(o_hi, m), half_staged(m), ACT.Copy).then_inc(hi, 1)

                probs(0)
                for i in range(len(ITEMS)):
                    if i + 1 < len(ITEMS):
                        probs(i + 1)
                    evict(i)
                    if i >= 5 and i % 4 == 1:
                        output((i - 5) // 4)
                output(HALVES - 1)


def mix_out(nc, ctx, M, K, io, o, h, y, ya, yb, scratch):
    sem = lambda n: ctx.enter_context(nc.semaphore("b_" + n))
    (o_hi, o_lo), (h_hi, h_lo), (y_hi, y_lo) = o, h, y
    BODIES = KT // 2 - 1
    with ExitStack() as mem, M.scope():
        raw = M.low("b_raw", [P, 2, KT, P])
        w_hi = M.low("b_w_hi", [P, 2, KT, P], F32R)
        w_lo = M.low("b_w_lo", [P, 2, KT, P], F32R)
        sg = M.low("b_sg", [P, 2, 2, N_TOK])
        ps = psum(nc, mem, "b_ps", [P, NCH, 2, 512])
        w_in, g_in = [sem("w_in0"), sem("w_in1")], [sem("g_in0"), sem("g_in1")]
        hi_ok, lo_ok, mm_ok, ya_ok, yb_ok, y_ok, yh_ok, yl_ok = (
            sem(n) for n in ("hi_ok", "lo_ok", "mm_ok", "ya_ok", "yb_ok", "y_ok", "yh_ok", "yl_ok"))
        wa = io["w_branch_attn"][0].rearrange("(k p) n -> p k n", p=P)
        wb = io["w_branch_mlstm"][0].rearrange("(k p) n -> p k n", p=P)
        ga, gb = (scratch.ap()[N_PLAIN + HM + u * KT:N_PLAIN + HM + (u + 1) * KT].rearrange("k p n -> p k n")
                  for u in range(2))

        def run(loop, before, unit):
            before(0, 0)
            for n0 in range(2):
                before(0, n0 + 1)
                unit(0, n0)
            with loop(0, BODIES - 1) as i:
                for n0 in (2, 3):
                    before(i, n0 + 1)
                    unit(i, n0)
            before(0, KT - 1)
            unit(0, KT - 2)
            unit(0, KT - 1)

        with nc.Block() as block:
            @block.sync
            def _(sp):
                def load(i, n0):
                    cols, tile = bass.ds((i * 2 + n0) * P, P), bass.ds(i * 2 + n0, 1)
                    if n0 >= 2:
                        sp.wait_ge(lo_ok, i * 2 + (n0 - 1))
                    sp.dma_start(raw[:, n0 % 2, 0:4], wa[:, :, cols]).then_inc(w_in[n0 % 2], 16)
                    sp.dma_start(raw[:, n0 % 2, 4:8], wb[:, :, cols]).then_inc(w_in[n0 % 2], 16)
                    if n0 >= 2:
                        sp.wait_ge(yb_ok, i * (2 * NCH) + NCH * (n0 - 1))
                    sp.dma_start(sg[:, n0 % 2, 0:1], ga[:, tile, :]).then_inc(g_in[n0 % 2], 16)
                    sp.dma_start(sg[:, n0 % 2, 1:2], gb[:, tile, :]).then_inc(g_in[n0 % 2], 16)
                run(nc.sync.Fori, load, lambda i, n0: None)

            @block.scalar
            def _(act):
                def split_hi(i, n0):
                    act.wait_ge(w_in[n0 % 2], i * 32 + 32 * (n0 // 2 + 1))
                    if n0 >= 2:
                        act.wait_ge(mm_ok, i * (2 * NCH) + NCH * (n0 - 1))
                    nc.scalar.activation(w_hi[:, n0 % 2], raw[:, n0 % 2], ACT.Copy).then_inc(hi_ok, 1)

                def unit(i, n0):
                    for c in range(NCH):
                        q0 = NCH * n0 + c
                        act.wait_ge(y_ok, i * (2 * NCH) + (q0 + 1))
                        nc.scalar.activation(y_hi[:, bass.ds(i * 2 + n0, 1), c * CH:(c + 1) * CH],
                                             ya[:, q0 % 2:q0 % 2 + 1], ACT.Copy).then_inc(yh_ok, 1)
                run(nc.scalar.Fori, split_hi, unit)

            @block.gpsimd
            def _(pool):
                def split_lo(i, n0):
                    pool.wait_ge(hi_ok, i * 2 + (n0 + 1))
                    nc.gpsimd.tensor_tensor(w_lo[:, n0 % 2], raw[:, n0 % 2], w_hi[:, n0 % 2].bitcast(F32),
                                            ALU.subtract).then_inc(lo_ok, 1)

                def unit(i, n0):
                    for c in range(NCH):
                        q0 = NCH * n0 + c
                        pool.wait_ge(yh_ok, i * (2 * NCH) + (q0 + 1))
                        at = (slice(None), bass.ds(i * 2 + n0, 1), slice(c * CH, (c + 1) * CH))
                        nc.gpsimd.tensor_tensor(y_lo[at], ya[:, q0 % 2:q0 % 2 + 1], y_hi[at].bitcast(F32),
                                                ALU.subtract).then_inc(yl_ok, 1)
                run(nc.gpsimd.Fori, split_lo, unit)

            @block.vector
            def _(dve):
                def unit(i, n0):
                    dve.wait_ge(g_in[n0 % 2], i * 32 + 32 * (n0 // 2 + 1))
                    for c in range(NCH):
                        q0 = NCH * n0 + c
                        q = i * (2 * NCH) + q0
                        tok = slice(c * CH, (c + 1) * CH)
                        dve.wait_ge(mm_ok, q + 1)
                        if q0 >= 2:
                            dve.wait_ge(yl_ok, q - 1)
                        nc.vector.tensor_tensor(ya[:, q0 % 2], ps[:, c, 0, 0:CH], sg[:, n0 % 2, 0, tok],
                                                ALU.mult).then_inc(ya_ok, 1)
                        nc.vector.tensor_tensor(yb[:, q0 % 2], ps[:, c, 1, 0:CH], sg[:, n0 % 2, 1, tok],
                                                ALU.mult).then_inc(yb_ok, 1)
                        dve.wait_ge(ya_ok, q + 1)
                        dve.wait_ge(yb_ok, q + 1)
                        nc.vector.tensor_tensor(ya[:, q0 % 2], ya[:, q0 % 2], yb[:, q0 % 2], ALU.add).then_inc(y_ok, 1)
                run(nc.vector.Fori, lambda i, n0: None, unit)

            @block.tensor
            def _(pe):
                def unit(i, n0):
                    pe.wait_ge(lo_ok, i * 2 + (n0 + 1))
                    for c in range(NCH):
                        tok = slice(c * CH, (c + 1) * CH)
                        if n0:
                            pe.wait_ge(yb_ok, i * (2 * NCH) + (NCH * n0 + c - 2))
                        for u, (x_hi, x_lo) in enumerate(((o_hi, o_lo), (h_hi, h_lo))):
                            for k in range(4):
                                last = product3(nc, ps[:, c, u, 0:CH], w_hi[:, n0 % 2, 4 * u + k],
                                                w_lo[:, n0 % 2, 4 * u + k], x_hi[:, k, tok], x_lo[:, k, tok],
                                                k == 0, k == 3)
                        last.then_inc(mm_ok, 1)
                run(nc.tensor.Fori, lambda i, n0: None, unit)


def output_projection(nc, ctx, M, K, io, y, xT, x_dram):
    sem = lambda n: ctx.enter_context(nc.semaphore("o_" + n))
    y_hi, y_lo = y
    with ExitStack() as mem, M.scope():
        raw = M.low("o_raw", [P, 2, KT, P])
        w_hi = M.low("o_w_hi", [P, 2, KT, P], F32R)
        w_lo = M.low("o_w_lo", [P, 2, KT, P], F32R)
        ps = psum(nc, mem, "o_ps", [P, NCH, 512])
        w_in, x_in = [sem("w_in0"), sem("w_in1")], sem("x_in")
        hi_ok, lo_ok, mm_ok, x_ok = (sem(n) for n in ("hi_ok", "lo_ok", "mm_ok", "x_ok"))
        w_v = io["w_out"][0].rearrange("(k p) n -> p k n", p=P)

        def run(loop, before, unit):
            before(0, 0)
            for n0 in range(2):
                before(0, n0 + 1)
                unit(0, n0)
            with loop(0, KT // 2 - 2) as i:
                for n0 in (2, 3):
                    before(i, n0 + 1)
                    unit(i, n0)
            before(0, KT - 1)
            unit(0, KT - 2)
            unit(0, KT - 1)

        with nc.Block() as block:
            @block.sync
            def _(sp):
                def load(i, n0):
                    if n0 >= 2:
                        sp.wait_ge(lo_ok, i * 2 + (n0 - 1))
                    sp.dma_start(raw[:, n0 % 2], w_v[:, :, bass.ds((i * 2 + n0) * P, P)]).then_inc(w_in[n0 % 2], 16)
                    if n0 == 0:
                        sp.dma_start(xT[:], x_dram.ap()).then_inc(x_in, 16)
                run(nc.sync.Fori, load, lambda i, n0: None)

            @block.scalar
            def _(act):
                def split_hi(i, n0):
                    act.wait_ge(w_in[n0 % 2], i * 16 + 16 * (n0 // 2 + 1))
                    if n0 >= 2:
                        act.wait_ge(mm_ok, i * (2 * NCH) + NCH * (n0 - 1))
                    nc.scalar.activation(w_hi[:, n0 % 2], raw[:, n0 % 2], ACT.Copy).then_inc(hi_ok, 1)
                run(nc.scalar.Fori, split_hi, lambda i, n0: None)

            @block.gpsimd
            def _(pool):
                def split_lo(i, n0):
                    pool.wait_ge(hi_ok, i * 2 + (n0 + 1))
                    nc.gpsimd.tensor_tensor(w_lo[:, n0 % 2], raw[:, n0 % 2], w_hi[:, n0 % 2].bitcast(F32),
                                            ALU.subtract).then_inc(lo_ok, 1)
                run(nc.gpsimd.Fori, split_lo, lambda i, n0: None)

            @block.vector
            def _(dve):
                dve.wait_ge(x_in, 16)

                def unit(i, n0):
                    for c in range(NCH):
                        dve.wait_ge(mm_ok, i * (2 * NCH) + (NCH * n0 + c + 1))
                        x = xT[:, bass.ds(i * 2 + n0, 1), c * CH:(c + 1) * CH]
                        nc.vector.tensor_tensor(x, ps[:, c:c + 1, 0:CH], x, ALU.add).then_inc(x_ok, 1)
                run(nc.vector.Fori, lambda i, n0: None, unit)

            @block.tensor
            def _(pe):
                def unit(i, n0):
                    pe.wait_ge(lo_ok, i * 2 + (n0 + 1))
                    for c in range(NCH):
                        tok = slice(c * CH, (c + 1) * CH)
                        if n0:
                            pe.wait_ge(x_ok, i * (2 * NCH) + (NCH * n0 + c - 2))
                        for k in range(KT):
                            last = product3(nc, ps[:, c, 0:CH], w_hi[:, n0 % 2, k], w_lo[:, n0 % 2, k],
                                            y_hi[:, k, tok], y_lo[:, k, tok], k == 0, k == KT - 1)
                        last.then_inc(mm_ok, 1)
                run(nc.tensor.Fori, lambda i, n0: None, unit)


def final_norm(nc, ctx, M, K, io, out, xT):
    sem = lambda n: ctx.enter_context(nc.semaphore("z_" + n))
    with ExitStack() as mem, M.scope():
        gain = M.low("z_gain", [P, D_MODEL])
        sq = M.low("z_sq", [P, D_MODEL])
        res = M.low("z_res", [P, 2, D_MODEL])
        ps = psum(nc, mem, "z_ps", [P, 4, D_MODEL])
        ld, tp, ss, s1, s2, s3, r_ok = (sem(n) for n in ("ld", "tp", "ss", "s1", "s2", "s3", "r_ok"))
        st = [sem("st0"), sem("st1")]
        with nc.Block() as block:
            @block.sync
            def _(sp):
                sp.dma_start(gain[:], io["norm_final"].rearrange("(a n) -> a n", a=1).to_broadcast([P, D_MODEL]))\
                    .then_inc(ld, 16)
                for t in range(NT):
                    sp.wait_ge(r_ok, t + 1)
                    dst = out["y_prompt"][0, t * P:(t + 1) * P, :] if t < NTP else \
                        out["y_sample"].rearrange("b q d -> (b q) d")
                    sp.dma_start(dst, res[:, t % 2]).then_inc(st[t % 2], 16)
                sp.wait_ge(st[0], 16 * ((NT + 1) // 2))
                sp.wait_ge(st[1], 16 * (NT // 2))

            @block.tensor
            def _(pe):
                for t in range(NT):
                    if t >= 4:
                        pe.wait_ge(r_ok, t - 3)
                    for k in range(KT):
                        last = nc.tensor.transpose(ps[:, t % 4, k * P:(k + 1) * P], xT[:, k, t * P:(t + 1) * P],
                                                   K["ident"][:])
                    last.then_inc(tp, 1)

            @block.scalar
            def _(act):
                def squares(t):
                    act.wait_ge(tp, t + 1)
                    if t:
                        act.wait_ge(ss, t)
                    nc.scalar.activation(sq[:], ps[:, t % 4], ACT.Square, accum_out=K["ssq"][:, t:t + 1])\
                        .then_inc(ss, 1)
                squares(0)
                for t in range(NT):
                    if t + 1 < NT:
                        squares(t + 1)
                    act.wait_ge(s2, t + 1)
                    nc.scalar.activation(K["st3"][:, t:t + 1], K["st2"][:, t:t + 1], ACT.Sqrt).then_inc(s3, 1)

            @block.vector
            def _(dve):
                def scale(t):
                    c = slice(t, t + 1)
                    dve.wait_ge(ss, t + 1)
                    nc.vector.tensor_scalar(K["st1"][:, c], K["ssq"][:, c], 1.0 / D_MODEL, EPS, ALU.mult, ALU.add)\
                        .then_inc(s1, 1)
                    dve.wait_ge(s1, t + 1)
                    nc.vector.reciprocal(K["st2"][:, c], K["st1"][:, c]).then_inc(s2, 1)
                scale(0)
                dve.wait_ge(ld, 16)
                for t in range(NT):
                    if t + 1 < NT:
                        scale(t + 1)
                    dve.wait_ge(s3, t + 1)
                    if t >= 2:
                        dve.wait_ge(st[t % 2], 16 * (t // 2))
                    nc.vector.scalar_tensor_tensor(res[:, t % 2], ps[:, t % 4], K["st3"][:, t:t + 1], gain[:],
                                                   ALU.mult, ALU.mult).then_inc(r_ok, 1)


def trunk(nc, io, out):
    ctx = ExitStack()
    M = Sbuf(nc)
    x_dram = nc.dram_tensor("x_dram", [P, KT, N_TOK], F32, kind="Internal")
    scratch = nc.dram_tensor("p_dram", [N_PLAIN + N_SIG + 1, P, N_TOK], F32, kind="Internal")
    with ctx:
        K = {n: M.low(n, [P, NT]) for n in ("ssq", "st1", "st2", "st3")}
        K["ident"] = M.low("ident_sb", [P, P])
        K["ones"] = M.low("ones_sb", [P, P])
        K["gains"] = M.low("gains", [P, 3 * KT + HM])
        for n, k in enumerate(("ffn1", "mix", "ffn2")):
            K["g_" + k] = K["gains"][:, n * KT:(n + 1) * KT]
        K["g_mlstm"] = K["gains"][:, 3 * KT:3 * KT + HM]
        def phase(f, *args):
            with ExitStack() as own:
                used = []
                f(nc, Scope(own, used), M, K, *args)
                used.sort()
                with nc.Block() as block:
                    @block.gpsimd
                    def _(pool):
                        at = 0
                        while at < len(used):
                            end = at + 1
                            while end < len(used) and used[end] == used[end - 1] + 1:
                                end += 1
                            pool.sem_clear(range(used[at], used[end - 1] + 1))
                            at = end

        high_end = M.high_end
        xn_hi = M.high("xn_hi", [P, KT, N_TOK], F32R)
        xn_lo = M.high("xn_lo", [P, KT, N_TOK], F32R)
        low_end = M.low_end
        xT = M.low("xT", [P, KT, N_TOK])
        phase(load_residual, io, xT)
        phase(ffn, io["w_ffn1_up"], io["w_ffn1_down"], K["g_ffn1"], xT, xn_hi, xn_lo, "f1")
        M.low_end = aq_at = low_end
        aq = M.low("aq", [P, 4, N_TOK])
        kvT = M.low("kvT", [P, N_TOK])
        DM = M.low("DM", [P, SCORE_COLS])
        phase(project, io, out, xT, x_dram, xn_hi, xn_lo, aq, kvT, DM, scratch)
        M.high_end = high_end
        E = {"aq": aq}
        E["kvtok"] = M.low("kvtok", [P, NT, P])
        low_end = M.low_end
        for n, shape in dict(mqk=[P, 4, N_TOK], vaug=[P, NT, HM, DV + 1], ktm=[P, NT, HM * DH],
                             mqd=[P, HM, P], Cn=[P, HM, DEC_BATCH, DH], CT=[P, HM, 4, DV + 1],
                             U=[HM, N_TOK], V=[HM, N_TOK], head_sel=[HM, HM, P], causal_p=[P, P],
                             causal_s=[P, P], batch_mask=[P, DEC_BATCH],
                             decB=[P, HM, NTP + DEC_BATCH], decP=[P, 2, NTP]).items():
            E[n] = M.low(n + "_sb", shape)
        E["Gt"], E["pair_mask"] = M.high("Gt", [P, NT, 4, HM]), M.high("pair_mask_e", [P, 4, P])
        phase(prepare_mix, io, out, kvT, E, scratch)
        for n, shape in dict(KTa=[P, 4, LS], kd=[P, N_TOK], aqr=[P, 4, P],
                             vn=[DEC_SEQ, DEC_BATCH, DH]).items():
            E[n] = M.high(n, shape)
        att_end = M.high_end
        num = M.high("num", [P, NT, HM, DV + 1])
        phase(mlstm, io, out, kvT, E, num)
        M.low_end = low_end
        h = M.low("h_hi", [P, HM, N_TOK], F32R), M.low("h_lo", [P, HM, N_TOK], F32R)
        phase(mlstm_output, E, num, *h, scratch)
        M.high_end = att_end
        o = M.low("o_hi", [P, HM, N_TOK], F32R), M.low("o_lo", [P, HM, N_TOK], F32R)
        phase(attention, io, E, DM, *o)
        M.high_end = high_end
        y = M.high("y_hi", [P, KT, N_TOK], F32R), M.high("y_lo", [P, KT, N_TOK], F32R)
        ya, yb = M.low("b_ya", [P, 2, CH]), M.low("b_yb", [P, 2, CH])
        M.low_end = aq_at
        mid_end = M.high_end
        M.high_end = low_end
        phase(mix_out, io, o, h, y, ya, yb, scratch)
        M.high_end = mid_end
        xT = M.low("xT_2", [P, KT, N_TOK])
        phase(output_projection, io, y, xT, x_dram)
        M.high_end = high_end
        xn = M.high("xn2_hi", [P, KT, N_TOK], F32R), M.high("xn2_lo", [P, KT, N_TOK], F32R)
        phase(ffn, io["w_ffn2_up"], io["w_ffn2_down"], K["g_ffn2"], xT, *xn, "f2")
        phase(final_norm, io, out, xT)


_INS = ["x_prompt", "x_sample", "cache_attn_k", "cache_attn_v", "cache_idx_k", "state_mlstm_C", "state_mlstm_n",
        "state_mlstm_m", "norm_ffn1", "w_ffn1_up", "w_ffn1_down", "norm_mix", "w_in", "b_mlstm_gates",
        "norm_mlstm_heads", "w_branch_attn", "w_branch_mlstm", "w_out", "norm_ffn2", "w_ffn2_up", "w_ffn2_down",
        "norm_final"]
_OUTS = {
    "y_prompt": (1, SEQ, D_MODEL), "y_sample": (DEC_BATCH, DEC_SEQ, D_MODEL),
    "new_k_prompt": (1, 1, SEQ, DH), "new_v_prompt": (1, 1, SEQ, DH), "new_idxk_prompt": (1, 1, SEQ, DH),
    "new_C_prompt": (1, 1, HM, DV, DH), "new_n_prompt": (1, 1, HM, DH), "new_m_prompt": (1, 1, HM),
    "new_k_sample": (1, DEC_BATCH, DEC_SEQ, DH), "new_v_sample": (1, DEC_BATCH, DEC_SEQ, DH),
    "new_idxk_sample": (1, DEC_BATCH, DEC_SEQ, DH), "new_C_sample": (1, DEC_BATCH, HM, DV, DH),
    "new_n_sample": (1, DEC_BATCH, HM, DH), "new_m_sample": (1, DEC_BATCH, HM),
}


def kernel(**inputs):
    import concourse.bacc as bacc
    from concourse.bass_utils import run_bass_kernel_spmd

    nc = bacc.Bacc("TRN2", target_bir_lowering=False, num_devices=1)
    arrays, io, out = {}, {}, {}
    given = {n: np.ascontiguousarray(inputs[n]) for n in _INS}
    for name, a in {**given, **constants()}.items():
        arrays["in_" + name] = a
        io[name] = nc.dram_tensor("in_" + name, a.shape, F32, kind="ExternalInput").ap()
    for name, shape in _OUTS.items():
        out[name] = nc.dram_tensor("out_" + name, shape, F32, kind="ExternalOutput").ap()
    trunk(nc, io, out)
    r = run_bass_kernel_spmd(nc, [arrays], core_ids=[0])
    return tuple(r.results[0]["out_" + n] for n in _OUTS)
```

```python
from contextlib import ExitStack, contextmanager

import numpy as np

import concourse.bass as bass
from concourse import mybir

F32 = mybir.dt.float32
F32R = mybir.dt.float32r
ALU = mybir.AluOpType
ACT = mybir.ActivationFunctionType
AX_X = mybir.AxisListType.X

P = 128
D_MODEL = 1024
KT = D_MODEL // P
SEQ = 1024
DEC_BATCH = 8
DEC_SEQ = 16
PAST = 512
N_TOK = SEQ + DEC_BATCH * DEC_SEQ
NT = N_TOK // P
NTP = SEQ // P
CH = 384
NCH = N_TOK // CH
CHUNK = 64
HA = 8
DH = 64
NI = 4
TOPK = 256
TOPK_S = (PAST + DEC_SEQ) // 4
HM = 4
DV = 128
D_FF = 2816
FT = D_FF // P
FG = 2
NG = FT // FG
EPS = 1e-6
IDX_SCALE = (NI * DH) ** -0.5
QK_SCALE = DH ** -0.5
LS = PAST + DEC_SEQ
SLOPE = [2.0 ** (-8.0 * (h + 1) / HA) / QK_SCALE for h in range(HA)]
BIG = 1e30
TAKEN = -3.4e38
BLOCKED = -3.0e38
FIRST_SEL = TOPK // P
SCORE_OFF = {}
_at = 0
for _b in range(NTP):
    SCORE_OFF[_b] = _at
    _at += P * (_b + 1)
SCORE_OFF[NTP] = _at
SCORE_COLS = _at + LS

C_AQ, C_AK, C_IQ, C_IK, C_MQ, C_MI, C_MO = 0, 512, 640, 896, 964, 1988, 1996
N_MIX = 8
N_SIG = 20


def constants():
    c = {}
    c["ident"] = np.eye(P, dtype=np.float32)
    p, x = np.arange(P)[:, None], np.arange(SEQ)[None, :]
    c["dist_p"] = np.abs(p + SEQ - P - x).astype(np.float32)
    c["dist_s"] = np.abs(PAST + p % DEC_SEQ - np.arange(LS)[None, :]).astype(np.float32)
    c["slope"] = -np.repeat(np.array(SLOPE, np.float32), DEC_SEQ)[:, None]
    b_of = np.arange(P) // DEC_SEQ
    par = (np.arange(P) // 64)[:, None, None]
    c["pair_mask"] = (b_of[None, None, :] == 2 * np.arange(4)[None, :, None] + par).astype(np.float32)
    c["batch_mask"] = (b_of[:, None] == np.arange(DEC_BATCH)[None, :]).astype(np.float32)
    s, t = np.arange(P)[:, None], np.arange(P)[None, :]
    c["causal_p"] = np.where(s <= t, 0, -BIG).astype(np.float32)
    c["causal_s"] = np.where((s <= t) & (s // DEC_SEQ == t // DEC_SEQ), 0, -BIG).astype(np.float32)
    sel = np.zeros((HM, HM, P), np.float32)
    for h in range(HM):
        sel[h, h] = 1
    c["head_sel"] = sel
    keep = np.ones((HM, N_TOK), np.float32)
    keep[:, 0:SEQ:P] = 0
    keep[:, SEQ::DEC_SEQ] = 0
    c["keep"] = keep
    return c


class Scope:

    def __init__(self, stack, numbers):
        self.stack, self.numbers = stack, numbers

    def enter_context(self, guard):
        got = self.stack.enter_context(guard)
        self.numbers.append(got.num)
        return got


class Sbuf:

    def __init__(self, nc):
        self.nc, self.gap = nc, (0, 0)
        self.low_end, self.high_end = (nc.sbuf_base + 63) // 64 * 64, nc.sbuf_usable_end // 64 * 64

    def low(self, name, shape, dt=F32):
        size = (int(np.prod(shape[1:])) * 4 + 63) // 64 * 64
        if self.gap[0] + size <= self.gap[1]:
            self.gap = (self.gap[0] + size, self.gap[1])
            return self.nc.alloc_sbuf_tensor_at(name, shape, dt, offset=self.gap[0] - size)
        at = self.low_end
        self.low_end += size
        assert self.low_end <= self.high_end, (name, self.low_end, self.high_end)
        return self.nc.alloc_sbuf_tensor_at(name, shape, dt, offset=at)

    def high(self, name, shape, dt=F32):
        self.high_end -= (int(np.prod(shape[1:])) * 4 + 63) // 64 * 64
        assert self.low_end <= self.high_end, (name, self.low_end, self.high_end)
        return self.nc.alloc_sbuf_tensor_at(name, shape, dt, offset=self.high_end)

    def at(self, name, shape, offset, dt=F32):
        return self.nc.alloc_sbuf_tensor_at(name, shape, dt, offset=offset)

    @contextmanager
    def scope(self):
        ends = self.low_end, self.high_end, self.gap
        yield
        self.low_end, self.high_end, self.gap = ends


def psum(nc, ctx, name, shape, dt=F32):
    return ctx.enter_context(nc.psum_tensor(name, shape, dt))


def load_residual(nc, ctx, M, K, io, xT):
    sem = lambda n: ctx.enter_context(nc.semaphore("a_" + n))
    NG_ROWS = 3 * KT + HM
    with ExitStack() as mem, M.scope():
        xt = M.low("x_tok", [P, NT, D_MODEL])
        grow = M.low("gain_rows", [P, P])
        sq = M.low("x_sq", [P, D_MODEL])
        pg = psum(nc, mem, "gain_tp", [P, P])
        pt = psum(nc, mem, "x_tp", [P, 6, 512])
        x_in = [sem(f"x_in{t}") for t in range(NT)]
        tp, tpg, ev, ss_ok, c_in, ones_ok = (sem(n) for n in ("tp", "tpg", "ev", "ss_ok", "c_in", "ones"))

        with nc.Block() as block:
            @block.sync
            def _(sp):
                sp.dma_start(K["ident"][:], io["ident"]).then_inc(c_in, 16)
                for t in range(NT):
                    src = io["x_prompt"][0, t * P:(t + 1) * P, :] if t < NTP else \
                        io["x_sample"].rearrange("b q d -> (b q) d")
                    sp.dma_start(xt[:, t, :], src).then_inc(x_in[t], 16)
                for n, k in enumerate(("ffn1", "mix", "ffn2")):
                    sp.dma_start(grow[n * KT:(n + 1) * KT, :],
                                 io["norm_" + k][0].rearrange("(k p) -> k p", p=P)).then_inc(c_in, 16)
                sp.dma_start(grow[3 * KT:3 * KT + HM, :],
                             io["norm_mlstm_heads"][0].rearrange("(k p) -> k p", p=P)).then_inc(c_in, 16)

            @block.gpsimd
            def _(pool):
                nc.gpsimd.memset(K["ones"][:], 1.0).then_inc(ones_ok, 1)
                pool.wait_ge(ones_ok, 1)

            @block.tensor
            def _(pe):
                for n in range(2 * NT):
                    t, half = n // 2, n % 2
                    if n == 0:
                        pe.wait_ge(c_in, 16)
                    if half == 0:
                        pe.wait_ge(x_in[t], 16)
                    if n >= 6:
                        pe.wait_ge(ev, n - 5)
                    for j in range(4):
                        last = nc.tensor.transpose(pt[:, n % 6, j * P:(j + 1) * P],
                                                   xt[:, t, (4 * half + j) * P:(4 * half + j + 1) * P],
                                                   K["ident"][:])
                    last.then_inc(tp, 1)
                pe.wait_ge(c_in, 80)
                nc.tensor.transpose(pg[:, 0:NG_ROWS], grow[0:NG_ROWS, :],
                                    K["ident"][0:NG_ROWS, 0:NG_ROWS]).then_inc(tpg, 1)

            @block.vector
            def _(dve):
                for n in range(2 * NT):
                    t, half = divmod(n, 2)
                    dve.wait_ge(tp, n + 1)
                    nc.vector.tensor_copy(xT[:, 4 * half:4 * half + 4, t * P:(t + 1) * P],
                                          pt[:, n % 6, :].rearrange("p (j t) -> p j t", j=4)).then_inc(ev, 1)
                dve.wait_ge(tpg, 1)
                nc.vector.tensor_copy(K["gains"][:, 0:NG_ROWS], pg[:, 0:NG_ROWS]).then_inc(ev, 1)

            @block.scalar
            def _(act):
                for t in range(NT):
                    act.wait_ge(x_in[t], 16)
                    if t:
                        act.wait_ge(ss_ok, t)
                    nc.scalar.activation(sq[:], xt[:, t, :], ACT.Square,
                                         accum_out=K["ssq"][:, t:t + 1]).then_inc(ss_ok, 1)


class Squares:

    def __init__(self, nc, sem, xT, acc, sq):
        self.nc, self.xT, self.acc, self.sq = nc, xT, acc, sq
        self.sq_ok, self.sum_ok = sem("sq_ok"), sem("sum_ok")

    def square(self, act, n):
        c, k = divmod(n, KT)
        m = (KT - 1) * c + k - 1
        tok = slice(c * CH, (c + 1) * CH)
        if k and m >= 2:
            act.wait_ge(self.sum_ok, m - 1)
        self.nc.scalar.activation(self.sq[:, m % 2, :] if k else self.acc[:, tok], self.xT[:, k, tok],
                                  ACT.Square).then_inc(self.sq_ok, 1)

    def add(self, dve, n):
        c, k = divmod(n, KT)
        m = (KT - 1) * c + k - 1
        a = self.acc[:, c * CH:(c + 1) * CH]
        if k:
            dve.wait_ge(self.sq_ok, n + 1)
            if m:
                dve.wait_ge(self.sum_ok, m)
            self.nc.vector.tensor_tensor(a, a, self.sq[:, m % 2, :], ALU.add).then_inc(self.sum_ok, 1)


class Norm:
    ON_VECTOR = (2, 5)

    def __init__(self, nc, sem, K, xT, gain, xn_hi, xn_lo, diag, full, ps, ps_sums):
        self.nc, self.K, self.xT, self.gain, self.xn_hi, self.xn_lo = nc, K, xT, gain, xn_hi, xn_lo
        self.diag, self.full, self.ps, self.ps_sums, self.slots = diag, full, ps, ps_sums, full.shape[1]
        (self.sums_ok, self.mean_ok, self.inv_ok, self.root_ok, self.diag_ok, self.spread_ok, self.full_ok,
         self.hi_ok, self.lo_v, self.lo_g) = (
             sem("n_" + n) for n in ("sums", "mean", "inv", "root", "diag", "spread", "full", "hi", "lo_v", "lo_g"))

    @staticmethod
    def tok(c):
        return slice(c * CH, (c + 1) * CH)

    def lo_before(self, eng, n):
        on_v = len(self.ON_VECTOR) * (n // KT) + sum(k < n % KT for k in self.ON_VECTOR)
        if on_v:
            eng.wait_ge(self.lo_v, on_v)
        if n - on_v:
            eng.wait_ge(self.lo_g, n - on_v)

    def inverse(self, dve):
        K, sums = self.K, self.K["ssq"]
        if self.ps_sums is not None:
            dve.wait_ge(self.sums_ok, 1)
            sums = self.ps_sums
        self.nc.vector.tensor_scalar(K["mean"], sums, 1.0 / D_MODEL, EPS, ALU.mult, ALU.add).then_inc(self.mean_ok, 1)
        dve.wait_ge(self.mean_ok, 1)
        self.nc.vector.reciprocal(K["inv"], K["mean"]).then_inc(self.inv_ok, 1)

    def diagonals(self, dve, c):
        for t in range(3 * c, 3 * c + 3):
            self.nc.vector.tensor_scalar(self.diag[:, t * P:(t + 1) * P], self.K["ident"][:],
                                         self.K["root"][:, t:t + 1], None, ALU.mult).then_inc(self.diag_ok, 1)

    def apply(self, dve, c):
        dve.wait_ge(self.spread_ok, c + 1)
        for k in range(KT):
            n = KT * c + k
            if n >= self.slots:
                self.lo_before(dve, n - self.slots + 1)
            self.nc.vector.scalar_tensor_tensor(self.full[:, n % self.slots, :], self.xT[:, k, self.tok(c)],
                                                self.gain[:, k:k + 1], self.ps[c],
                                                ALU.mult, ALU.mult).then_inc(self.full_ok, 1)
            if k - 1 in self.ON_VECTOR:
                self.lo(self.nc.vector, dve, c, k - 1, self.lo_v)

    def lo(self, engine, eng, c, k, done):
        n = KT * c + k
        eng.wait_ge(self.hi_ok, n + 1)
        engine.tensor_tensor(self.xn_lo[:, k, self.tok(c)], self.full[:, n % self.slots, :],
                             self.xn_hi[:, k, self.tok(c)].bitcast(F32), ALU.subtract).then_inc(done, 1)

    def on_vector(self, dve):
        self.inverse(dve)
        dve.wait_ge(self.root_ok, 1)
        self.diagonals(dve, 0)
        self.diagonals(dve, 1)
        self.apply(dve, 0)
        self.diagonals(dve, 2)
        self.apply(dve, 1)
        self.apply(dve, 2)
        self.lo_before(dve, KT * NCH)

    def root(self, act):
        act.wait_ge(self.inv_ok, 1)
        self.nc.scalar.activation(self.K["root"], self.K["inv"], ACT.Sqrt).then_inc(self.root_ok, 1)

    def on_scalar(self, act):
        for n in range(KT * NCH):
            c, k = divmod(n, KT)
            act.wait_ge(self.full_ok, n + 1)
            self.nc.scalar.activation(self.xn_hi[:, k, self.tok(c)], self.full[:, n % self.slots, :], ACT.Copy)\
                .then_inc(self.hi_ok, 1)

    def on_gpsimd(self, pool):
        for c in range(NCH):
            for k in range(KT):
                if k not in self.ON_VECTOR:
                    self.lo(self.nc.gpsimd, pool, c, k, self.lo_g)

    def on_tensor(self, pe, chunks):
        if self.ps_sums is not None and 0 in chunks:
            for t in range(NT):
                last = self.nc.tensor.matmul(self.ps_sums[:, t:t + 1], self.K["acc"][:, t * P:(t + 1) * P],
                                             self.K["ones"][:, 0:1], start=True, stop=True)
            last.then_inc(self.sums_ok, 1)
        for c in chunks:
            pe.wait_ge(self.diag_ok, 3 * (c + 1))
            self.nc.tensor.matmul(self.ps[c], self.K["ones"][:], self.diag[:, self.tok(c)],
                                  start=True, stop=True).then_inc(self.spread_ok, 1)


def product3(nc, out, w_hi, w_lo, x_hi, x_lo, first, final):
    nc.tensor.matmul(out, w_hi, x_lo, start=first, stop=False)
    nc.tensor.matmul(out, w_lo, x_hi, start=False, stop=False)
    return nc.tensor.matmul(out, w_hi, x_hi, start=False, stop=final)


def ffn(nc, ctx, M, K, w_up, w_down, gain, xT, xn_hi, xn_lo, tag, summed):
    sem = lambda n: ctx.enter_context(nc.semaphore(tag + n))
    PAIRS = [("up", 0), ("up", 1), ("up", 2), ("up", 3), ("down", 0), ("up", 4), ("up", 5), ("down", 1)]
    LAST = ("down", 2)
    PER = {"up": 4, "down": 2}
    BODIES = (NG - 1) // 2
    ND = KT * NCH
    with ExitStack() as mem, M.scope():
        raw = M.low(tag + "raw", [P, 2, 2, KT, P])
        w_hi = M.low(tag + "w_hi", [P, 2, 2, KT, P], F32R)
        w_lo = M.low(tag + "w_lo", [P, 2, 2, KT, P], F32R)
        h_at, h_group = M.low_end, FG * N_TOK * 4
        h_hi = M.low(tag + "h_hi", [P, 2, FG, N_TOK], F32R)
        h_lo = M.low(tag + "h_lo", [P, 2, FG, N_TOK], F32R)
        gate = M.low(tag + "gate", [P, 2, CH])
        hid = M.low(tag + "hid", [P, 2, CH])
        ps_up = psum(nc, mem, tag + "ps_up", [P, 3, 2, 512])
        ps_dn = psum(nc, mem, tag + "ps_dn", [P, 2, 512])
        w_in = [sem("w_in0"), sem("w_in1")]
        hi_ok, lo_ok = sem("hi_ok"), sem("lo_ok")
        up_ok, gate_ok, hid_ok = sem("up_ok"), sem("gate_ok"), sem("hid_ok")
        hhi_ok, hlo_ok = sem("hhi_ok"), sem("hlo_ok")
        dn_ok, dn_ev = sem("dn_ok"), sem("dn_ev")
        diag = M.at(tag + "diag", [P, N_TOK], h_at + h_group)
        full = M.at(tag + "full", [P, 4, CH], h_at + 3 * h_group)
        norm = Norm(nc, sem, K, xT, gain, xn_hi, xn_lo, diag, full, [ps_up[:, c, 1, 0:CH] for c in range(NCH)],
                    None if summed else ps_dn[:, 0, 0:NT])
        squares = Squares(nc, sem, xT, K["acc"], gate)

        up_v = w_up[0].rearrange("(k p) n -> p k n", p=P)
        dn_v = w_down[0].rearrange("(k p) n -> p k n", p=P)

        def wait_multiplied(eng, i, n0):
            kind, m = PAIRS[n0]
            if n0 == 1:
                eng.wait_ge(dn_ok, i * (ND * 2))
            if kind == "up":
                eng.wait_ge(up_ok, i * (NCH * 4) + NCH * (m + 1))
            else:
                eng.wait_ge(dn_ok, i * (ND * 2) + ND * (m + 1))

        def load(sp, i, n0, kind, m):
            if n0 >= 2:
                sp.wait_ge(lo_ok, i * 6 + (n0 - 1))
            m = i * PER[kind] + m
            if kind == "up":
                for u in range(2):
                    sp.dma_start(raw[:, n0 % 2, u], up_v[:, :, bass.ds(m * P + u * D_FF, P)])\
                        .then_inc(w_in[n0 % 2], 16)
            else:
                sp.dma_start(raw[:, n0 % 2].rearrange("p u k n -> p u (k n)"), dn_v[:, bass.ds(m * FG, FG), :])\
                    .then_inc(w_in[n0 % 2], 32)

        def slot(t, n0):
            return t[:, n0 % 2].rearrange("p u k n -> p (u k n)")

        def split_hi(act, i, n0):
            act.wait_ge(w_in[n0 % 2], i * 96 + 32 * (n0 // 2 + 1))
            if n0 >= 2:
                wait_multiplied(act, i, n0 - 2)
            nc.scalar.activation(slot(w_hi, n0), slot(raw, n0), ACT.Copy).then_inc(hi_ok, 1)

        def split_lo(pool, i, n0):
            pool.wait_ge(hi_ok, i * 6 + (n0 + 1))
            nc.gpsimd.tensor_tensor(slot(w_lo, n0), slot(raw, n0), slot(w_hi, n0).bitcast(F32),
                                    ALU.subtract).then_inc(lo_ok, 1)

        def run(loop, before, pair, first=lambda: None):
            before(0, 0)
            first()
            for n0 in range(2):
                before(0, n0 + 1)
                pair(0, n0, *PAIRS[n0])
            with loop(0, BODIES) as i:
                for n0 in range(2, 8):
                    before(i, n0 + 1)
                    pair(i, n0, *PAIRS[n0])
            pair(BODIES - 1, 8, *LAST)

        with nc.Block() as block:
            @block.sync
            def _(sp):
                load(sp, 0, 0, "up", 0)
                load(sp, 0, 1, "up", 1)
                with nc.sync.Fori(0, BODIES) as i:
                    for n0 in range(2, 8):
                        load(sp, i, n0, *PAIRS[n0])
                load(sp, BODIES - 1, 8, *LAST)

            @block.scalar
            def _(act):
                def pair(i, n0, kind, m):
                    if n0 == 8:
                        for r in range(ND):
                            act.wait_ge(dn_ev, ND * (NG - 1) + r + 1)
                            squares.square(act, r)
                    if kind == "down":
                        return
                    for c in range(NCH):
                        q0 = NCH * m + c
                        q = i * (NCH * 4) + q0
                        act.wait_ge(up_ok, q + 1)
                        if q0 >= 2:
                            act.wait_ge(hid_ok, q - 1)
                        nc.scalar.activation(gate[:, q0 % 2], ps_up[:, c, 0, 0:CH], ACT.Silu).then_inc(gate_ok, 1)
                        act.wait_ge(hid_ok, q + 1)
                        nc.scalar.activation(h_hi[:, m // 2 % 2, m % 2, c * CH:(c + 1) * CH], hid[:, q0 % 2],
                                             ACT.Copy).then_inc(hhi_ok, 1)
                norm.root(act)
                run(nc.scalar.Fori, lambda i, n0: split_hi(act, i, n0), pair, lambda: norm.on_scalar(act))

            @block.gpsimd
            def _(pool):
                def pair(i, n0, kind, m):
                    if kind == "down":
                        return
                    for c in range(NCH):
                        q0 = NCH * m + c
                        pool.wait_ge(hhi_ok, i * (NCH * 4) + (q0 + 1))
                        out = slice(c * CH, (c + 1) * CH)
                        nc.gpsimd.tensor_tensor(h_lo[:, m // 2 % 2, m % 2, out], hid[:, q0 % 2],
                                                h_hi[:, m // 2 % 2, m % 2, out].bitcast(F32),
                                                ALU.subtract).then_inc(hlo_ok, 1)
                run(nc.gpsimd.Fori, lambda i, n0: split_lo(pool, i, n0), pair, lambda: norm.on_gpsimd(pool))

            @block.vector
            def _(dve):
                def pair(i, n0, kind, m):
                    if kind == "up":
                        for c in range(NCH):
                            q0 = NCH * m + c
                            q = i * (NCH * 4) + q0
                            dve.wait_ge(gate_ok, q + 1)
                            if q0 >= 2:
                                dve.wait_ge(hlo_ok, q - 1)
                            nc.vector.tensor_tensor(hid[:, q0 % 2], gate[:, q0 % 2], ps_up[:, c, 1, 0:CH],
                                                    ALU.mult).then_inc(hid_ok, 1)
                    else:
                        for r in range(ND):
                            c, k = divmod(r, KT)
                            dve.wait_ge(dn_ok, i * (ND * 2) + (ND * m + r + 1))
                            x = xT[:, k, c * CH:(c + 1) * CH]
                            nc.vector.scalar_tensor_tensor(x, ps_dn[:, r % 2, 0:CH], 0.5, x,
                                                           ALU.mult, ALU.add).then_inc(dn_ev, 1)
                            if n0 == 8 and r:
                                squares.add(dve, r - 1)
                            if r == ND - 1:
                                dve.wait_ge(dn_ev, i * (ND * 2) + ND * (m + 1))
                    if n0 == 8:
                        squares.add(dve, ND - 1)
                norm.on_vector(dve)
                run(nc.vector.Fori, lambda i, n0: None, pair)

            @block.tensor
            def _(pe):
                def pair(i, n0, kind, m):
                    pe.wait_ge(lo_ok, i * 6 + (n0 + 1))
                    s = n0 % 2
                    if kind == "up":
                        for c in range(NCH):
                            q0 = NCH * m + c
                            if n0 == 0 and c == 1:
                                norm.on_tensor(pe, (2,))
                            if q0 >= 3:
                                pe.wait_ge(hid_ok, i * (NCH * 4) + (q0 - 2))
                            tok = slice(c * CH, (c + 1) * CH)
                            for u in range(2):
                                for k in range(KT):
                                    if n0 == 0 and u == 0:
                                        norm.lo_before(pe, KT * c + k + 1)
                                    last = product3(nc, ps_up[:, c, u, 0:CH], w_hi[:, s, u, k], w_lo[:, s, u, k],
                                                    xn_hi[:, k, tok], xn_lo[:, k, tok], k == 0, k == KT - 1)
                            last.then_inc(up_ok, 1)
                    else:
                        pe.wait_ge(hlo_ok, i * (NCH * 4) + NCH * FG * (m + 1))
                        for r in range(ND):
                            c, k = divmod(r, KT)
                            if ND * m + r >= 2:
                                pe.wait_ge(dn_ev, i * (ND * 2) + (ND * m + r - 1))
                            tok = slice(c * CH, (c + 1) * CH)
                            for j in range(FG):
                                last = product3(nc, ps_dn[:, r % 2, 0:CH], w_hi[:, s, j, k], w_lo[:, s, j, k],
                                                h_hi[:, m % 2, j, tok], h_lo[:, m % 2, j, tok],
                                                j == 0, j == FG - 1)
                            last.then_inc(dn_ok, 1)
                norm.on_tensor(pe, (0, 1))
                run(nc.tensor.Fori, lambda i, n0: None, pair)


def project(nc, ctx, M, K, io, out, xT, x_dram, xn_hi, xn_lo, aq, kvT, DM, mix, aq_at, kvT_at, mix_at, scratch):
    sem = lambda n: ctx.enter_context(nc.semaphore("d_" + n))
    COLS = [C_IQ, C_IQ + P, C_IK, C_AQ, C_AQ + P, C_AQ + 2 * P, C_AQ + 3 * P, C_AK, C_MI]
    HEAD, LOOP1, MID, LOOP2, TAIL = range(9), (9, N_MIX // 2 - 1), range(15, 19), (19, N_SIG // 2 - 2), (35, 36)
    GATES, MIX, SIG = 8, 9, 17
    TILES = [7, 6, 5, 4, 3, 2, NTP]
    with ExitStack() as mem, M.scope():
        at = mix_at
        over = {}
        for n, shape in dict(iq=[P, 2, N_TOK],
                             ikw=[P, N_TOK],
                             ikd=[P, N_TOK],
                             iqd=[P, NI, P],
                             iqm=[P, NI, 4, P],
                             rel=[P, 2, SEQ]).items():
            over[n] = M.at(n, shape, at)
            at += int(np.prod(shape[1:])) * 4
        assert at <= mix_at + N_MIX * N_TOK * 4
        iq, ikw, ikd, iqd, iqm, rel = (over[n] for n in ("iq", "ikw", "ikd", "iqd", "iqm", "rel"))
        raw = M.low("d_raw", [P, 2, KT, P])
        w_hi = M.low("d_w_hi", [P, 2, KT, P], F32R)
        w_lo = M.low("d_w_lo", [P, 2, KT, P], F32R)
        KTi = M.high("KTi", [P, 4, LS])
        dist_p, dist_s = M.high("dist_p_sb", [P, SEQ]), M.high("dist_s_sb", [P, LS])
        pair_mask = M.high("pair_mask_sb", [P, 4, P])
        k_lo = M.at("d_k_lo", [P, SEQ], M.low_end, F32R)
        stage = M.low("stage", [P, 2, N_TOK])
        qs = M.at("d_qs", [P, NI, SEQ], aq_at, F32R)
        k_hi = M.at("d_k_hi", [P, SEQ], kvT_at, F32R)
        tok_ik = M.at("tok_ik", [P, NT, DH + NI], K["acc_at"])
        top8 = M.low("top8", [P, 8])
        ik_raw = iqm[:].rearrange("p h j n -> p (h j n)").rearrange(
            "p (k b d) -> p k b d", k=PAST // P, b=DEC_BATCH)
        ps = psum(nc, mem, "d_ps", [P, NCH, 512])
        ps_s = psum(nc, mem, "d_ps_s", [P, 2, 1024])
        ps_t = psum(nc, mem, "d_ps_t", [P, 4, P])
        w_in, st_out = [sem("w_in0"), sem("w_in1")], [sem("st_out0"), sem("st_out1")]
        gates_out = sem("gates_out")
        hi_ok, lo_ok, mm_ok, ev_ok = sem("hi_ok"), sem("lo_ok"), sem("mm_ok"), sem("ev_ok")
        dup, kcol, tp, tp_ev, o_out = sem("dup"), sem("kcol"), sem("tp"), sem("tp_ev"), sem("o_out")
        im_ok, sc_ok, rel_ok, acc_ok, ch = sem("im_ok"), sem("sc_ok"), sem("rel_ok"), sem("acc_ok"), sem("ch")
        ld, spilled, kt_tp, kt_ev = sem("ld"), sem("spilled"), sem("kt_tp"), sem("kt_ev")
        kh_ok, kl_ok, qh_ok, ql_ok = sem("kh_ok"), sem("kl_ok"), sem("qh_ok"), sem("ql_ok")
        w_v = io["w_in"][0].rearrange("(k p) n -> p k n", p=P)
        sc_v = scratch.ap()
        norm = Norm(nc, sem, K, xT, K["g_mix"], xn_hi, xn_lo, stage[:, 1],
                    rel[:].rearrange("p a n -> p (a n)")[:, 0:4 * CH].rearrange("p (s n) -> p s n", s=4),
                    [ps_s[:, 0, 0:CH], ps_s[:, 0, 512:512 + CH], ps_s[:, 1, 0:CH]], ps_t[:, 0, 0:NT])

        def run(loop, before, unit, scores=lambda: None, first=lambda: None):
            before(0, 0)
            first()
            for n0 in HEAD:
                before(0, n0 + 1)
                unit(0, n0)
                if n0 == 2:
                    scores()
            for (first, bodies), then in ((LOOP1, MID), (LOOP2, ())):
                with loop(0, bodies) as i:
                    for n0 in (first, first + 1):
                        before(i, n0 + 1)
                        unit(i, n0)
                for n0 in then:
                    before(0, n0 + 1)
                    unit(0, n0)
            before(0, TAIL[1])
            unit(0, TAIL[0])
            unit(0, TAIL[1])

        def query_parts(t, r):
            rows, other = slice(64 * r, 64 * r + 64), slice(64 - 64 * r, 128 - 64 * r)
            tok = slice(t * P, (t + 1) * P)
            return iq[rows, :, tok], qs[rows, r::2, tok], qs[other, r::2, tok]

        def score_dims(t):
            return (LS if t == NTP else P * (t + 1)), SCORE_OFF[t]

        with nc.Block() as block:
            @block.sync
            def _(sp):
                def load(i, n0):
                    if n0 >= 2:
                        sp.wait_ge(lo_ok, i * 2 + (n0 - 1))
                    if n0 < len(COLS):
                        src = w_v[:, :, COLS[n0]:COLS[n0] + P]
                    elif n0 < SIG:
                        src = w_v[:, :, bass.ds(i * (2 * P) + (C_MQ + (n0 - 9) * P), P)]
                    else:
                        src = w_v[:, :, bass.ds(i * (2 * P) + (C_MO + (n0 - 17) * P), P)]
                    sp.dma_start(raw[:, n0 % 2], src).then_inc(w_in[n0 % 2], 16)

                def store(i, n0):
                    if n0 != GATES and n0 < SIG:
                        return
                    sp.wait_ge(ev_ok, i * (2 * NCH) + NCH * (n0 + 1))
                    if n0 == GATES:
                        sp.dma_start(sc_v[N_SIG], stage[:, 0]).then_inc(gates_out, 16)
                        return
                    tile = i * 2 + (n0 - SIG)
                    dst = sc_v[tile] if isinstance(tile, int) else \
                        sc_v[bass.ds(tile, 1)].rearrange("a p n -> p (a n)")
                    sp.dma_start(dst, stage[:, n0 % 2]).then_inc(st_out[n0 % 2], 16)

                def copies():
                    sp.wait_ge(ev_ok, 3 * NCH)
                    for half in range(2):
                        rows = slice(64 * half, 64 * half + 64)
                        sp.dma_start(ikd[rows, :], ikw[0:DH, :]).then_inc(dup, 16)
                        for par in range(2):
                            sp.dma_start(iqd[rows, par::2, :], iq[64 * par:64 * par + 64, :, SEQ:N_TOK])\
                                .then_inc(dup, 16)
                        new = ikw[0:DH, SEQ:N_TOK].rearrange("d (j r q) -> d j r q", r=2, q=DEC_SEQ)
                        sp.dma_start(KTi[rows, :, PAST:LS], new[:, :, half, :]).then_inc(kcol, 16)
                    sp.wait_ge(tp_ev, 3)
                    sp.dma_start(out["new_idxk_prompt"][0, 0].rearrange("(t p) d -> p t d", p=P),
                                 tok_ik[:, 0:NTP, 0:DH]).then_inc(o_out, 16)
                    sp.dma_start(out["new_idxk_sample"][0].rearrange("b q d -> (b q) d"),
                                 tok_ik[:, NTP, 0:DH]).then_inc(o_out, 16)
                def first():
                    sp.dma_start(x_dram.ap(), xT[:]).then_inc(spilled, 16)
                    for b in range(DEC_BATCH):
                        sp.dma_start(ik_raw[:, :, b, :], io["cache_idx_k"][0, b].rearrange("(k p) d -> p k d", p=P))\
                            .then_inc(ld, 16)
                    for dst, n in ((dist_p, "dist_p"), (dist_s, "dist_s"), (pair_mask, "pair_mask")):
                        sp.dma_start(dst[:], io[n]).then_inc(ld, 16)
                run(nc.sync.Fori, load, store, copies, first)
                for s in range(2):
                    sp.wait_ge(st_out[s], 16 * (N_SIG // 2))
                sp.wait_ge(gates_out, 16)
                sp.wait_ge(o_out, 32)

            @block.scalar
            def _(act):
                def split_hi(i, n0):
                    act.wait_ge(w_in[n0 % 2], i * 16 + 16 * (n0 // 2 + 1))
                    if n0 >= 2:
                        act.wait_ge(mm_ok, i * (2 * NCH) + NCH * (n0 - 1))
                    nc.scalar.activation(w_hi[:, n0 % 2], raw[:, n0 % 2], ACT.Copy).then_inc(hi_ok, 1)

                def evict(i, n0):
                    if n0 == 3:
                        act.wait_ge(spilled, 16)
                    if n0 == MIX:
                        act.wait_ge(acc_ok, len(TILES) * NI)
                    if n0 == SIG:
                        act.wait_ge(gates_out, 16)
                    if n0 >= SIG + 2:
                        act.wait_ge(st_out[n0 % 2], i * 16 + 16 * ((n0 - SIG) // 2))
                    for c in range(NCH):
                        act.wait_ge(mm_ok, i * (2 * NCH) + (NCH * n0 + c + 1))
                        tok = slice(c * CH, (c + 1) * CH)
                        if n0 < 2:
                            dst = iq[:, n0, tok]
                        elif n0 == 2:
                            dst = ikw[:, tok]
                        elif n0 < 7:
                            dst = aq[:, n0 - 3, tok]
                        elif n0 == 7:
                            dst = kvT[:, tok]
                        elif MIX <= n0 < SIG:
                            dst = mix[:, bass.ds(i * 2 + (n0 - MIX), 1), tok]
                        else:
                            dst = stage[:, n0 % 2, tok]
                        src = ps[:, c:c + 1, 0:CH] if MIX <= n0 < SIG else ps[:, c, 0:CH]
                        nc.scalar.activation(dst, src, ACT.Sigmoid if n0 >= SIG else ACT.Copy)\
                            .then_inc(ev_ok, 1)

                def scores():
                    def query_hi(j):
                        if TILES[j] < NTP:
                            for r in range(2):
                                q, q_hi, _ = query_parts(TILES[j], r)
                                nc.scalar.activation(q_hi, q, ACT.Copy).then_inc(qh_ok, 1)

                    act.wait_ge(spilled, 16)
                    act.wait_ge(ev_ok, 3 * NCH)
                    query_hi(0)
                    query_hi(1)
                    act.wait_ge(dup, 16 * 6)
                    nc.scalar.activation(k_hi[:], ikd[:, 0:SEQ], ACT.Copy).then_inc(kh_ok, 1)
                    g = 0
                    for j, t in enumerate(TILES):
                        L, _ = score_dims(t)
                        if j and j + 1 < len(TILES):
                            query_hi(j + 1)
                        for h in range(NI):
                            act.wait_ge(sc_ok, g + 1)
                            if g >= 2:
                                act.wait_ge(acc_ok, g - 1)
                            nc.scalar.activation(rel[:, g % 2, 0:L], ps_s[:, g % 2, 0:L], ACT.Relu,
                                                 scale=IDX_SCALE).then_inc(rel_ok, 1)
                            g += 1
                norm.root(act)
                run(nc.scalar.Fori, split_hi, evict, scores, lambda: norm.on_scalar(act))

            @block.gpsimd
            def _(pool):
                def split_lo(i, n0):
                    pool.wait_ge(hi_ok, i * 2 + (n0 + 1))
                    nc.gpsimd.tensor_tensor(w_lo[:, n0 % 2], raw[:, n0 % 2], w_hi[:, n0 % 2].bitcast(F32),
                                            ALU.subtract).then_inc(lo_ok, 1)
                run(nc.gpsimd.Fori, split_lo, lambda i, n0: None, first=lambda: norm.on_gpsimd(pool))

            @block.tensor
            def _(pe):
                def unit(i, n0):
                    pe.wait_ge(lo_ok, i * 2 + (n0 + 1))
                    for c in range(NCH):
                        if n0 == 0 and c == 1:
                            norm.on_tensor(pe, (2,))
                        if n0:
                            pe.wait_ge(ev_ok, i * (2 * NCH) + (NCH * n0 + c - 2))
                        tok = slice(c * CH, (c + 1) * CH)
                        for k in range(KT):
                            if n0 == 0:
                                norm.lo_before(pe, KT * c + k + 1)
                            last = product3(nc, ps[:, c, 0:CH], w_hi[:, n0 % 2, k], w_lo[:, n0 % 2, k],
                                            xn_hi[:, k, tok], xn_lo[:, k, tok], k == 0, k == KT - 1)
                        last.then_inc(mm_ok, 1)

                def scores():
                    pe.wait_ge(ld, 16 * (DEC_BATCH + 3))
                    for j in range(DEC_BATCH // 2):
                        if j:
                            pe.wait_ge(kt_ev, j)
                        for k in range(PAST // P):
                            last = nc.tensor.transpose(ps_t[:, k, :],
                                                       ik_raw[:, k, 2 * j:2 * j + 2, :].rearrange("p b d -> p (b d)"),
                                                       K["ident"][:])
                        last.then_inc(kt_tp, 1)
                    pe.wait_ge(kt_ev, DEC_BATCH // 2)
                    pe.wait_ge(ev_ok, 3 * NCH)
                    for b in range(3):
                        if b:
                            pe.wait_ge(tp_ev, b)
                        for j in range(3):
                            t = 3 * b + j
                            last = nc.tensor.transpose(ps_t[:, j, :], ikw[:, t * P:(t + 1) * P], K["ident"][:])
                        last.then_inc(tp, 1)
                    pe.wait_ge(dup, 16 * 6)
                    pe.wait_ge(kl_ok, 1)
                    g = 0
                    for j, t in enumerate(TILES):
                        L, _ = score_dims(t)
                        if t < NTP:
                            pe.wait_ge(ql_ok, 2 * (j + 1))
                        if t == NTP:
                            pe.wait_ge(kcol, 32)
                            pe.wait_ge(im_ok, NI)
                        for h in range(NI):
                            if g >= 2:
                                pe.wait_ge(rel_ok, g - 1)
                            for at in range(0, L, 512):
                                w = min(512, L - at)
                                o = ps_s[:, g % 2, at:at + w]
                                if t < NTP:
                                    q = qs[:, h, t * P:(t + 1) * P]
                                    nc.tensor.matmul(o, q, k_hi[:, at:at + w], start=True, stop=False)
                                    last = nc.tensor.matmul(o, q, k_lo[:, at:at + w], start=False, stop=True)
                                else:
                                    for b in range(4):
                                        last = nc.tensor.matmul(o, iqm[:, h, b, :], KTi[:, b, at:at + w],
                                                                start=b == 0, stop=b == 3)
                            last.then_inc(sc_ok, 1)
                            g += 1
                norm.on_tensor(pe, (0, 1))
                run(nc.tensor.Fori, lambda i, n0: None, unit, scores)

            @block.vector
            def _(dve):
                norm.on_vector(dve)
                for j in range(DEC_BATCH // 2):
                    dve.wait_ge(kt_tp, j + 1)
                    nc.vector.tensor_copy(KTi[:, j, 0:PAST], ps_t[:].rearrange("p k n -> p (k n)")).then_inc(kt_ev, 1)
                dve.wait_ge(spilled, 16)
                n = 0
                for t in range(FIRST_SEL):
                    L, off = score_dims(t)
                    nc.vector.tensor_copy(DM[:, off:off + L], dist_p[:, SEQ - L:SEQ]).then_inc(ch, 1)
                    n += 1
                    dve.wait_ge(ch, n)
                    nc.vector.memset(DM[0:CHUNK, off + L - CHUNK:off + L], BIG).then_inc(ch, 1)
                    n += 1
                for b in range(3):
                    dve.wait_ge(tp, b + 1)
                    nc.vector.tensor_copy(tok_ik[:, 3 * b:3 * b + 3, :], ps_t[:, 0:3, 0:DH + NI]).then_inc(tp_ev, 1)
                def query_lo(j):
                    if TILES[j] < NTP:
                        dve.wait_ge(qh_ok, 2 * (j + 1))
                        for r in range(2):
                            q, q_hi, q_lo = query_parts(TILES[j], r)
                            nc.vector.tensor_tensor(q_lo, q, q_hi.bitcast(F32), ALU.subtract).then_inc(ql_ok, 1)

                query_lo(0)
                dve.wait_ge(kh_ok, 1)
                nc.vector.tensor_tensor(k_lo[:], ikd[:, 0:SEQ], k_hi[:].bitcast(F32), ALU.subtract).then_inc(kl_ok, 1)
                query_lo(1)
                for h in range(NI):
                    nc.vector.tensor_tensor(iqm[:, h], pair_mask[:], iqd[:, h:h + 1, :].to_broadcast([P, 4, P]),
                                            ALU.mult).then_inc(im_ok, 1)
                dve.wait_ge(tp_ev, 3)
                g = 0
                for j, t in enumerate(TILES):
                    L, off = score_dims(t)
                    S = DM[:, off:off + L]
                    if j and j + 1 < len(TILES):
                        query_lo(j + 1)
                    for h in range(NI):
                        dve.wait_ge(rel_ok, g + 1)
                        w = tok_ik[:, t, DH + h:DH + h + 1]
                        if h == 0:
                            nc.vector.tensor_scalar(S, rel[:, g % 2, 0:L], w, None, ALU.mult).then_inc(acc_ok, 1)
                        else:
                            dve.wait_ge(acc_ok, g)
                            nc.vector.scalar_tensor_tensor(S, rel[:, g % 2, 0:L], w, S, ALU.mult, ALU.add)\
                                .then_inc(acc_ok, 1)
                        g += 1
                dve.wait_ge(acc_ok, g)
                for t in TILES:
                    L, off = score_dims(t)
                    S = DM[:, off:off + L]
                    full, rest = divmod(TOPK_S if t == NTP else TOPK, 8)
                    if t < NTP:
                        nc.vector.memset(DM[0:CHUNK, off + L - CHUNK:off + L], BLOCKED).then_inc(ch, 1)
                        n += 1
                    dve.wait_ge(ch, n)
                    for _ in range(full):
                        dve.wait_ge(ch, n)
                        nc.vector.max(top8[:], S).then_inc(ch, 1)
                        dve.wait_ge(ch, n + 1)
                        nc.vector.match_replace(S, top8[:], S, TAKEN).then_inc(ch, 1)
                        n += 2
                    if rest:
                        dve.wait_ge(ch, n)
                        nc.vector.max(top8[:], S).then_inc(ch, 1)
                        dve.wait_ge(ch, n + 1)
                        nc.vector.memset(top8[:, rest:8], TAKEN).then_inc(ch, 1)
                        dve.wait_ge(ch, n + 2)
                        nc.vector.match_replace(S, top8[:], S, TAKEN).then_inc(ch, 1)
                        n += 3
                    dve.wait_ge(ch, n)
                    nc.vector.tensor_scalar(S, S, TAKEN * 0.999, BIG, ALU.is_gt, ALU.mult).then_inc(ch, 1)
                    dist = dist_s[:] if t == NTP else dist_p[:, SEQ - L:SEQ]
                    dve.wait_ge(ch, n + 1)
                    nc.vector.tensor_tensor(S, S, dist, ALU.add).then_inc(ch, 1)
                    n += 2


def prepare_mix(nc, ctx, M, K, io, out, kvT, E, scratch):
    sem = lambda n: ctx.enter_context(nc.semaphore("e_" + n))
    with ExitStack() as mem, M.scope():
        mvT = E["mix"][:, 4:8]
        nrow = M.low("n_rows", [DEC_BATCH * HM, DH])
        ri, rf = M.low("row_i", [HM, N_TOK]), M.low("row_f", [HM, N_TOK])
        t1, t2, t3 = (M.low(n, [HM, N_TOK]) for n in ("row_t1", "row_t2", "row_t3"))
        b_, m_ = M.low("row_b", [HM, N_TOK]), M.low("row_m", [HM, N_TOK])
        keep = M.low("row_keep", [HM, N_TOK])
        G4 = M.low("gate_rows", [P, N_TOK])
        bi, bf = M.low("bias_i", [HM, 1]), M.low("bias_f", [HM, 1])
        m0 = M.low("m0", [HM, DEC_BATCH])
        NCK = NTP + DEC_BATCH
        mp, ml, ul = M.low("m_prev", [HM, NCK]), M.low("m_last", [HM, NCK]), M.low("u_last", [HM, NCK])
        dec = M.low("decay", [HM, NCK])
        ps = psum(nc, mem, "e_ps", [P, 4, 512])
        ps_n = psum(nc, mem, "e_ps_n", [P, 64])
        ps_d = psum(nc, mem, "e_ps_d", [P, HM, NCK])
        ld, ldc, ldg, ldf, ldi, i_ok = (sem(n) for n in ("ld", "ldc", "ldg", "ldf", "ldi", "i_ok"))
        dup, o_out = sem("dup"), sem("o_out")
        tp, ev, row, exp_ok, ones_ok, arg_ok = (sem(n) for n in ("tp", "ev", "row", "exp_ok", "ones", "arg_ok"))
        dec_ok, n_tp, d_ok, ml_ok = sem("dec_ok"), sem("n_tp"), sem("d_ok"), sem("ml_ok")
        sc_v = scratch.ap()
        vaug, ktm, kvtok, CT, Gt = E["vaug"], E["ktm"], E["kvtok"], E["CT"], E["Gt"]

        BATCHES = [("kv", b) for b in range(3)] + [("v", t) for t in range(NT)] + \
                  [("mk", t) for t in range(NT)] + [("C", h) for h in range(HM)] + [("G", b) for b in range(3)]
        KV_DONE = 3

        with nc.Block() as block:
            @block.sync
            def _(sp):
                bg = io["b_mlstm_gates"][0].rearrange("(g h a) -> g h a", g=2, a=1)
                sp.dma_start(rf[:], sc_v[N_SIG, HM:2 * HM, :]).then_inc(ldf, 16)
                sp.dma_start(bf[:], bg[1]).then_inc(ldf, 16)
                sp.dma_start(ri[:], sc_v[N_SIG, 0:HM, :]).then_inc(ldi, 16)
                sp.dma_start(bi[:], bg[0]).then_inc(ldi, 16)
                sp.dma_start(keep[:], io["keep"]).then_inc(ldg, 16)
                sp.dma_start(m0[:], io["state_mlstm_m"][0].rearrange("b h -> h b"),
                             allow_slow_non_contiguous=True).then_inc(ldg, 16)
                sp.dma_start(E["head_sel"][:], io["head_sel"].rearrange("h k p -> k h p")).then_inc(ldg, 16)
                for h in range(HM):
                    sp.dma_start(E["Cn"][:, h], io["state_mlstm_C"][0, :, h].rearrange("b v d -> v b d"))\
                        .then_inc(ldc, 16)
                sp.dma_start(nrow[:], io["state_mlstm_n"][0].rearrange("b h d -> (b h) d")).then_inc(ldc, 16)
                for n in ("causal_p", "causal_s", "batch_mask", "pair_mask"):
                    sp.dma_start(E[n][:], io[n]).then_inc(ld, 16)
                for half in range(2):
                    rows = slice(64 * half, 64 * half + 64)
                    for par in range(2):
                        src = slice(64 * par, 64 * par + 64)
                        sp.dma_start(E["mqd"][rows, par::2, :], E["mqk"][src, 0:2, SEQ:N_TOK]).then_inc(dup, 16)
                sp.wait_ge(ev, KV_DONE)
                for n, cols in (("k", slice(0, DH)), ("v", slice(DH, 2 * DH))):
                    sp.dma_start(out[f"new_{n}_prompt"][0, 0].rearrange("(t p) d -> p t d", p=P),
                                 kvtok[:, 0:NTP, cols]).then_inc(o_out, 16)
                    sp.dma_start(out[f"new_{n}_sample"][0].rearrange("b q d -> (b q) d"),
                                 kvtok[:, NTP, cols]).then_inc(o_out, 16)
                sp.wait_ge(ml_ok, 2)
                sp.dma_start(out["new_m_prompt"][0, 0].rearrange("(h a) -> h a", a=1),
                             ml[:, NTP - 1:NTP]).then_inc(o_out, 16)
                sp.dma_start(out["new_m_sample"][0].rearrange("b h -> h b"), ml[:, NTP:NCK],
                             allow_slow_non_contiguous=True).then_inc(o_out, 16)
                sp.wait_ge(o_out, 96)
                sp.wait_ge(ld, 16 * 4)
                sp.wait_ge(dup, 16 * 4)
                sp.wait_ge(ldc, 16 * 5)

            @block.gpsimd
            def _(pool):
                nc.gpsimd.memset(G4[:], 0.0).then_inc(ones_ok, 1)
                nc.gpsimd.memset(vaug[:, :, :, DV:DV + 1], 1.0).then_inc(ones_ok, 1)
                nc.gpsimd.memset(mp[:, 0:1], 0.0).then_inc(ones_ok, 1)
                pool.wait_ge(ones_ok, 3)
                pool.wait_ge(ldi, 32)
                nc.gpsimd.tensor_scalar(ri[:], ri[:], bi[:], None, ALU.add).then_inc(i_ok, 1)
                pool.wait_ge(i_ok, 1)
                nc.gpsimd.tensor_copy(t3[:], ri[:]).then_inc(i_ok, 1)

            @block.vector
            def _(dve):
                cnt = [0]
                V = G4[0:HM, :]

                def step(ins):
                    cnt[0] += 1
                    ins.then_inc(row, 1)
                    dve.wait_ge(row, cnt[0])
                v = nc.vector
                smp = lambda t: t[:, SEQ:N_TOK].rearrange("h (b q) -> h b q", q=DEC_SEQ)
                prm = lambda t: t[:, 0:SEQ].rearrange("h (c q) -> h c q", q=P)
                dve.wait_ge(ldf, 32)
                step(v.tensor_scalar(rf[:], rf[:], bf[:], None, ALU.add))
                step(v.scalar_tensor_tensor(t1[:], rf[:], -1.0, rf[:], ALU.mult, ALU.max))
                v.tensor_scalar(rf[:], rf[:], 0.0, None, ALU.min).then_inc(arg_ok, 1)
                dve.wait_ge(arg_ok, 1)
                dve.wait_ge(exp_ok, 2)
                dve.wait_ge(ldg, 16 * 3)
                dve.wait_ge(i_ok, 2)
                step(v.tensor_tensor(rf[:], rf[:], t2[:], ALU.subtract))
                step(v.tensor_tensor_scan(b_[:], keep[:], rf[:], 0.0, ALU.mult, ALU.add))
                step(v.tensor_tensor(dec[:, 0:DEC_BATCH], smp(rf)[:, :, 0], m0[:], ALU.add))
                step(v.tensor_tensor(smp(t3)[:, :, 0], dec[:, 0:DEC_BATCH], smp(ri)[:, :, 0], ALU.max))
                step(v.memset(smp(rf)[:, :, 0], -BIG))
                step(v.tensor_tensor_scan(m_[:], rf[:], t3[:], 0.0, ALU.add, ALU.max))
                v.tensor_copy(ml[:, 0:NTP], prm(m_)[:, :, P - 1]).then_inc(ml_ok, 1)
                v.tensor_copy(ml[:, NTP:NCK], smp(m_)[:, :, DEC_SEQ - 1]).then_inc(ml_ok, 1)
                dve.wait_ge(ml_ok, 2)
                dve.wait_ge(ones_ok, 3)
                step(v.tensor_copy(mp[:, 1:NTP], ml[:, 0:NTP - 1]))
                step(v.tensor_copy(mp[:, NTP:NCK], m0[:]))
                step(v.tensor_tensor(V, ri[:], b_[:], ALU.subtract))
                step(v.tensor_tensor(E["U"][:], b_[:], m_[:], ALU.subtract))
                step(v.tensor_tensor(prm(t1), prm(E["U"]), mp[:, 0:NTP, None].to_broadcast([HM, NTP, P]), ALU.add))
                step(v.tensor_tensor(smp(t1), smp(E["U"]),
                                     mp[:, NTP:NCK, None].to_broadcast([HM, DEC_BATCH, DEC_SEQ]), ALU.add))
                step(v.tensor_copy(ul[:, 0:NTP], prm(E["U"])[:, :, P - 1]))
                step(v.tensor_copy(ul[:, NTP:NCK], smp(E["U"])[:, :, DEC_SEQ - 1]))
                step(v.tensor_tensor(prm(t2), prm(V), ul[:, 0:NTP, None].to_broadcast([HM, NTP, P]), ALU.add))
                v.tensor_tensor(smp(t2), smp(V), ul[:, NTP:NCK, None].to_broadcast([HM, DEC_BATCH, DEC_SEQ]), ALU.add)\
                    .then_inc(arg_ok, 1)
                dve.wait_ge(arg_ok, 2)
                dve.wait_ge(exp_ok, 5)
                gw = G4[32:32 + HM, :]
                v.tensor_copy(dec[:, 0:NTP], prm(gw)[:, :, P - 1]).then_inc(dec_ok, 1)
                v.tensor_copy(dec[:, NTP:NCK], smp(gw)[:, :, DEC_SEQ - 1]).then_inc(dec_ok, 1)
                dve.wait_ge(d_ok, 1)
                v.tensor_copy(E["decB"][:], ps_d[:]).then_inc(d_ok, 1)
                dve.wait_ge(d_ok, 2)
                for h in range(HM):
                    half = slice(64 * (h % 2), 64 * (h % 2) + 64)
                    step(v.tensor_copy(E["decP"][half, h // 2, :], E["decB"][half, h, 0:NTP]))

            @block.scalar
            def _(act):
                act.wait_ge(arg_ok, 1)
                nc.scalar.activation(t2[:], t1[:], ACT.Exp, scale=-1.0).then_inc(exp_ok, 1)
                act.wait_ge(exp_ok, 1)
                nc.scalar.activation(t2[:], t2[:], ACT.Ln, bias=1.0).then_inc(exp_ok, 1)

                def evict(n):
                    kind, x = BATCHES[n]
                    act.wait_ge(tp, n + 1)
                    src = ps[:, n % 4, :]
                    if kind == "kv":
                        dst, src = kvtok[:, 3 * x:3 * x + 3, :], src[:, 0:3 * P].rearrange("p (j n) -> p j n", j=3)
                    elif kind == "v":
                        dst, src = vaug[:, x, :, 0:DV], src.rearrange("p (h v) -> p h v", h=HM)
                    elif kind == "mk":
                        dst, src = ktm[:, x, :], src[:, 0:HM * DH]
                    elif kind == "C":
                        dst, src = CT[:, x, :, 0:DV], src.rearrange("p (j v) -> p j v", j=4)
                    else:
                        for j in range(3):
                            s3 = src[:, j * P:(j + 1) * P].rearrange("p (q n) -> p q n", q=4)[:, :, 0:HM]
                            last = nc.scalar.activation(Gt[:, 3 * x + j], s3, ACT.Copy)
                        last.then_inc(ev, 1)
                        return
                    nc.scalar.activation(dst, src, ACT.Copy).then_inc(ev, 1)

                for n in range(len(BATCHES) - 3):
                    evict(n)
                act.wait_ge(arg_ok, 2)
                act.wait_ge(ones_ok, 3)
                nc.scalar.activation(G4[32:32 + HM, :], t1[:], ACT.Exp).then_inc(exp_ok, 1)
                nc.scalar.activation(G4[64:64 + HM, :], m_[:], ACT.Exp, scale=-1.0).then_inc(exp_ok, 1)
                nc.scalar.activation(G4[96:96 + HM, :], t2[:], ACT.Exp).then_inc(exp_ok, 1)
                for n in range(len(BATCHES) - 3, len(BATCHES)):
                    evict(n)
                act.wait_ge(n_tp, 1)
                nsrc = ps_n[0:DH, 0:DEC_BATCH * HM].rearrange("d (j r h) -> d h j r", r=2, h=HM)
                for par in range(2):
                    last = nc.scalar.activation(CT[64 * par:64 * par + 64, :, :, DV], nsrc[:, :, :, par], ACT.Copy)
                last.then_inc(n_tp, 1)

            @block.tensor
            def _(pe):
                for n, (kind, x) in enumerate(BATCHES):
                    if n >= 4:
                        pe.wait_ge(ev, n - 3)
                    o = lambda j, w=P: ps[:, n % 4, j * w:(j + 1) * w]
                    tok = lambda t: slice(t * P, (t + 1) * P)
                    if kind == "kv":
                        for j in range(3):
                            last = nc.tensor.transpose(o(j), kvT[:, tok(3 * x + j)], K["ident"][:])
                    elif kind == "v":
                        for h in range(HM):
                            last = nc.tensor.transpose(o(h), mvT[:, h, tok(x)], K["ident"][:])
                    elif kind == "mk":
                        for h in range(2):
                            last = nc.tensor.transpose(o(h), E["mqk"][:, 2 + h, tok(x)], K["ident"][:])
                    elif kind == "C":
                        pe.wait_ge(ldc, 16 * 5)
                        for j in range(4):
                            last = nc.tensor.transpose(o(j), E["Cn"][:, x, 2 * j:2 * j + 2, :]
                                                       .rearrange("p b d -> p (b d)"), K["ident"][:])
                    else:
                        pe.wait_ge(exp_ok, 5)
                        for j in range(3):
                            last = nc.tensor.transpose(o(j), G4[:, tok(3 * x + j)], K["ident"][:])
                    last.then_inc(tp, 1)
                NR = DEC_BATCH * HM
                nc.tensor.transpose(ps_n[0:DH, 0:NR], nrow[:], K["ident"][0:NR, 0:NR]).then_inc(n_tp, 1)
                pe.wait_ge(dec_ok, 2)
                for h in range(HM):
                    last = nc.tensor.matmul(ps_d[:, h, :], E["head_sel"][:, h, :], dec[:], start=True, stop=True)
                last.then_inc(d_ok, 1)


def mlstm(nc, ctx, M, K, io, out, kvT, E, num):
    sem = lambda n: ctx.enter_context(nc.semaphore("m_" + n))
    with ExitStack() as mem, M.scope():
        St = M.low("state", [P, 2, 2, DV + 1])
        lg = M.low("m_lg", [P, 2, HM * P])
        W = lg
        SW = M.low("m_sw", [P, 2, HM * P])
        kw = M.at("m_kw", [P, 2, HM, DH], K["acc_at"])
        ti = M.low("m_ti", [P, 2, HM, DV + 1])
        gws = M.low("m_gws", [P, NT, HM])
        qm = M.at("m_qm", [P, HM, 4, P], E["free_at"])
        n1 = M.low("m_n1", [1, HM, DEC_BATCH, DH])
        kwb = M.at("m_kwb", [P, HM, DEC_BATCH, DH], E["free_at"] + HM * 4 * P * 4)
        sq = M.at("m_sq", [P, DV], K["acc_at"] + 2 * HM * DH * 4)
        kraw = kwb
        Cd, nd = E["Cn"], n1
        Cp = M.at("m_cp", [P, HM, DH], K["acc_at"] + (2 * HM * DH + DV) * 4)
        ps_d = psum(nc, mem, "m_ps_d", [P, 512])
        ps_s = psum(nc, mem, "m_ps_s", [P, 512])
        ps_i = [psum(nc, mem, f"m_ps_i{x}", [P, 512]) for x in range(2)]
        ps_n = [psum(nc, mem, f"m_ps_n{x}", [P, 512]) for x in range(2)]
        ps_u = psum(nc, mem, "m_ps_u", [P, 512])
        ps_x = psum(nc, mem, "m_ps_x", [P, 512])
        (d_ok, lg_ok, w_ok, s_ok, sw_ok, i_ok, n_ok, ti_ok, num_ok, kw_ok, u_ok, st_ok, init, q_ok, kb_ok, c_ok,
         n1_ok, cd_ok, cs_ok, nd_ok, o_out, fp, fe) = (sem(n) for n in (
             "d_ok", "lg_ok", "w_ok", "s_ok", "sw_ok", "i_ok", "n_ok", "ti_ok", "num_ok", "kw_ok", "u_ok", "st_ok",
             "init", "q_ok", "kb_ok", "c_ok", "n1_ok", "cd_ok", "cs_ok", "nd_ok", "o_out", "fp", "fe"))
        ldk, lda, ldn, kt_tp, kt_ev, half_ok, ss_ok = (
            sem(n) for n in ("ldk", "lda", "ldn", "kt_tp", "kt_ev", "half_ok", "ss_ok"))
        mqk, vaug, ktm, Gt, CT = E["mqk"], E["vaug"], E["ktm"], E["Gt"], E["CT"]
        pair = lambda b: b[:, 0:2 * (DV + 1)].rearrange("p (h v) -> p h v", h=2)

        with nc.Block() as block:
            @block.sync
            def _(sp):
                sp.dma_start(n1[:], io["state_mlstm_n"][0:1].rearrange("a b h d -> a h b d")).then_inc(ldn, 16)
                for b in range(DEC_BATCH):
                    sp.dma_start(kraw[:, :, b, :], io["cache_attn_k"][0, b].rearrange("(k p) d -> p k d", p=P))\
                        .then_inc(ldk, 16)
                for b in range(DEC_BATCH):
                    sp.dma_start(E["vn"][:, b, :], E["kvtok"][b * DEC_SEQ:(b + 1) * DEC_SEQ, NTP, DH:2 * DH])\
                        .then_inc(lda, 16)
                for half in range(2):
                    rows = slice(64 * half, 64 * half + 64)
                    sp.dma_start(E["kd"][rows, :], kvT[0:DH, :]).then_inc(lda, 16)
                    new = kvT[0:DH, SEQ:N_TOK].rearrange("d (j r q) -> d j r q", r=2, q=DEC_SEQ)
                    sp.dma_start(E["KTa"][rows, :, PAST:LS], new[:, :, half, :]).then_inc(lda, 16)
                sp.wait_ge(lda, 16 * (DEC_BATCH + 4))
                sp.wait_ge(fe, 1)
                sp.dma_start(out["new_C_prompt"][0, 0].rearrange("h v d -> v h d"), Cp[:]).then_inc(o_out, 16)
                for h in range(HM):
                    half = slice(64 * (h % 2), 64 * (h % 2) + 64)
                    sp.dma_start(out["new_n_prompt"][0, 0, h].rearrange("(d a) -> d a", a=1),
                                 St[half, NTP % 2, h // 2, DV:DV + 1]).then_inc(o_out, 16)
                for h in range(HM):
                    sp.wait_ge(cs_ok, h + 1)
                    sp.dma_start(out["new_C_sample"][0, :, h].rearrange("b v d -> v b d"), Cd[:, h]).then_inc(o_out, 16)
                sp.wait_ge(nd_ok, HM)
                sp.dma_start(out["new_n_sample"][0:1].rearrange("a b h d -> a h b d"), nd[:]).then_inc(o_out, 16)
                sp.wait_ge(o_out, 16 * (2 + 2 * HM))

            @block.gpsimd
            def _(pool):
                nc.gpsimd.memset(St[:, 0], 0.0).then_inc(init, 1)
                dB = E["decB"][:, :, NTP:]
                nc.gpsimd.tensor_tensor(Cd[:], E["Cn"][:], dB[:, :, :, None].to_broadcast([P, HM, DEC_BATCH, DH]),
                                        ALU.mult).then_inc(cd_ok, 1)
                pool.wait_ge(ldn, 16)
                nc.gpsimd.tensor_tensor(nd[:], n1[:], dB[0:1, :, :, None].to_broadcast([1, HM, DEC_BATCH, DH]),
                                        ALU.mult).then_inc(cd_ok, 1)
                for h in range(HM):
                    nc.gpsimd.tensor_tensor(qm[:, h], E["pair_mask"][:], E["mqd"][:, h:h + 1, :]
                                            .to_broadcast([P, 4, P]), ALU.mult).then_inc(q_ok, 1)
                for r in range(2):
                    for par in range(2):
                        dst = E["aqr"][64 * r:64 * r + 64].rearrange("d j (g p q) -> d p g j q", g=4, p=2)
                        src = E["aq"][64 * par:64 * par + 64, :, SEQ:N_TOK].rearrange(
                            "d g (j r q) -> d r g j q", r=2, q=DEC_SEQ)
                        pool.wait_ge(q_ok, HM + 2 * r + par)
                        nc.gpsimd.tensor_copy(dst[:, par], src[:, r]).then_inc(q_ok, 1)
                pool.wait_ge(q_ok, HM + 4)

            @block.scalar
            def _(act):
                def squares(t):
                    act.wait_ge(num_ok, 2 * (t + 1))
                    for h in range(HM):
                        if t or h:
                            act.wait_ge(ss_ok, HM * t + h)
                        nc.scalar.activation(sq[:], num[:, t, h, 0:DV], ACT.Square,
                                             accum_out=E["ss"][:, t, h:h + 1]).then_inc(ss_ok, 1)

                act.wait_ge(init, 2)
                for t in range(NT):
                    act.wait_ge(lg_ok, t + 1)
                    for h in range(HM):
                        w = slice(h * P, (h + 1) * P)
                        nc.scalar.activation(W[:, t % 2, w], lg[:, t % 2, w], ACT.Exp, bias=Gt[:, t, 0, h:h + 1])\
                            .then_inc(w_ok, 1)
                    if t >= 2:
                        act.wait_ge(num_ok, 2 * (t - 1))
                    for y in range(2):
                        act.wait_ge(n_ok, 2 * t + y + 1)
                        for x in range(2):
                            h = 2 * x + y
                            nc.scalar.activation(ti[:, t % 2, h], pair(ps_n[y])[:, x], ACT.Copy,
                                                 scale=gws[:, t, h:h + 1]).then_inc(ti_ok, 1)
                    if t < 4:
                        act.wait_ge(kt_tp, t + 1)
                        nc.scalar.activation(E["KTa"][:, t, 0:PAST], ps_x[:], ACT.Copy).then_inc(kt_ev, 1)
                    if t:
                        squares(t - 1)
                squares(NT - 1)
                act.wait_ge(fp, 1)
                nc.scalar.activation(Cp[:], ps_x[:, 0:HM * DH].rearrange("p (h d) -> p h d", h=HM), ACT.Copy)\
                    .then_inc(fe, 1)

            @block.vector
            def _(dve):
                nc.vector.tensor_scalar(gws[:], Gt[:, :, 1, :], QK_SCALE, None, ALU.mult).then_inc(init, 1)
                for t in range(NT):
                    mask = E["causal_s" if t == NTP else "causal_p"][:, None, :].to_broadcast([P, HM, P])
                    if t >= 2:
                        dve.wait_ge(u_ok, t - 1)
                    nc.vector.tensor_tensor(kw[:, t % 2], ktm[:, t, :].rearrange("p (h d) -> p h d", h=HM),
                                            Gt[:, t, 3, :, None].to_broadcast([P, HM, DH]), ALU.mult).then_inc(kw_ok, 1)
                    dve.wait_ge(d_ok, t + 1)
                    if t >= 2:
                        dve.wait_ge(sw_ok, t - 1)
                    nc.vector.tensor_tensor(lg[:, t % 2].rearrange("p (h t) -> p h t", h=HM),
                                            ps_d[:, :].rearrange("p (h t) -> p h t", h=HM), mask, ALU.add)\
                        .then_inc(lg_ok, 1)
                    if t < NTP:
                        dve.wait_ge(u_ok, t + 1)
                        if t == 0:
                            dve.wait_ge(init, 2)
                        for x in range(2):
                            if t:
                                dve.wait_ge(st_ok, 2 * t)
                            nc.vector.scalar_tensor_tensor(St[:, (t + 1) % 2, x], St[:, t % 2, x],
                                                           E["decP"][:, x, t:t + 1], pair(ps_u)[:, x],
                                                           ALU.mult, ALU.add).then_inc(st_ok, 1)
                    dve.wait_ge(w_ok, HM * (t + 1))
                    dve.wait_ge(s_ok, t + 1)
                    if t >= 2:
                        dve.wait_ge(i_ok, 2 * (t - 1))
                    nc.vector.scalar_tensor_tensor(SW[:, t % 2], ps_s[:], QK_SCALE, W[:, t % 2], ALU.mult, ALU.mult)\
                        .then_inc(sw_ok, 1)
                    for x in range(2):
                        dve.wait_ge(i_ok, 2 * t + x + 1)
                        dve.wait_ge(ti_ok, 4 * t + 4)
                        nc.vector.tensor_tensor(num[:, t, 2 * x:2 * x + 2, :], ti[:, t % 2, 2 * x:2 * x + 2, :],
                                                pair(ps_i[x]), ALU.add).then_inc(num_ok, 1)
                dve.wait_ge(kw_ok, NT)
                dve.wait_ge(kt_tp, 4)
                for h in range(HM):
                    nc.vector.tensor_tensor(kwb[:, h], kw[:, NTP % 2, h:h + 1, :].to_broadcast([P, DEC_BATCH, DH]),
                                            E["batch_mask"][:, :, None].to_broadcast([P, DEC_BATCH, DH]),
                                            ALU.mult).then_inc(kb_ok, 1)
                dve.wait_ge(cd_ok, 2)
                for h in range(HM):
                    dve.wait_ge(c_ok, h + 1)
                    nc.vector.tensor_tensor(Cd[:, h], Cd[:, h], ps_d[:].rearrange("p (b d) -> p b d", b=DEC_BATCH),
                                            ALU.add).then_inc(cs_ok, 1)
                    dve.wait_ge(n1_ok, h + 1)
                    nc.vector.tensor_tensor(nd[:, h], nd[:, h], ps_s[0:1].rearrange("p (b d) -> p b d", b=DEC_BATCH),
                                            ALU.add).then_inc(nd_ok, 1)

            @block.tensor
            def _(pe):
                for t in range(NT):
                    tok = slice(t * P, (t + 1) * P)
                    if t:
                        pe.wait_ge(lg_ok, t)
                    for h in range(HM):
                        o = ps_d[:, h * P:(h + 1) * P]
                        last = nc.tensor.matmul(o, E["head_sel"][:, h, :], E["U"][:, tok], start=True, stop=True)
                    last.then_inc(d_ok, 1)
                    if t:
                        pe.wait_ge(sw_ok, t)
                    for h in (0, 2, 1, 3):
                        if h == 1:
                            pe.wait_ge(half_ok, t + 1)
                        half = slice(64 * (h % 2), 64 * (h % 2) + 64)
                        last = nc.tensor.matmul(ps_s[:, h * P:(h + 1) * P], mqk[half, 2 + h // 2, tok],
                                                mqk[half, h // 2, tok], start=True, stop=True)
                        if h == 2:
                            last.then_inc(half_ok, 1)
                    last.then_inc(s_ok, 1)
                    pe.wait_ge(kw_ok, t + 1)
                    if t < NTP:
                        if t:
                            pe.wait_ge(st_ok, 2 * t)
                        for h in range(HM):
                            half = slice(64 * (h % 2), 64 * (h % 2) + 64)
                            last = nc.tensor.matmul(pair(ps_u)[half, h // 2], kw[:, t % 2, h, :], vaug[:, t, h, :],
                                                    start=True, stop=True)
                        last.then_inc(u_ok, 1)
                    if t == 0:
                        pe.wait_ge(init, 2)
                    if t == NTP:
                        pe.wait_ge(q_ok, HM)
                    for y in range(2):
                        if t:
                            pe.wait_ge(ti_ok, 4 * (t - 1) + 2 * y + 2)
                        for x in range(2):
                            h = 2 * x + y
                            half = slice(64 * y, 64 * y + 64)
                            o = pair(ps_n[y])[:, x]
                            if t < NTP:
                                last = nc.tensor.matmul(o, mqk[half, h // 2, tok], St[half, t % 2, h // 2, :],
                                                        start=True, stop=True)
                            else:
                                for j in range(4):
                                    last = nc.tensor.matmul(o, qm[:, h, j, :], CT[:, h, j, :],
                                                            start=j == 0, stop=j == 3)
                        last.then_inc(n_ok, 1)
                    pe.wait_ge(sw_ok, t + 1)
                    for x in range(2):
                        if t:
                            pe.wait_ge(num_ok, 2 * (t - 1) + x + 1)
                        for y in range(2):
                            h = 2 * x + y
                            last = nc.tensor.matmul(pair(ps_i[x])[:, y], SW[:, t % 2, h * P:(h + 1) * P],
                                                    vaug[:, t, h, :], start=True, stop=True)
                        last.then_inc(i_ok, 1)
                    if t < 4:
                        pe.wait_ge(ldk, 16 * DEC_BATCH)
                        if t:
                            pe.wait_ge(kt_ev, t)
                        for k in range(4):
                            last = nc.tensor.transpose(ps_x[:, k * P:(k + 1) * P],
                                                       kraw[:, k, 2 * t:2 * t + 2, :].rearrange("p b d -> p (b d)"),
                                                       K["ident"][:])
                        last.then_inc(kt_tp, 1)
                pe.wait_ge(kt_ev, 4)
                pe.wait_ge(st_ok, 2 * NTP)
                for h in (0, 2, 1, 3):
                    if h == 1:
                        pe.wait_ge(half_ok, NT + 1)
                    half = slice(64 * (h % 2), 64 * (h % 2) + 64)
                    last = nc.tensor.transpose(ps_x[:, h * DH:(h + 1) * DH], St[half, NTP % 2, h // 2, 0:DV],
                                               K["ident"][half, half])
                    if h == 2:
                        last.then_inc(half_ok, 1)
                last.then_inc(fp, 1)
                for h in range(HM):
                    pe.wait_ge(kb_ok, HM)
                    if h:
                        pe.wait_ge(cs_ok, h)
                    f = kwb[:, h].rearrange("p b d -> p (b d)")
                    nc.tensor.matmul(ps_d[:], vaug[:, NTP, h, 0:DV], f, start=True, stop=True).then_inc(c_ok, 1)
                    if h:
                        pe.wait_ge(nd_ok, h)
                    nc.tensor.matmul(ps_s[0:1, :], K["ones"][:, 0:1], f, start=True, stop=True).then_inc(n1_ok, 1)


def mlstm_output(nc, ctx, M, K, E, num, h_hi, h_lo, scratch):
    sem = lambda n: ctx.enter_context(nc.semaphore("h_" + n))
    with ExitStack() as mem, M.scope():
        og = M.low("h_og", [P, HM, N_TOK])
        den, inv, rs, sc = (M.low("h_" + n, [P, NT, HM]) for n in ("den", "inv", "rs", "sc"))
        hn = M.low("h_n", [P, 2, HM, DV])
        full = M.low("h_full", [P, 2, HM, P])
        ps = psum(nc, mem, "h_ps", [P, 2, 512])
        ld, row, rs_in, rs_ok, n_ok, tp, f_ok, hi, lo = (
            sem(n) for n in ("ld", "row", "rs_in", "rs_ok", "n_ok", "tp", "f_ok", "hi", "lo"))
        with nc.Block() as block:
            @block.sync
            def _(sp):
                sp.dma_start(og[:], scratch.ap()[0:HM].rearrange("k p n -> p k n")).then_inc(ld, 16)

            @block.scalar
            def _(act):
                act.wait_ge(rs_in, 1)
                nc.scalar.activation(rs[:], rs[:], ACT.Sqrt).then_inc(rs_ok, 1)
                for t in range(NT):
                    act.wait_ge(f_ok, HM * (t + 1))
                    nc.scalar.activation(h_hi[:, :, t * P:(t + 1) * P], full[:, t % 2], ACT.Copy).then_inc(hi, 1)

            @block.vector
            def _(dve):
                v, cnt = nc.vector, [0]

                def step(ins):
                    cnt[0] += 1
                    ins.then_inc(row, 1)
                    dve.wait_ge(row, cnt[0])
                nq = num[:, :, :, DV]
                step(v.scalar_tensor_tensor(den[:], nq, -1.0, nq, ALU.mult, ALU.max))
                step(v.tensor_tensor(den[:], den[:], E["Gt"][:, :, 2, :], ALU.max))
                step(v.reciprocal(inv[:], den[:]))
                step(v.tensor_tensor(rs[:], E["ss"][:], inv[:], ALU.mult))
                step(v.tensor_tensor(rs[:], rs[:], inv[:], ALU.mult))
                step(v.tensor_scalar(rs[:], rs[:], 1.0 / DV, EPS, ALU.mult, ALU.add))
                v.reciprocal(rs[:], rs[:]).then_inc(rs_in, 1)
                dve.wait_ge(rs_ok, 1)
                step(v.tensor_tensor(sc[:], inv[:], rs[:], ALU.mult))

                def scaled(t):
                    if t >= 2:
                        dve.wait_ge(tp, t - 1)
                    v.tensor_tensor(hn[:, t % 2], num[:, t, :, 0:DV], sc[:, t, :, None].to_broadcast([P, HM, DV]),
                                    ALU.mult).then_inc(n_ok, 1)
                scaled(0)
                dve.wait_ge(ld, 16)
                for t in range(NT):
                    if t + 1 < NT:
                        scaled(t + 1)
                    dve.wait_ge(tp, t + 1)
                    if t >= 2:
                        dve.wait_ge(lo, t - 1)
                    for h in range(HM):
                        v.scalar_tensor_tensor(full[:, t % 2, h], ps[:, t % 2, h * P:(h + 1) * P],
                                               K["g_mlstm"][:, h:h + 1], og[:, h, t * P:(t + 1) * P],
                                               ALU.mult, ALU.mult).then_inc(f_ok, 1)

            @block.gpsimd
            def _(pool):
                for t in range(NT):
                    pool.wait_ge(hi, t + 1)
                    tok = slice(t * P, (t + 1) * P)
                    nc.gpsimd.tensor_tensor(h_lo[:, :, tok], full[:, t % 2], h_hi[:, :, tok].bitcast(F32),
                                            ALU.subtract).then_inc(lo, 1)

            @block.tensor
            def _(pe):
                for t in range(NT):
                    pe.wait_ge(n_ok, t + 1)
                    if t >= 2:
                        pe.wait_ge(f_ok, HM * (t - 1))
                    for h in range(HM):
                        last = nc.tensor.transpose(ps[:, t % 2, h * P:(h + 1) * P], hn[:, t % 2, h, :], K["ident"][:])
                    last.then_inc(tp, 1)


def attention(nc, ctx, M, K, io, E, DM, o_hi, o_lo):
    sem = lambda n: ctx.enter_context(nc.semaphore("t_" + n))
    ITEMS = [(t, x, g) for t in range(NT) for g in [4 if t < 2 else 2 if t < 4 else 1] for x in range(0, HA, g)]
    NKS = PAST // P
    HALVES = NT * HA // 4
    LAST = [max(i for i, (t, x, g) in enumerate(ITEMS) if t * HA + x < 4 * m + 4) for m in range(HALVES)]
    FIRST = {t: min(i for i, item in enumerate(ITEMS) if item[0] == t) for t in range(NT)}
    with ExitStack() as mem, M.scope():
        vc = M.low("vc", [P, NKS, DEC_BATCH, DH])
        lg = M.low("t_lg", [P, 2, SEQ])
        pr = M.low("t_p", [P, 2, SEQ])
        PT = M.low("t_pt", [P, 2, NTP, P])
        DMr = M.low("t_dmr", [P, DEC_BATCH, LS])
        slope = M.low("t_slope", [P, 1])
        qs = M.low("t_qs", [P, 2, HA, P], F32R)
        k_hi = M.low("t_k_hi", [P, SEQ], F32R)
        k_lo = M.at("t_k_lo", [P, SEQ], E["kvT_at"], F32R)
        mx, nm, sm, inv = (M.low("t_" + n, [P, 2, 4]) for n in ("mx", "nm", "sm", "inv"))
        ofs = M.low("t_ofs", [P, 2, 2 * P])
        ps_l = psum(nc, mem, "t_ps_l", [P, 2, 1024])
        ps_t = psum(nc, mem, "t_ps_t", [P, 2, 512])
        ps_o = psum(nc, mem, "t_ps_o", [P, HA, P])
        (ld, ldm, qk, lg_ok, mx_ok, nm_ok, p_ok, inv_ok, pn_ok, tr, tr_ev, pv, of_ok, hi, lo,
         kh_ok, kl_ok, qh_ok, ql_ok) = (
            sem(n) for n in ("ld", "ldm", "qk", "lg_ok", "mx_ok", "nm_ok", "p_ok", "inv_ok", "pn_ok", "tr",
                             "tr_ev", "pv", "of_ok", "hi", "lo", "kh_ok", "kl_ok", "qh_ok", "ql_ok"))

        def query_parts(t, r):
            rows, other = slice(64 * r, 64 * r + 64), slice(64 - 64 * r, 128 - 64 * r)
            return E["aq"][rows, :, t * P:(t + 1) * P], qs[rows, t % 2, r::2, :], qs[other, t % 2, r::2, :]

        def keys(t):
            return LS if t == NTP else P * (t + 1)

        def heads(buf, i):
            t, _, g = ITEMS[i]
            return buf[:, i % 2, 0:g * keys(t)].rearrange("p (h n) -> p h n", h=g)

        BATCH = []
        for t, _, g in ITEMS:
            n = -(-g * keys(t) // P)
            BATCH.append([(k, min(k + 4, n)) for k in range(0, n, 4)])
        UPTO = np.cumsum([0] + [len(b) for b in BATCH]).tolist()

        def half_out(a, m):
            t, g = divmod(m, 2)
            if t < NTP:
                return a[:, 2 * g:2 * g + 2, t * P:(t + 1) * P]
            return a[:, :, SEQ + 64 * g:SEQ + 64 * g + 64]

        def half_staged(m):
            return ofs[:, m % 2].rearrange("p (j n) -> p j n", j=2 if m // 2 < NTP else 4)

        with nc.Block() as block:
            @block.sync
            def _(sp):
                for b in range(DEC_BATCH):
                    sp.dma_start(vc[:, :, b, :], io["cache_attn_v"][0, b].rearrange("(k p) d -> p k d", p=P))\
                        .then_inc(ld, 16)
                sp.dma_start(slope[:], io["slope"]).then_inc(ldm, 16)
                for b in range(DEC_BATCH):
                    rows = slice(b * DEC_SEQ, (b + 1) * DEC_SEQ)
                    for h in range(HA):
                        sp.dma_start(DMr[h * DEC_SEQ:(h + 1) * DEC_SEQ, b, :],
                                     DM[rows, SCORE_OFF[NTP]:SCORE_OFF[NTP] + LS]).then_inc(ldm, 16)

            @block.gpsimd
            def _(pool):
                def query_lo(t, m):
                    pool.wait_ge(qh_ok, 2 * (t + 1))
                    if m:
                        pool.wait_ge(lo, m)
                    for r in range(2):
                        if t or r:
                            pool.wait_ge(ql_ok, 2 * t + r)
                        q, q_hi, q_lo = query_parts(t, r)
                        nc.gpsimd.tensor_tensor(q_lo, q, q_hi.bitcast(F32), ALU.subtract).then_inc(ql_ok, 1)

                def output_lo(t, m):
                    pool.wait_ge(hi, m + 1)
                    pool.wait_ge(ql_ok, 2 * (t + 1))
                    nc.gpsimd.tensor_tensor(half_out(o_lo, m), half_staged(m), half_out(o_hi, m).bitcast(F32),
                                            ALU.subtract).then_inc(lo, 1)

                query_lo(0, 0)
                query_lo(1, 0)
                m, split = 0, 1
                for i, (t, x, g) in enumerate(ITEMS):
                    if t + 2 < NTP and i + 1 == FIRST[t + 1]:
                        split = t + 2
                        query_lo(split, m)
                    if i >= LAST[m] + 2:
                        output_lo(split, m)
                        m += 1
                while m < HALVES:
                    output_lo(split, m)
                    m += 1

            @block.tensor
            def _(pe):
                def product(i):
                    t, x0, g = ITEMS[i]
                    if i >= 2:
                        pe.wait_ge(lg_ok, i - 1)
                    if t < NTP and x0 == 0:
                        pe.wait_ge(kl_ok, 1)
                        pe.wait_ge(ql_ok, 2 * (t + 1))
                    L = keys(t)
                    for y in range(g):
                        x = x0 + y
                        half = slice(64 * (x % 2), 64 * (x % 2) + 64)
                        for at in range(0, L, 512):
                            w = min(512, L - at)
                            base = y * (1024 // g) + at
                            o = ps_l[:, i % 2, base:base + w]
                            if t < NTP:
                                nc.tensor.matmul(o, qs[:, t % 2, x, :], k_hi[:, at:at + w], start=True, stop=False)
                                last = nc.tensor.matmul(o, qs[:, t % 2, x, :], k_lo[:, at:at + w],
                                                        start=False, stop=True)
                            else:
                                last = nc.tensor.matmul(o, E["aqr"][half, x // 2, :],
                                                        E["KTa"][half, x // 2, at:at + w], start=True, stop=True)
                    last.then_inc(qk, 1)

                def transposes(i):
                    t, _, g = ITEMS[i]
                    pe.wait_ge(pn_ok, i + 1)
                    for n, (k0, k1) in enumerate(BATCH[i], UPTO[i]):
                        if n >= 2:
                            pe.wait_ge(tr_ev, n - 1)
                        for k in range(k0, k1):
                            w = min(P, g * keys(t) - k * P)
                            last = nc.tensor.transpose(ps_t[0:w, n % 2, (k - k0) * P:(k - k0 + 1) * P],
                                                       pr[:, i % 2, k * P:k * P + w], K["ident"][:])
                        last.then_inc(tr, 1)

                def values(i):
                    t, x0, g = ITEMS[i]
                    pe.wait_ge(tr_ev, UPTO[i + 1])
                    m = (t * HA + x0) // 4
                    if x0 % 4 == 0 and m >= 2:
                        pe.wait_ge(of_ok, 2 * (m - 1))
                    n = t + 1 if t < NTP else NKS + 1
                    for y in range(g):
                        x = x0 + y
                        for k in range(n):
                            if t < NTP:
                                v, w = E["kvtok"][:, k, DH:2 * DH], PT[:, i % 2, y * n + k, :]
                            elif k < NKS:
                                v, w = vc[:, k, x, :], PT[:, i % 2, k, :]
                            else:
                                v, w = E["vn"][:, x, :], PT[0:DEC_SEQ, i % 2, k, :]
                            last = nc.tensor.matmul(ps_o[0:DH, x, :], v, w, start=k == 0, stop=k == n - 1)
                    last.then_inc(pv, 1)

                product(0)
                product(1)
                for i in range(len(ITEMS)):
                    if i + 2 < len(ITEMS):
                        product(i + 2)
                    transposes(i)
                    if i == FIRST[NTP] + 1:
                        pe.wait_ge(ld, 16 * DEC_BATCH)
                    if i:
                        values(i - 1)
                values(len(ITEMS) - 1)

            @block.vector
            def _(dve):
                v = nc.vector

                def logits(i):
                    t, x0, g = ITEMS[i]
                    L = keys(t)
                    if i == FIRST[NTP]:
                        dve.wait_ge(ldm, 16 * (DEC_BATCH * HA + 1))
                    dve.wait_ge(qk, i + 1)
                    if i >= 2:
                        dve.wait_ge(p_ok, i - 1)
                    for y in range(g):
                        x = x0 + y
                        if t < NTP:
                            dist, by = DM[:, SCORE_OFF[t]:SCORE_OFF[t] + L], -SLOPE[x]
                        else:
                            dist, by = DMr[:, x, :], slope[:]
                        base = y * (1024 // g)
                        last = v.scalar_tensor_tensor(heads(lg, i)[:, y], dist, by, ps_l[:, i % 2, base:base + L],
                                                      ALU.mult, ALU.add)
                    last.then_inc(lg_ok, 1)
                    dve.wait_ge(lg_ok, i + 1)
                    v.reduce_max(mx[:, i % 2, 0:g], heads(lg, i), AX_X).then_inc(mx_ok, 1)
                    dve.wait_ge(mx_ok, i + 1)
                    v.tensor_scalar(nm[:, i % 2, 0:g], mx[:, i % 2, 0:g], -QK_SCALE, None, ALU.mult)\
                        .then_inc(nm_ok, 1)

                def normalise(i):
                    t, _, g = ITEMS[i]
                    dve.wait_ge(p_ok, i + 1)
                    v.reciprocal(inv[:, i % 2, 0:g], sm[:, i % 2, 0:g]).then_inc(inv_ok, 1)
                    dve.wait_ge(inv_ok, i + 1)
                    if g == 1:
                        p = pr[:, i % 2, 0:keys(t)]
                        v.tensor_scalar(p, p, inv[:, i % 2, 0:1], None, ALU.mult).then_inc(pn_ok, 1)
                    else:
                        v.tensor_tensor(heads(pr, i), heads(pr, i),
                                        inv[:, i % 2, 0:g, None].to_broadcast([P, g, keys(t)]), ALU.mult)\
                            .then_inc(pn_ok, 1)

                dve.wait_ge(kh_ok, 1)
                v.tensor_tensor(k_lo[:], E["kd"][:, 0:SEQ], k_hi[:].bitcast(F32), ALU.subtract).then_inc(kl_ok, 1)
                logits(0)
                logits(1)
                for i, (t, x, g) in enumerate(ITEMS):
                    normalise(i)
                    if i + 2 < len(ITEMS):
                        logits(i + 2)

            @block.scalar
            def _(act):
                def probs(i):
                    _, _, g = ITEMS[i]
                    act.wait_ge(nm_ok, i + 1)
                    if i >= 2:
                        act.wait_ge(tr, UPTO[i - 1])
                    for y in range(g):
                        last = nc.scalar.activation(heads(pr, i)[:, y], heads(lg, i)[:, y], ACT.Exp,
                                                    bias=nm[:, i % 2, y:y + 1], scale=QK_SCALE,
                                                    accum_out=sm[:, i % 2, y:y + 1])
                    last.then_inc(p_ok, 1)

                def evict(i):
                    if i >= 2:
                        act.wait_ge(pv, i - 1)
                    for n, (k0, k1) in enumerate(BATCH[i], UPTO[i]):
                        act.wait_ge(tr, n + 1)
                        src = ps_t[:, n % 2, 0:(k1 - k0) * P].rearrange("p (k n) -> p k n", n=P)
                        rows = slice(0, min(P, ITEMS[i][2] * keys(ITEMS[i][0]) - k0 * P))
                        nc.scalar.activation(PT[rows, i % 2, k0:k1, :], src[rows], ACT.Copy).then_inc(tr_ev, 1)

                def output(m):
                    t, g = divmod(m, 2)
                    act.wait_ge(pv, LAST[m] + 1)
                    if m >= 2:
                        act.wait_ge(lo, m - 1)
                    for r in range(2):
                        src, dst = ps_o[0:DH, 4 * g:4 * g + 4, :], half_staged(m)[64 * r:64 * r + 64]
                        if t < NTP:
                            src = src.rearrange("d (j r) n -> d r j n", r=2)[:, r]
                        else:
                            src = src.rearrange("d b (j r q) -> d r j b q", j=4, r=2)[:, r]
                            dst = dst.rearrange("d j (b q) -> d j b q", b=4)
                        nc.scalar.activation(dst, src, ACT.Copy).then_inc(of_ok, 1)
                    act.wait_ge(of_ok, 2 * (m + 1))
                    nc.scalar.activation(half_out(o_hi, m), half_staged(m), ACT.Copy).then_inc(hi, 1)

                def query_hi(t):
                    if t >= 2:
                        act.wait_ge(qk, FIRST[t - 1])
                    for r in range(2):
                        q, q_hi, _ = query_parts(t, r)
                        nc.scalar.activation(q_hi, q, ACT.Copy).then_inc(qh_ok, 1)

                nc.scalar.activation(k_hi[:], E["kd"][:, 0:SEQ], ACT.Copy).then_inc(kh_ok, 1)
                query_hi(0)
                query_hi(1)
                probs(0)
                m = 0
                for i, (t, x, g) in enumerate(ITEMS):
                    if i + 1 < len(ITEMS):
                        probs(i + 1)
                    evict(i)
                    if t + 2 < NTP and i + 1 == FIRST[t + 1]:
                        query_hi(t + 2)
                    if i >= LAST[m] + 2:
                        output(m)
                        m += 1
                while m < HALVES:
                    output(m)
                    m += 1


def output(nc, ctx, M, K, io, o, h, y, ya, yb, xT, scratch, x_dram):
    sem = lambda n: ctx.enter_context(nc.semaphore("b_" + n))
    (o_hi, o_lo), (h_hi, h_lo), (y_hi, y_lo) = o, h, y
    with ExitStack() as mem, M.scope():
        raw = M.low("b_raw", [P, 2, KT, P])
        w_hi = M.low("b_w_hi", [P, 2, KT, P], F32R)
        w_lo = M.low("b_w_lo", [P, 2, KT, P], F32R)
        sg = M.low("b_sg", [P, 2, 2, N_TOK])
        sq = ya
        ps = psum(nc, mem, "b_ps", [P, NCH, 2, 512])
        w_in, g_in = [sem("w_in0"), sem("w_in1")], [sem("g_in0"), sem("g_in1")]
        hi_ok, lo_ok, mm_ok, ya_ok, yb_ok, y_ok, yh_ok, yl_ok, x_in, x_ok, sq_ok, sum_ok = (
            sem(n) for n in ("hi_ok", "lo_ok", "mm_ok", "ya_ok", "yb_ok", "y_ok", "yh_ok", "yl_ok", "x_in", "x_ok",
                             "sq_ok", "sum_ok"))
        wa = io["w_branch_attn"][0].rearrange("(k p) n -> p k n", p=P)
        wb = io["w_branch_mlstm"][0].rearrange("(k p) n -> p k n", p=P)
        wo = io["w_out"][0].rearrange("(k p) n -> p k n", p=P)
        ga, gb = (scratch.ap()[HM + u * KT:HM + (u + 1) * KT].rearrange("k p n -> p k n") for u in range(2))

        def run(loop, before, unit):
            before(0, 0)
            for n0 in (0, 1):
                before(0, n0 + 1)
                unit(0, n0)
            with loop(0, KT // 2 - 2) as i:
                for n0 in (2, 3):
                    before(i, n0 + 1)
                    unit(i, n0)
            for n0 in (KT - 2, KT - 1, KT, KT + 1):
                before(0, n0 + 1)
                unit(0, n0)
            with loop(0, KT // 2 - 2) as i:
                for n0 in (KT + 2, KT + 3):
                    before(i, n0 + 1)
                    unit(i, n0)
            before(0, 2 * KT - 1)
            unit(0, 2 * KT - 2)
            unit(0, 2 * KT - 1)

        with nc.Block() as block:
            @block.sync
            def _(sp):
                def load(i, n0):
                    if n0 >= KT:
                        cols = bass.ds((i * 2 + (n0 - KT)) * P, P)
                        sp.wait_ge(lo_ok, i * 2 + (n0 - 1))
                        sp.dma_start(raw[:, n0 % 2], wo[:, :, cols]).then_inc(w_in[n0 % 2], 32)
                        return
                    cols, tile = bass.ds((i * 2 + n0) * P, P), bass.ds(i * 2 + n0, 1)
                    if n0 >= 2:
                        sp.wait_ge(lo_ok, i * 2 + (n0 - 1))
                    sp.dma_start(raw[:, n0 % 2, 0:4], wa[:, :, cols]).then_inc(w_in[n0 % 2], 16)
                    sp.dma_start(raw[:, n0 % 2, 4:8], wb[:, :, cols]).then_inc(w_in[n0 % 2], 16)
                    if n0 >= 2:
                        sp.wait_ge(yb_ok, i * (2 * NCH) + NCH * (n0 - 1))
                    sp.dma_start(sg[:, n0 % 2, 0:1], ga[:, tile, :]).then_inc(g_in[n0 % 2], 16)
                    sp.dma_start(sg[:, n0 % 2, 1:2], gb[:, tile, :]).then_inc(g_in[n0 % 2], 16)

                def unit(i, n0):
                    if n0 == KT:
                        sp.wait_ge(mm_ok, NCH * KT)
                        sp.dma_start(xT[:], x_dram.ap()).then_inc(x_in, 16)
                run(nc.sync.Fori, load, unit)

            @block.scalar
            def _(act):
                def split_hi(i, n0):
                    act.wait_ge(w_in[n0 % 2], i * 32 + 32 * (n0 // 2 + 1))
                    if n0 >= 2:
                        act.wait_ge(mm_ok, i * (2 * NCH) + NCH * (n0 - 1))
                    nc.scalar.activation(w_hi[:, n0 % 2], raw[:, n0 % 2], ACT.Copy).then_inc(hi_ok, 1)

                def unit(i, n0):
                    for c in range(NCH):
                        q0 = NCH * n0 + c
                        tok = slice(c * CH, (c + 1) * CH)
                        if n0 < KT:
                            act.wait_ge(y_ok, i * (2 * NCH) + (q0 + 1))
                            nc.scalar.activation(y_hi[:, bass.ds(i * 2 + n0, 1), tok], ya[:, q0 % 2:q0 % 2 + 1],
                                                 ACT.Copy).then_inc(yh_ok, 1)
                            continue
                        act.wait_ge(x_ok, i * (2 * NCH) + (q0 - NCH * KT + 1))
                        if n0 == KT:
                            if c == 0:
                                act.wait_ge(yl_ok, NCH * KT)
                            nc.scalar.activation(K["acc"][:, tok], xT[:, 0, tok], ACT.Square).then_inc(sq_ok, 1)
                            continue
                        m0 = q0 - NCH * (KT + 1)
                        if m0 >= 2:
                            act.wait_ge(sum_ok, i * (2 * NCH) + (m0 - 1))
                        nc.scalar.activation(sq[:, m0 % 2:m0 % 2 + 1], xT[:, bass.ds(i * 2 + (n0 - KT), 1), tok],
                                             ACT.Square).then_inc(sq_ok, 1)
                run(nc.scalar.Fori, split_hi, unit)

            @block.gpsimd
            def _(pool):
                def split_lo(i, n0):
                    pool.wait_ge(hi_ok, i * 2 + (n0 + 1))
                    nc.gpsimd.tensor_tensor(w_lo[:, n0 % 2], raw[:, n0 % 2], w_hi[:, n0 % 2].bitcast(F32),
                                            ALU.subtract).then_inc(lo_ok, 1)

                def unit(i, n0):
                    if n0 >= KT:
                        return
                    for c in range(NCH):
                        q0 = NCH * n0 + c
                        pool.wait_ge(yh_ok, i * (2 * NCH) + (q0 + 1))
                        at = (slice(None), bass.ds(i * 2 + n0, 1), slice(c * CH, (c + 1) * CH))
                        nc.gpsimd.tensor_tensor(y_lo[at], ya[:, q0 % 2:q0 % 2 + 1], y_hi[at].bitcast(F32),
                                                ALU.subtract).then_inc(yl_ok, 1)
                run(nc.gpsimd.Fori, split_lo, unit)

            @block.vector
            def _(dve):
                def mix(i, n0):
                    dve.wait_ge(g_in[n0 % 2], i * 32 + 32 * (n0 // 2 + 1))
                    for c in range(NCH):
                        q0 = NCH * n0 + c
                        q = i * (2 * NCH) + q0
                        tok = slice(c * CH, (c + 1) * CH)
                        dve.wait_ge(mm_ok, q + 1)
                        if q0 >= 2:
                            dve.wait_ge(yl_ok, q - 1)
                        nc.vector.tensor_tensor(ya[:, q0 % 2], ps[:, c, 0, 0:CH], sg[:, n0 % 2, 0, tok],
                                                ALU.mult).then_inc(ya_ok, 1)
                        nc.vector.tensor_tensor(yb[:, q0 % 2], ps[:, c, 1, 0:CH], sg[:, n0 % 2, 1, tok],
                                                ALU.mult).then_inc(yb_ok, 1)
                        dve.wait_ge(ya_ok, q + 1)
                        dve.wait_ge(yb_ok, q + 1)
                        nc.vector.tensor_tensor(ya[:, q0 % 2], ya[:, q0 % 2], yb[:, q0 % 2], ALU.add).then_inc(y_ok, 1)

                def add_square(i, q0):
                    m0 = q0 - NCH * (KT + 1)
                    a = K["acc"][:, q0 % NCH * CH:(q0 % NCH + 1) * CH]
                    dve.wait_ge(sq_ok, i * (2 * NCH) + (q0 - NCH * KT + 1))
                    if m0:
                        dve.wait_ge(sum_ok, i * (2 * NCH) + m0)
                    nc.vector.tensor_tensor(a, a, sq[:, m0 % 2], ALU.add).then_inc(sum_ok, 1)

                def unit(i, n0):
                    if n0 < KT:
                        mix(i, n0)
                        return
                    if n0 == KT:
                        dve.wait_ge(x_in, 16)
                    for c in range(NCH):
                        q0 = NCH * n0 + c
                        dve.wait_ge(mm_ok, i * (2 * NCH) + (q0 + 1))
                        x = xT[:, bass.ds(i * 2 + (n0 - KT), 1), c * CH:(c + 1) * CH]
                        nc.vector.tensor_tensor(x, ps[:, c, 0:1, 0:CH], x, ALU.add).then_inc(x_ok, 1)
                        if q0 > NCH * (KT + 1):
                            add_square(i, q0 - 1)
                run(nc.vector.Fori, lambda i, n0: None, unit)
                add_square(0, 2 * NCH * KT - 1)

            @block.tensor
            def _(pe):
                def unit(i, n0):
                    pe.wait_ge(lo_ok, i * 2 + (n0 + 1))
                    for c in range(NCH):
                        tok = slice(c * CH, (c + 1) * CH)
                        if 0 < n0 <= KT:
                            pe.wait_ge(yb_ok, i * (2 * NCH) + (NCH * n0 + c - 2))
                        if n0 > KT:
                            pe.wait_ge(x_ok, i * (2 * NCH) + (NCH * (n0 - KT) + c - 2))
                        if n0 < KT:
                            for u, (x_hi, x_lo) in enumerate(((o_hi, o_lo), (h_hi, h_lo))):
                                for k in range(4):
                                    last = product3(nc, ps[:, c, u, 0:CH], w_hi[:, n0 % 2, 4 * u + k],
                                                    w_lo[:, n0 % 2, 4 * u + k], x_hi[:, k, tok], x_lo[:, k, tok],
                                                    k == 0, k == 3)
                        else:
                            if n0 == KT:
                                pe.wait_ge(yl_ok, NCH * (KT - 1) + c + 1)
                            for k in range(KT):
                                last = product3(nc, ps[:, c, 0, 0:CH], w_hi[:, n0 % 2, k], w_lo[:, n0 % 2, k],
                                                y_hi[:, k, tok], y_lo[:, k, tok], k == 0, k == KT - 1)
                        last.then_inc(mm_ok, 1)
                run(nc.tensor.Fori, lambda i, n0: None, unit)


def final_norm(nc, ctx, M, K, io, out, xT):
    sem = lambda n: ctx.enter_context(nc.semaphore("z_" + n))
    ON_SCALAR = [t for t in range(NT) if t % 3 == 1]
    with ExitStack() as mem, M.scope():
        gain = M.low("z_gain", [P, D_MODEL])
        part = M.low("z_part", [P, len(ON_SCALAR), D_MODEL])
        res = M.low("z_res", [P, NT, D_MODEL])
        ss, inv, rms = (M.low("z_" + n, [P, NT]) for n in ("ss", "inv", "rms"))
        ps = psum(nc, mem, "z_ps", [P, 3, D_MODEL])
        ps_s = psum(nc, mem, "z_ps_s", [P, NT, 1])
        ld, sums, tp, s1, s2, s3, part_ok, r_v, r_g, st = (
            sem(n) for n in ("ld", "sums", "tp", "s1", "s2", "s3", "part_ok", "r_v", "r_g", "st"))

        def results(t):
            g = sum(x <= t for x in ON_SCALAR)
            return t + 1 - g, g

        def wait_out(eng, t):
            if t in ON_SCALAR:
                eng.wait_ge(part_ok, results(t)[1])
            else:
                eng.wait_ge(r_v, results(t)[0])

        with nc.Block() as block:
            @block.sync
            def _(sp):
                sp.dma_start(gain[:], io["norm_final"].rearrange("(a n) -> a n", a=1).to_broadcast([P, D_MODEL]))\
                    .then_inc(ld, 16)
                for t in range(NT):
                    if t in ON_SCALAR:
                        sp.wait_ge(r_g, results(t)[1])
                    else:
                        sp.wait_ge(r_v, results(t)[0])
                    dst = out["y_prompt"][0, t * P:(t + 1) * P, :] if t < NTP else \
                        out["y_sample"].rearrange("b q d -> (b q) d")
                    sp.dma_start(dst, res[:, t]).then_inc(st, 16)
                sp.wait_ge(st, 16 * NT)

            @block.tensor
            def _(pe):
                for t in range(NT):
                    last = nc.tensor.matmul(ps_s[:, t, :], K["acc"][:, t * P:(t + 1) * P], K["ones"][:, 0:1],
                                            start=True, stop=True)
                last.then_inc(sums, 1)
                for t in range(NT):
                    if t >= 3:
                        wait_out(pe, t - 3)
                    for k in range(KT):
                        last = nc.tensor.transpose(ps[:, t % 3, k * P:(k + 1) * P], xT[:, k, t * P:(t + 1) * P],
                                                   K["ident"][:])
                    last.then_inc(tp, 1)

            @block.scalar
            def _(act):
                act.wait_ge(s2, 1)
                nc.scalar.activation(rms[:], inv[:], ACT.Sqrt).then_inc(s3, 1)
                act.wait_ge(s3, 1)
                for x, t in enumerate(ON_SCALAR):
                    act.wait_ge(tp, t + 1)
                    nc.scalar.activation(part[:, x], ps[:, t % 3], ACT.Copy, scale=rms[:, t:t + 1]).then_inc(part_ok, 1)

            @block.gpsimd
            def _(pool):
                pool.wait_ge(ld, 16)
                for x, t in enumerate(ON_SCALAR):
                    pool.wait_ge(part_ok, x + 1)
                    nc.gpsimd.tensor_tensor(res[:, t], part[:, x], gain[:], ALU.mult).then_inc(r_g, 1)

            @block.vector
            def _(dve):
                dve.wait_ge(sums, 1)
                nc.vector.tensor_scalar(ss[:], ps_s[:, :, 0], 1.0 / D_MODEL, EPS, ALU.mult, ALU.add).then_inc(s1, 1)
                dve.wait_ge(s1, 1)
                nc.vector.reciprocal(inv[:], ss[:]).then_inc(s2, 1)
                dve.wait_ge(s3, 1)
                dve.wait_ge(ld, 16)
                for t in range(NT):
                    if t not in ON_SCALAR:
                        dve.wait_ge(tp, t + 1)
                        nc.vector.scalar_tensor_tensor(res[:, t], ps[:, t % 3], rms[:, t:t + 1], gain[:],
                                                       ALU.mult, ALU.mult).then_inc(r_v, 1)


def trunk(nc, io, out):
    ctx = ExitStack()
    M = Sbuf(nc)
    x_dram = nc.dram_tensor("x_dram", [P, KT, N_TOK], F32, kind="Internal")
    scratch = nc.dram_tensor("p_dram", [N_SIG + 1, P, N_TOK], F32, kind="Internal")
    with ctx:
        stats = M.low("stats", [P, 4, NT])
        K = {n: stats[:, x] for x, n in enumerate(("ssq", "mean", "inv", "root"))}
        K["acc_at"] = M.low_end
        K["acc"] = M.low("acc", [P, N_TOK])
        K["ident"] = M.low("ident_sb", [P, P])
        K["ones"] = M.low("ones_sb", [P, P])
        K["gains"] = M.low("gains", [P, 3 * KT + HM])
        for n, k in enumerate(("ffn1", "mix", "ffn2")):
            K["g_" + k] = K["gains"][:, n * KT:(n + 1) * KT]
        K["g_mlstm"] = K["gains"][:, 3 * KT:3 * KT + HM]

        def phase(f, *args):
            f(nc, Scope(own[0], used), M, K, *args)

        def renew():
            used.sort()
            with nc.Block() as block:
                @block.gpsimd
                def _(pool):
                    at = 0
                    while at < len(used):
                        end = at + 1
                        while end < len(used) and used[end] == used[end - 1] + 1:
                            end += 1
                        pool.sem_clear(range(used[at], used[end - 1] + 1))
                        at = end
            used.clear()
            own[0].close()
            own[0] = ctx.enter_context(ExitStack())

        used, own = [], [ctx.enter_context(ExitStack())]
        high_end = M.high_end
        xn_hi = M.high("xn_hi", [P, KT, N_TOK], F32R)
        xn_lo = M.high("xn_lo", [P, KT, N_TOK], F32R)
        low_end = M.low_end
        xT = M.low("xT", [P, KT, N_TOK])
        phase(load_residual, io, xT)
        phase(ffn, io["w_ffn1_up"], io["w_ffn1_down"], K["g_ffn1"], xT, xn_hi, xn_lo, "f1", True)
        M.low_end = aq_at = low_end
        aq = M.low("aq", [P, 4, N_TOK])
        kvT_at = M.low_end
        kvT = M.low("kvT", [P, N_TOK])
        DM = M.low("DM", [P, SCORE_COLS])
        mix_at = M.low_end
        mix = M.low("mix", [P, N_MIX, N_TOK])
        phase(project, io, out, xT, x_dram, xn_hi, xn_lo, aq, kvT, DM, mix, aq_at, kvT_at, mix_at,
              scratch)
        M.high_end = high_end
        E = {"aq": aq, "mix": mix, "mqk": mix[:, 0:4], "free_at": mix_at + 4 * N_TOK * 4,
             "kvT_at": kvT_at}
        E["kvtok"] = M.low("kvtok", [P, NT, P])
        low_end = M.low_end
        for n, shape in dict(vaug=[P, NT, HM, DV + 1], ktm=[P, NT, HM * DH],
                             mqd=[P, HM, P], Cn=[P, HM, DEC_BATCH, DH], CT=[P, HM, 4, DV + 1],
                             U=[HM, N_TOK], head_sel=[HM, HM, P], causal_p=[P, P],
                             causal_s=[P, P], batch_mask=[P, DEC_BATCH],
                             decB=[P, HM, NTP + DEC_BATCH], decP=[P, 2, NTP]).items():
            E[n] = M.low(n + "_sb", shape)
        E["Gt"], E["pair_mask"] = M.high("Gt", [P, NT, 4, HM]), M.high("pair_mask_e", [P, 4, P])
        phase(prepare_mix, io, out, kvT, E, scratch)
        for n, shape in dict(KTa=[P, 4, LS], kd=[P, N_TOK], aqr=[P, 4, P],
                             vn=[DEC_SEQ, DEC_BATCH, DH]).items():
            E[n] = M.high(n, shape)
        att_end = M.high_end
        num = M.high("num", [P, NT, HM, DV + 1])
        E["ss"] = M.high("num_ss", [P, NT, HM])
        phase(mlstm, io, out, kvT, E, num)
        renew()
        M.low_end = low_end
        h = M.at("h_hi", [P, HM, N_TOK], mix_at, F32R), M.at("h_lo", [P, HM, N_TOK], E["free_at"], F32R)
        phase(mlstm_output, E, num, *h, scratch)
        M.high_end = att_end
        o = M.low("o_hi", [P, HM, N_TOK], F32R), M.low("o_lo", [P, HM, N_TOK], F32R)
        phase(attention, io, E, DM, *o)
        M.high_end = high_end
        y = M.high("y_hi", [P, KT, N_TOK], F32R), M.high("y_lo", [P, KT, N_TOK], F32R)
        ya, yb = M.low("b_ya", [P, 2, CH]), M.low("b_yb", [P, 2, CH])
        M.low_end = aq_at
        M.high_end = xT_at = mix_at - 576
        xT = M.at("xT_2", [P, KT, N_TOK], xT_at)
        phase(output, io, o, h, y, ya, yb, xT, scratch, x_dram)
        M.high_end = high_end
        M.low_end, M.gap = xT_at + KT * N_TOK * 4, (aq_at, xT_at)
        xn = M.high("xn2_hi", [P, KT, N_TOK], F32R), M.high("xn2_lo", [P, KT, N_TOK], F32R)
        phase(ffn, io["w_ffn2_up"], io["w_ffn2_down"], K["g_ffn2"], xT, *xn, "f2", False)
        phase(final_norm, io, out, xT)


_INS = ["x_prompt", "x_sample", "cache_attn_k", "cache_attn_v", "cache_idx_k", "state_mlstm_C", "state_mlstm_n",
        "state_mlstm_m", "norm_ffn1", "w_ffn1_up", "w_ffn1_down", "norm_mix", "w_in", "b_mlstm_gates",
        "norm_mlstm_heads", "w_branch_attn", "w_branch_mlstm", "w_out", "norm_ffn2", "w_ffn2_up", "w_ffn2_down",
        "norm_final"]
_OUTS = {
    "y_prompt": (1, SEQ, D_MODEL), "y_sample": (DEC_BATCH, DEC_SEQ, D_MODEL),
    "new_k_prompt": (1, 1, SEQ, DH), "new_v_prompt": (1, 1, SEQ, DH), "new_idxk_prompt": (1, 1, SEQ, DH),
    "new_C_prompt": (1, 1, HM, DV, DH), "new_n_prompt": (1, 1, HM, DH), "new_m_prompt": (1, 1, HM),
    "new_k_sample": (1, DEC_BATCH, DEC_SEQ, DH), "new_v_sample": (1, DEC_BATCH, DEC_SEQ, DH),
    "new_idxk_sample": (1, DEC_BATCH, DEC_SEQ, DH), "new_C_sample": (1, DEC_BATCH, HM, DV, DH),
    "new_n_sample": (1, DEC_BATCH, HM, DH), "new_m_sample": (1, DEC_BATCH, HM),
}


def kernel(**inputs):
    import concourse.bacc as bacc
    from concourse.bass_utils import run_bass_kernel_spmd

    nc = bacc.Bacc("TRN2", target_bir_lowering=False, num_devices=1)
    arrays, io, out = {}, {}, {}
    given = {n: np.ascontiguousarray(inputs[n]) for n in _INS}
    for name, a in {**given, **constants()}.items():
        arrays["in_" + name] = a
        io[name] = nc.dram_tensor("in_" + name, a.shape, F32, kind="ExternalInput").ap()
    for name, shape in _OUTS.items():
        out[name] = nc.dram_tensor("out_" + name, shape, F32, kind="ExternalOutput").ap()
    trunk(nc, io, out)
    r = run_bass_kernel_spmd(nc, [arrays], core_ids=[0])
    return tuple(r.results[0]["out_" + n] for n in _OUTS)
```
